# Optimizing a Trainium2 kernel written in Bass

```python
import jax, jax.numpy as jnp
from jax import lax
import numpy as np

D_MODEL = 1024
BATCH = 1
SEQ = 512
DEPTH = 1

GDN_H = 4
GDN_DK = 128
GDN_DV = 128
GDN_W = GDN_H * GDN_DV
CONV_W = 4
CHUNK = 64
SB_H = 4
SB_D = 128
SB_W = SB_H * SB_D
Q_BLOCK = 128
MEM_H = 4
MEM_D = 128
MEM_W = MEM_H * MEM_D
N_MEM = 256
N_BRANCH = 3
D_FF = 4 * D_MODEL
EPS = 1e-6
IN_SIZES = (3 * GDN_W, GDN_W, GDN_H, GDN_H, 3 * SB_W, MEM_W, N_BRANCH * D_MODEL)
D_IN = sum(IN_SIZES)

kernel_name = "hybrid_gdn_stickbreak_memxattn_gated_merge"

def rms_norm(x, g):
    xf = x.astype(jnp.float32)
    y = xf * lax.rsqrt(jnp.mean(xf * xf, axis=-1, keepdims=True) + EPS)
    return (y * g.astype(jnp.float32)).astype(x.dtype)

def l2norm(x):
    return x * lax.rsqrt(jnp.sum(x * x, axis=-1, keepdims=True) + EPS)

def causal_dwconv(x, w):
    c = x.shape[-1]
    return lax.conv_general_dilated(
        x, w[:, None, :].astype(x.dtype), window_strides=(1,),
        padding=[(w.shape[0] - 1, 0)], dimension_numbers=("NWC", "WIO", "NWC"),
        feature_group_count=c)

def gated_delta_rule_chunked(q, k, v, g, beta):
    b, s, h, dk = q.shape
    dv = v.shape[-1]
    n = s // CHUNK

    def to_chunks(t):
        return jnp.moveaxis(t.reshape(b, n, CHUNK, h, *t.shape[3:]), 3, 1)

    qc, kc, vc, gc, bc = (to_chunks(t) for t in (q, k, v, g, beta))
    gc = jnp.cumsum(gc, axis=-1)
    idx = jnp.arange(CHUNK)
    causal = idx[:, None] >= idx[None, :]
    strict = idx[:, None] > idx[None, :]
    decay = jnp.exp(jnp.where(causal, gc[..., :, None] - gc[..., None, :], -jnp.inf))
    kb = kc * bc[..., None]
    vb = vc * bc[..., None]
    lower = jnp.where(strict, jnp.einsum("bhncd,bhnsd->bhncs", kb, kc) * decay, 0.0)
    eye = jnp.eye(CHUNK, dtype=jnp.float32)
    t_inv = lax.linalg.triangular_solve(eye + lower, jnp.broadcast_to(eye, lower.shape),
                                        left_side=True, lower=True, unit_diagonal=True)
    u = jnp.einsum("bhncs,bhnsv->bhncv", t_inv, vb)
    w = jnp.einsum("bhncs,bhnsk->bhnck", t_inv, kb * jnp.exp(gc)[..., None])
    a_qk = jnp.where(causal, jnp.einsum("bhncd,bhnsd->bhncs", qc, kc) * decay, 0.0)
    q_dec = qc * jnp.exp(gc)[..., None]
    k_dec = kc * jnp.exp(gc[..., -1:] - gc)[..., None]
    g_last = jnp.exp(gc[..., -1])
    xs = tuple(jnp.moveaxis(t, 2, 0) for t in (u, w, a_qk, q_dec, k_dec, g_last))

    def step(state, inp):
        u_i, w_i, a_i, qd_i, kd_i, gl_i = inp
        v_new = u_i - jnp.einsum("bhck,bhkv->bhcv", w_i, state)
        o_i = (jnp.einsum("bhck,bhkv->bhcv", qd_i, state)
               + jnp.einsum("bhcs,bhsv->bhcv", a_i, v_new))
        state = state * gl_i[..., None, None] + jnp.einsum("bhck,bhcv->bhkv", kd_i, v_new)
        return state, o_i

    s0 = jnp.zeros((b, h, dk, dv), jnp.float32)
    _, o = lax.scan(step, s0, xs)
    o = jnp.moveaxis(jnp.moveaxis(o, 0, 2), 1, 3)
    return o.reshape(b, s, h, dv)

def stick_breaking_attention(q, k, v):
    s = q.shape[2]
    scale = q.shape[-1] ** -0.5
    outs = []
    for blk in range(s // Q_BLOCK):
        q0 = blk * Q_BLOCK
        kl = q0 + Q_BLOCK
        z = jnp.einsum("bhqd,bhkd->bhqk", q[:, :, q0:kl], k[:, :, :kl]) * scale
        mask = jnp.arange(kl)[None, :] < (q0 + jnp.arange(Q_BLOCK))[:, None]
        log_1mb = jnp.where(mask, jax.nn.log_sigmoid(-z), 0.0)
        between = lax.cumsum(log_1mb, axis=3, reverse=True) - log_1mb
        att = jnp.where(mask, jnp.exp(jax.nn.log_sigmoid(z) + between), 0.0)
        outs.append(jnp.einsum("bhqk,bhkd->bhqd", att, v[:, :, :kl]))
    return jnp.concatenate(outs, axis=2)

def setup_inputs(seed: int = 0) -> dict:
    key = jax.random.key(seed)
    ks = jax.random.split(key, 24)
    f32 = jnp.float32
    nrm = lambda k, shape, scale: jax.random.normal(k, shape, f32) * scale
    gain = lambda k, n: 1.0 + 0.02 * jax.random.normal(k, (DEPTH, n), f32)
    dt = jnp.exp(jax.random.uniform(ks[5], (DEPTH, GDN_H), f32, np.log(1e-3), np.log(1e-1)))
    return {
        "x": nrm(ks[0], (BATCH, SEQ, D_MODEL), 1.0),
        "mem": nrm(ks[1], (BATCH, N_MEM, D_MODEL), 1.0),
        "norm1_g": gain(ks[2], D_MODEL),
        "w_in": nrm(ks[3], (DEPTH, D_MODEL, D_IN), D_MODEL ** -0.5),
        "conv_w": nrm(ks[4], (DEPTH, CONV_W, 3 * GDN_W), CONV_W ** -0.5),
        "a_log": jnp.log(jax.random.uniform(ks[6], (DEPTH, GDN_H), f32, 1.0, 16.0)),
        "dt_bias": jnp.log(jnp.expm1(dt)),
        "gdn_norm_g": gain(ks[7], GDN_DV),
        "sb_q_norm_g": gain(ks[8], SB_D),
        "sb_k_norm_g": gain(ks[9], SB_D),
        "mem_norm_g": gain(ks[10], D_MODEL),
        "w_mem_kv": nrm(ks[11], (DEPTH, D_MODEL, 2 * MEM_W), D_MODEL ** -0.5),
        "mem_q_norm_g": gain(ks[12], MEM_D),
        "mem_k_norm_g": gain(ks[13], MEM_D),
        "w_br_gdn": nrm(ks[14], (DEPTH, GDN_W, D_MODEL), GDN_W ** -0.5),
        "w_br_sb": nrm(ks[15], (DEPTH, SB_W, D_MODEL), SB_W ** -0.5),
        "w_br_mem": nrm(ks[16], (DEPTH, MEM_W, D_MODEL), MEM_W ** -0.5),
        "w_o": nrm(ks[17], (DEPTH, D_MODEL, D_MODEL), D_MODEL ** -0.5),
        "norm2_g": gain(ks[18], D_MODEL),
        "w_up": nrm(ks[19], (DEPTH, D_MODEL, D_FF), D_MODEL ** -0.5),
        "w_down": nrm(ks[20], (DEPTH, D_FF, D_MODEL), D_FF ** -0.5),
    }

def reference(x, mem, norm1_g, w_in, conv_w, a_log, dt_bias, gdn_norm_g, sb_q_norm_g, sb_k_norm_g,
              mem_norm_g, w_mem_kv, mem_q_norm_g, mem_k_norm_g, w_br_gdn, w_br_sb, w_br_mem, w_o,
              norm2_g, w_up, w_down):
    b, s, _ = x.shape
    f32 = jnp.float32
    splits = np.cumsum(IN_SIZES)[:-1].tolist()
    for l in range(DEPTH):
        h = rms_norm(x, norm1_g[l])
        proj = h @ w_in[l]
        gdn_qkv, gdn_z, gdn_a, gdn_b, sb_qkv, mem_q, gate_logits = jnp.split(proj, splits, axis=-1)

        gdn_qkv = jax.nn.silu(causal_dwconv(gdn_qkv, conv_w[l])).astype(f32)
        gq, gk, gv = jnp.split(gdn_qkv, 3, axis=-1)
        gq = l2norm(gq.reshape(b, s, GDN_H, GDN_DK)) * (GDN_DK ** -0.5)
        gk = l2norm(gk.reshape(b, s, GDN_H, GDN_DK))
        gv = gv.reshape(b, s, GDN_H, GDN_DV)
        beta = jax.nn.sigmoid(gdn_b.astype(f32))
        g = -jnp.exp(a_log[l].astype(f32)) * jax.nn.softplus(gdn_a.astype(f32) + dt_bias[l].astype(f32))
        o_gdn = gated_delta_rule_chunked(gq, gk, gv, g, beta)
        o_gdn = rms_norm(o_gdn, gdn_norm_g[l]) * jax.nn.silu(gdn_z.astype(f32).reshape(b, s, GDN_H, GDN_DV))
        y_gdn = o_gdn.reshape(b, s, GDN_W).astype(x.dtype) @ w_br_gdn[l]

        sq, sk, sv = jnp.split(sb_qkv, 3, axis=-1)
        sq = rms_norm(sq.reshape(b, s, SB_H, SB_D), sb_q_norm_g[l])
        sk = rms_norm(sk.reshape(b, s, SB_H, SB_D), sb_k_norm_g[l])
        sv = sv.reshape(b, s, SB_H, SB_D)
        to_bhsd = lambda t: jnp.transpose(t, (0, 2, 1, 3)).astype(f32)
        o_sb = stick_breaking_attention(to_bhsd(sq), to_bhsd(sk), to_bhsd(sv))
        y_sb = jnp.transpose(o_sb, (0, 2, 1, 3)).reshape(b, s, SB_W).astype(x.dtype) @ w_br_sb[l]

        kv = rms_norm(mem, mem_norm_g[l]) @ w_mem_kv[l]
        km, vm = jnp.split(kv, 2, axis=-1)
        km = rms_norm(km.reshape(b, N_MEM, MEM_H, MEM_D), mem_k_norm_g[l]).astype(f32)
        vm = vm.reshape(b, N_MEM, MEM_H, MEM_D).astype(f32)
        qm = rms_norm(mem_q.reshape(b, s, MEM_H, MEM_D), mem_q_norm_g[l]).astype(f32)
        p = jax.nn.softmax(jnp.einsum("bshd,bmhd->bhsm", qm, km) * (MEM_D ** -0.5), axis=-1)
        o_mem = jnp.einsum("bhsm,bmhd->bshd", p, vm).reshape(b, s, MEM_W).astype(x.dtype)
        y_mem = o_mem @ w_br_mem[l]

        g_gdn, g_sb, g_mem = jnp.split(jax.nn.sigmoid(gate_logits), N_BRANCH, axis=-1)
        mix = g_gdn * y_gdn + g_sb * y_sb + g_mem * y_mem
        x = x + mix @ w_o[l]

        h2 = rms_norm(x, norm2_g[l])
        x = x + jnp.square(jax.nn.relu(h2 @ w_up[l])) @ w_down[l]
    return x


_drawn_inputs = setup_inputs


def setup_inputs(seed=0):
    import zlib

    import numpy as np

    out = dict(_drawn_inputs(seed))
    spreads = {}
    factors = {'norm1_g': 4.036,
     'gdn_norm_g': 21.83,
     'sb_q_norm_g': 32.046,
     'sb_k_norm_g': 27.096,
     'mem_norm_g': 8.0,
     'mem_q_norm_g': 8.0,
     'mem_k_norm_g': 8.0,
     'norm2_g': 12.304}
    for name, (base, spread) in spreads.items():
        noise = np.random.default_rng([zlib.crc32(name.encode()), seed]).standard_normal(out[name].shape)
        drawn = base * np.exp(spread * noise) if base else spread * noise
        out[name] = __import__('jax').numpy.asarray(drawn.astype(out[name].dtype))
    for name, factor in factors.items():
        out[name] = (out[name] * factor).astype(out[name].dtype)
    return out
```

```python
import numpy as np

import concourse.bass as bass
from concourse import mybir
from contextlib import ExitStack


def hybrid_layer_kernel(nc, x, mem, norm1_g, w_in, conv_w, a_log, dt_bias, gdn_norm_g, sb_q_norm_g,
                        sb_k_norm_g, mem_norm_g, w_mem_kv, mem_q_norm_g, mem_k_norm_g, w_br_gdn,
                        w_br_sb, w_br_mem, w_o, norm2_g, w_up, w_down, out):
    F32, F32R, I32 = mybir.dt.float32, mybir.dt.float32r, mybir.dt.int32
    ALU, ACT, AX = mybir.AluOpType, mybir.ActivationFunctionType, mybir.AxisListType

    P = 128
    SEQ, D = x.shape[1], x.shape[2]
    N_MEM = mem.shape[1]
    H, DH, CHUNK = 4, 128, 64
    HW = H * DH
    EPS = 1e-6
    TT, KT = SEQ // P, D // P
    MT = N_MEM // P
    FF = w_up.shape[2]
    KU = 4
    UW = 512
    QUARTERS = FF // D
    SCALE = float(DH) ** -0.5
    MASKED = -1e30
    CONV = conv_w.shape[1]

    C_GDN, C_Z = 0, 3 * HW
    C_AB = C_Z + HW
    C_SB = C_AB + 2 * H
    C_MEMQ = C_SB + 3 * HW
    C_GATE = C_MEMQ + HW

    win = w_in[0].rearrange("(t p) n -> p t n", p=P)
    wkv = w_mem_kv[0].rearrange("(t p) n -> p t n", p=P)
    wbr = [w[0].rearrange("(t p) n -> p t n", p=P) for w in (w_br_sb, w_br_mem, w_br_gdn)]
    wo = w_o[0].rearrange("(t p) n -> p t n", p=P)
    wup = w_up[0].rearrange("(t p) n -> p t n", p=P)
    wdown = w_down[0].rearrange("(t p) n -> p t n", p=P)

    UNITS = []

    def stage(name, i, w, col, act, kts, tiles, kind="tok", bank0=0, kt0=0):
        for n, k in enumerate(range(0, kts, KU)):
            UNITS.append(dict(stage=name, i=i, src=w[:, k:k + KU, col:col + UW], act=act, kt0=kt0 + k, kts=KU,
                              first=n == 0, last=k + KU == kts, kind=kind,
                              outs=[(bank0 + j, j) for j in range(tiles)]))

    stage("sbq", 0, win, C_SB, "A", KT, TT)
    stage("sbk", 0, win, C_SB + HW, "A", KT, TT)
    stage("sbv", 0, win, C_SB + 2 * HW, "A", KT, TT)
    stage("memq", 0, win, C_MEMQ, "A", KT, TT)
    stage("memk", 0, wkv, 0, "B", KT, MT)
    stage("memv", 0, wkv, HW, "B", KT, MT, bank0=MT)
    for part in range(3):
        stage("conv", part, win, C_GDN + part * HW, "A", KT, H, kind="chan")
    stage("z", 0, win, C_Z, "A", KT, TT)
    UNITS.append(dict(stage="ab", i=0, src=win[:, :, C_AB:C_AB + P], act="A", kt0=0, kts=KT, first=True,
                      last=True, kind="chan", outs=[(0, 0)]))
    GATE_OF = (1, 2, 0)
    BR_KT0 = (0, H, 0)
    for br in range(3):
        for half in range(2):
            stage("gate", 2 * br + half, win, C_GATE + GATE_OF[br] * D + half * UW, "A", KT, TT)
            stage("branch", 2 * br + half, wbr[br], half * UW, "B", H, TT, kt0=BR_KT0[br])
    for half in range(2):
        stage("wo", half, wo, half * UW, "A", KT, TT)
    NU = len(UNITS)

    PIECES, BANK_USES, chunk = [], [0] * TT, 0
    for u, unit in enumerate(UNITS):
        for n, (bank, j) in enumerate(unit["outs"]):
            if unit["first"]:
                BANK_USES[bank] += 1
            for k in range(0, unit["kts"], 2):
                PIECES.append(dict(unit=u, chunk=chunk, bank=bank, j=j, k=k, opens_unit=n == 0 and k == 0,
                                   opens_chunk=k == 0, closes_chunk=k + 2 == unit["kts"],
                                   use=BANK_USES[bank]))
            chunk += 1
        unit["chunks_after"] = chunk
    CHUNKS = chunk
    EMPTIED = {(UNITS[p["unit"]]["stage"], UNITS[p["unit"]]["i"], p["j"]): (p["bank"], p["use"]) for p in PIECES}
    LOOP_UNITS, LOOP_CHUNKS = 8, 8 * TT

    TIMELINE = []
    placed = [0]

    before_gdn = min(n for n, p in enumerate(PIECES)
                     if (UNITS[p["unit"]]["stage"], UNITS[p["unit"]]["i"]) == ("branch", 4))
    limit = [before_gdn]

    def dense(n):
        n = min(n, limit[0] - placed[0])
        placed[0] += n
        if n:
            TIMELINE.append(("dense", n))

    def dense_to(stage_name, i=0):
        end = max(n for n, p in enumerate(PIECES)
                  if (UNITS[p["unit"]]["stage"], UNITS[p["unit"]]["i"]) == (stage_name, i)) + 1
        dense(end - placed[0])

    def step(name, *i):
        TIMELINE.append((name, *i))

    for i in range(TT):
        step("norm", i)
        if i:
            step("norm_T", i - 1)
    step("norm_T", TT - 1)
    heads = 0
    dense(TT * 2 + 2)
    for i in range(TT, TT + MT):
        step("norm", i)
        dense(1)
        step("norm_T", i)
        dense(1)
    for name, tiles in (("sbq", TT), ("sbk", TT), ("sbv", 0), ("memq", TT), ("memk", MT)):
        dense_to(name)
        for _ in range(tiles):
            if name == "sbq" or name == "sbk" or name == "memq":
                dense(2)
            step("heads_T", heads)
            heads += 1
    dense_to("memv")
    for h in range(H):
        step("sb_scores", h)
        dense(5)
        step("sb_suffix", h)
        dense(4)
        step("sb_out", h)
        dense(2)
    dense_to("conv", 2)
    dense_to("ab")
    step("decay_logits")
    for h in range(H):
        step("mem_scores", h)
        dense(2)
        step("mem_T", h)
        dense(2)
        step("mem_out", h)
        dense(2)
    LEVELS = [2, 4, 8, 16, 32]
    for t in range(TT):
        step("gdn_tok", t)
        dense(2)
        step("gdn_chan", t)
        dense(2)
        step("gdn_gram", t)
        dense(1)
        step("inv_T", t, 0)
        for lv in range(len(LEVELS)):
            dense(1)
            step("inv_X", t, lv)
            dense(1)
            step("inv_P", t, lv)
            if lv + 1 < len(LEVELS):
                dense(1)
                step("inv_T", t, lv + 1)
        dense(1)
        step("gdn_uw", t)
        for c in range(2):
            dense(1)
            step("gdn_read", t, c)
            dense(1)
            step("gdn_update", t, c)
        dense(2)
        step("gdn_out", t)
    limit[0] = len(PIECES)
    dense_to("branch", 5)
    for t in range(TT):
        step("mix_T", t)
    dense_to("wo", 1)
    for i in range(TT):
        step("norm", TT + MT + i)
        if i:
            step("norm_T", TT + MT + i - 1)
    step("norm_T", TT + MT + TT - 1)
    assert placed[0] == len(PIECES)

    ctx = ExitStack()
    with ctx:
        def sb(name, shape, dt=F32):
            return ctx.enter_context(nc.sbuf_tensor(name, shape, dt))

        w_raw = sb("w_raw", [P, 2, KU * UW])
        w_hi = sb("w_hi", [P, 2, KU * UW], F32R)
        w_lo = sb("w_lo", [P, 2, KU * UW], F32R)
        act_A = sb("act_A", [P, 2, KT, SEQ], F32R)
        act_B = sb("act_B", [P, 2, KT, SEQ], F32R)
        ACTS = {"A": act_A, "B": act_B}
        slab_S = sb("slab_S", [P, 12, UW])
        slab_C = sb("slab_C", [P, 12, UW])
        slab_M = sb("slab_M", [P, 8, UW])
        slab_Z = sb("slab_Z", [P, TT, UW])
        work = sb("work", [P, 8, UW])
        sbq_T, sbk_T, sb_v = slab_S[:, 0:4, :], slab_S[:, 4:8, :], slab_S[:, 8:12, :]
        gate_t = slab_S[:, 8:12, :]
        memq_T = slab_M[:, 0:4, :]
        memk_T = slab_M[:, 4:6, :].rearrange("p a (b m) -> p (a b) m", m=N_MEM)
        mem_v = slab_M[:, 6:8, :]

        mats = sb("mats", [P, 12, P])
        ident, neg_ones, tri_inc, tri_after, neg_tri, neg_big = (mats[:, i, :] for i in range(6))
        lvl = [mats[:, 6 + i, :] for i in range(6)]
        small = sb("small", [P, 440])
        used = [0]

        def cols(n):
            used[0] += n
            return small[:, used[0] - n:used[0]]

        g1, g2, gm = cols(KT), cols(KT), cols(KT)
        g_gdn, g_sbq, g_sbk, g_mq, g_mk = cols(1), cols(1), cols(1), cols(1), cols(1)
        conv_c = cols(CONV * 3 * H).rearrange("p (w c) -> p w c", w=CONV)
        alog, dtb = cols(H), cols(H)
        ssx, rsx = cols(TT + MT + TT), cols(2)
        nt_v, nt_a, nt_i = cols(8), cols(8), cols(8)
        ssh, rsh = cols(2 * H), cols(2 * H)
        ab = cols(TT * 2 * H).rearrange("p (t c) -> p t c", c=2 * H)
        tg = cols(TT * H).rearrange("p (t c) -> p t c", c=H)
        glog = cols(TT * H).rearrange("p (t c) -> p t c", c=H)
        beta = cols(TT * H).rearrange("p (t c) -> p t c", c=H)
        gcum = cols(TT * H).rearrange("p (t c) -> p t c", c=H)
        eg = cols(TT * H).rearrange("p (t c) -> p t c", c=H)
        e2 = cols(TT * H).rearrange("p (t c) -> p t c", c=H)
        ssqk, rqk = cols(2 * H), cols(2 * H)
        sc_kb, sc_kbg, sc_kdec, sc_vb, sc_qd = cols(H), cols(H), cols(H), cols(H), cols(H)
        gl = cols(2 * H).rearrange("p (h c) -> p h c", c=2)
        sso, rso = cols(H), cols(H)
        mx, rs = cols(H), cols(H)

        banks = [ctx.enter_context(nc.psum_tensor(f"sum{i}", [P, UW], F32)) for i in range(TT)]
        pa = [ctx.enter_context(nc.psum_tensor(f"mixer{i}", [P, UW], F32)) for i in range(4)]

        def heads_of(ap):
            return ap.rearrange("p (h d) -> p h d", h=H)

        def per_head(c):
            return c.unsqueeze(2).to_broadcast([P, H, DH])

        def all_heads(m):
            return m.unsqueeze(1).to_broadcast([P, H, P])

        names = """split_begun w_split w_ready chunk_done
            par_small par_conv masks_step masks_ready x_landed0 x_landed1 x_landed2 x_landed3 m_landed0 m_landed1
            x_again stored
            norm_ss norm_scaled norm_T_done norm_gained norm_hi act_ready
            gain_scaled head_scaled head_T_done head_ready
            conv_tap ab_T_done ab_tok ab_exp ab_ln glog_ready
            decay_sums decay_exps decay_tok
            sb_scored sb_abs sb_exp sb_ln sb_soft sb_summed sb_att sb_oT sb_hi sb_ready
            ms_scored ms_top ms_max ms_exp ms_prob ms_T ms_pT ms_oT ms_hi ms_ready
            mixed
            g_tanh g_silu g_tok g_sq g_scaled g_decay_sub g_decay g_last g_lastx g_chan g_chan_act g_chan_dve g_grams
            g_tri i_T i_T_copied i_X i_X_copied i_P i_Tt i_C g_uw g_u g_w g_read g_vnew g_upd g_state
            g_o_sq g_zt g_o_scaled g_oT g_o_gained g_o_hi g_ready state_zero
            mixT_done mixT_hi mixT_ready
            up_relu up_hi up_ready dve_order act_order""".split()
        S = {n: ctx.enter_context(nc.semaphore(n)) for n in names}
        raw_landed = [ctx.enter_context(nc.semaphore(f"raw_landed{i}")) for i in range(2)]
        bank_free = [ctx.enter_context(nc.semaphore(f"bank_free{i}")) for i in range(TT)]
        block = ctx.enter_context(nc.Block())

        def wait_emptied(eng, name, i, j):
            bank, use = EMPTIED[name, i, j]
            eng.wait_ge(bank_free[bank], use)

        def wait_mixed(eng, i, j):
            if i < 2:
                wait_emptied(eng, "branch", i, j)
            else:
                eng.wait_ge(S["mixed"], TT * (i - 2) + j + 1)

        def norm_source(i):
            if i < TT:
                return slab_C[:, 2 * i:2 * i + 2, :]
            if i < TT + MT:
                return slab_C[:, 8 + 2 * (i - TT):10 + 2 * (i - TT), :]
            return slab_C[:, 2 * (i - TT - MT):2 * (i - TT - MT) + 2, :]

        def norm_dest(i, half, part):
            buf, t = (act_A, i) if i < TT else (act_B, i - TT) if i < TT + MT else (act_B, i - TT - MT)
            return buf[:, part, KU * half:KU * half + KU, t * P:(t + 1) * P]

        HEADS = ([(sbq_T, t, g_sbq) for t in range(TT)] + [(sbk_T, t, g_sbk) for t in range(TT)] +
                 [(memq_T, t, g_mq) for t in range(TT)] + [(memk_T, t, g_mk) for t in range(MT)])
        HEAD_STAGE = {"sbq": 0, "sbk": TT, "memq": 2 * TT, "memk": 3 * TT}
        SBO = [0, SEQ, 2 * SEQ - P, 3 * SEQ - 3 * P, 4 * SEQ - 6 * P]
        SBW = SBO[TT]
        sb_flat = work.rearrange("p a n -> p (a n)")
        sb_soft, sb_exps, sb_att = (sb_flat[:, i * SBW:(i + 1) * SBW] for i in range(3))
        sb_bank = [pa[0][:, 0:SEQ], pa[1][:, 0:SEQ - P], pa[2][:, 0:SEQ - 2 * P], pa[2][:, SEQ - 2 * P:SEQ - P]]
        G = [heads_of(slab_M[:, i, :]) for i in range(8)] + [heads_of(work[:, i, :]) for i in range(8)]
        (g_kbg, g_vb, g_kdec, g_kn, g_kb, g_qn, g_qd, g_kT, g_kbT, g_qT, g_qdT, g_at, g_lt, g_state, g_t1, g_t2) = G
        g_Tt, g_T, g_X, g_u, g_wT = g_kb, g_qn, g_qd, g_kbT, g_qT
        g_C = [g_kT, g_t1]
        g_vnew = g_T
        g_o = g_t2
        pah = [heads_of(p[:, :]) for p in pa]

        @block.sync
        def _(sp):
            for i in range(TT):
                sp.dma_start(norm_source(i), x[0, i * P:(i + 1) * P, :].rearrange("p (a n) -> p a n", a=2))\
                  .then_inc(S[f"x_landed{i}"], 16)
                if i == 0:
                    for u in range(2):
                        sp.dma_start(w_raw[:, u, :].rearrange("p (t n) -> p t n", t=KU), UNITS[u]["src"])\
                          .then_inc(raw_landed[u], 16)
            for i in range(MT):
                sp.dma_start(norm_source(TT + i), mem[0, i * P:(i + 1) * P, :].rearrange("p (a n) -> p a n", a=2))\
                  .then_inc(S[f"m_landed{i}"], 16)
            for u in range(2, NU):
                if UNITS[u]["stage"] == "wo" and UNITS[u]["first"] and UNITS[u]["i"] == 0:
                    sp.wait_ge(S["g_tok"], 3 * TT)
                    for t in range(TT):
                        sp.dma_start(norm_source(t), x[0, t * P:(t + 1) * P, :].rearrange("p (a n) -> p a n", a=2))\
                          .then_inc(S["x_again"], 16)
                sp.wait_ge(S["w_ready"], u - 1)
                kts = UNITS[u]["kts"]
                sp.dma_start(w_raw[:, u % 2, 0:kts * UNITS[u]["src"].shape[2]].rearrange("p (t n) -> p t n", t=kts),
                             UNITS[u]["src"]).then_inc(raw_landed[u % 2], 16)
            with sp.Fori(0, QUARTERS) as q:
                for n in range(LOOP_UNITS):
                    u = NU + n
                    if n < 4:
                        src = wup[:, KU * (n % 2):KU * (n % 2) + KU, bass.ds(q * D + (n // 2) * UW, UW)]
                    else:
                        src = wdown[:, bass.ds(q * KT + KU * (n % 2), KU), (n // 2 - 2) * UW:(n // 2 - 1) * UW]
                    sp.wait_ge(S["w_ready"], u - 1 + q * LOOP_UNITS)
                    sp.dma_start(w_raw[:, u % 2, :].rearrange("p (t n) -> p t n", t=KU), src)\
                      .then_inc(raw_landed[u % 2], 16)
            for half in range(2):
                for t in range(TT):
                    sp.wait_ge(bank_free[t], BANK_USES[t] + (QUARTERS - 1) * 4 + 3 + half)
                    sp.dma_start(out[0, t * P:(t + 1) * P, half * UW:(half + 1) * UW], slab_C[:, 2 * t + half, :])\
                      .then_inc(S["stored"], 16)
            sp.wait_ge(S["stored"], 16 * 2 * TT)

        @block.gpsimd
        def _(pool):
            sel = [0]

            def then(ins):
                sel[0] += 1
                ins.then_inc(S["masks_step"], 1)
                pool.wait_ge(S["masks_step"], sel[0])

            def blocks(dst, size, value):
                v = dst.rearrange("p (b s) -> p b s", s=size)
                then(pool.memset(dst, value))
                then(pool.affine_select(out=v, in_=v, compare_op=ALU.is_ge, fill=0.0, base=0,
                                        pattern=[[-size, P // size], [0, size]], channel_multiplier=1))
                then(pool.affine_select(out=v, in_=v, compare_op=ALU.is_ge, fill=0.0, base=size - 1,
                                        pattern=[[size, P // size], [0, size]], channel_multiplier=-1))

            def triangle(dst, base, step_p, step_f, fill=0.0):
                then(pool.affine_select(out=dst, in_=dst, compare_op=ALU.is_ge, fill=fill, base=base,
                                        pattern=[[step_f, P]], channel_multiplier=step_p))

            blocks(ident, 1, 1.0)
            then(pool.memset(neg_ones, -1.0))
            then(pool.memset(neg_tri, -1.0))
            triangle(neg_tri, 0, 1, -1)
            then(pool.memset(neg_big, 0.0))
            triangle(neg_big, -1, -1, 1, fill=MASKED)
            blocks(tri_inc, CHUNK, 1.0)
            triangle(tri_inc, 0, -1, 1)
            blocks(tri_after, CHUNK, 1.0)
            triangle(tri_after, -1, 1, -1)
            for n in range(6):
                blocks(lvl[n], 2 << n, 1.0)
            for n in range(5, 0, -1):
                then(pool.tensor_tensor(lvl[n], lvl[n], lvl[n - 1], ALU.subtract))
            for n in range(6):
                triangle(lvl[n], -1, -1, 1)
            pool.memset(nt_i, 0.0).then_inc(S["masks_ready"], 1)

            def split(u_slot, n, landed, freed, count):
                pool.wait_ge(raw_landed[u_slot], landed)
                if freed is not None:
                    pool.wait_ge(S["chunk_done"], freed)
                pool.sem_inc(S["split_begun"], 1)
                pool.tensor_copy(w_hi[:, u_slot, 0:n], w_raw[:, u_slot, 0:n]).then_inc(S["w_split"], 1)
                pool.wait_ge(S["w_split"], count)
                pool.tensor_tensor(w_lo[:, u_slot, 0:n], w_raw[:, u_slot, 0:n],
                                   w_hi[:, u_slot, 0:n].bitcast(F32), ALU.subtract).then_inc(S["w_ready"], 1)

            for u, unit in enumerate(UNITS):
                split(u % 2, unit["kts"] * unit["src"].shape[2], 16 * (u // 2 + 1),
                      UNITS[u - 2]["chunks_after"] if u >= 2 else None, u + 1)
            with pool.Fori(0, QUARTERS) as q:
                for n in range(LOOP_UNITS):
                    u = NU + n
                    freed = UNITS[u - 2]["chunks_after"] if n < 2 else CHUNKS + (n - 1) * TT
                    split(u % 2, KU * UW, 16 * (u // 2 + 1) + q * (8 * LOOP_UNITS), freed + q * LOOP_CHUNKS,
                          u + 1 + q * LOOP_UNITS)

        @block.tensor
        def _(pe):
            at = [0]

            def product(dst, lhs, rhs, first, last):
                pe.matmul(dst, lhs[0], rhs[0], start=first, stop=False)
                pe.matmul(dst, lhs[0], rhs[1], start=False, stop=False)
                return pe.matmul(dst, lhs[1], rhs[0], start=False, stop=last)

            def weights(slot, n, a, b):
                v = [w[:, slot, 0:n] for w in (w_hi, w_lo)]
                return [w[:, a:b] for w in v]

            def piece(p):
                unit = UNITS[p["unit"]]
                slot, j, act = p["unit"] % 2, p["j"], ACTS[unit["act"]]
                width = unit["src"].shape[2]
                if p["opens_unit"]:
                    pe.wait_ge(S["w_ready"], p["unit"] + 1)
                if p["opens_chunk"]:
                    if unit["first"] and p["use"] > 1:
                        pe.wait_ge(bank_free[p["bank"]], p["use"] - 1)
                    if unit["stage"] == "sbq":
                        pe.wait_ge(S["act_ready"], 2 * (j + 1))
                    if unit["stage"] == "memk":
                        pe.wait_ge(S["act_ready"], 2 * (TT + MT))
                    if unit["stage"] == "branch":
                        pe.wait_ge(S[("sb_ready", "ms_ready", "g_ready")[unit["i"] // 2]], H)
                    if unit["stage"] == "wo":
                        pe.wait_ge(S["mixT_ready"], 2 * (j + 1))
                for k in range(p["k"], p["k"] + 2):
                    w = weights(slot, unit["kts"] * width, k * width, (k + 1) * width)
                    opens, closes = unit["first"] and k == 0, unit["last"] and k == unit["kts"] - 1
                    kt = unit["kt0"] + k
                    if unit["kind"] == "tok":
                        a = [act[:, part, kt, j * P:(j + 1) * P] for part in range(2)]
                        last = product(banks[p["bank"]][:, :], a, w, opens, closes)
                    else:
                        a = [act[:, part, kt, :] for part in range(2)]
                        last = product(banks[p["bank"]][:, :], [v[:, j * P:(j + 1) * P] for v in w], a, opens, closes)
                if p["closes_chunk"]:
                    last.then_inc(S["chunk_done"], 1)

            def four(dst, lhs, rhs, transpose=False):
                for h in range(H):
                    if transpose:
                        last = pe.transpose(dst[:, h, :], lhs[:, h, :], ident)
                    else:
                        last = pe.matmul(dst[:, h, :], lhs[:, h, :], rhs[:, h, :], start=True, stop=True)
                return last

            pe.wait_ge(S["masks_ready"], 1)
            for what, *i in TIMELINE:
                if what == "dense":
                    for _ in range(i[0]):
                        piece(PIECES[at[0]])
                        at[0] += 1
                elif what == "norm_T":
                    n = i[0]
                    pe.wait_ge(S["norm_scaled"], n + 1)
                    if n >= TT + MT and n < TT + MT + 2:
                        pe.wait_ge(S["mixT_ready"], 2 * TT)
                    xn = work[:, 2 * (n % 2):2 * (n % 2) + 2, :]
                    for half in range(2):
                        if n >= 2:
                            pe.wait_ge(S["norm_gained"], 2 * (n - 2) + half + 1)
                        for k in range(KU):
                            last = pe.transpose(pah[2 * (n % 2) + half][:, k, :], xn[:, half, k * P:(k + 1) * P], ident)
                        last.then_inc(S["norm_T_done"], 1)
                elif what == "heads_T":
                    m = i[0]
                    pe.wait_ge(S["head_scaled"], m + 1)
                    if m < 4:
                        pe.wait_ge(S["norm_gained"], 2 * (TT + MT))
                    else:
                        pe.wait_ge(S["head_ready"], m - 3)
                    four(pah[m % 4], heads_of(work[:, 6 + m % 2, :]), None, transpose=True)\
                        .then_inc(S["head_T_done"], 1)
                elif what == "sb_scores":
                    h = i[0]
                    pe.wait_ge(S["head_ready"], 3 * TT + MT)
                    if h:
                        pe.wait_ge(S["sb_att"], 3 * h)
                    for j in range(TT):
                        alone = j < 3
                        pe.matmul(sb_bank[j], sbk_T[:, h, j * P:(j + 1) * P], sbq_T[:, h, j * P:SEQ],
                                  start=alone, stop=False, skip_group_check=True)
                        pe.matmul(sb_bank[j][:, 0:P], ident, neg_big, start=False, stop=True,
                                  skip_group_check=True).then_inc(S["sb_scored"], 1)
                elif what == "sb_suffix":
                    h = i[0]
                    pe.wait_ge(S["sb_soft"], 3 * (h + 1))
                    for j in range(TT):
                        last = pe.matmul(sb_bank[j], neg_tri, sb_soft[:, SBO[j]:SBO[j + 1]], start=False, stop=True,
                                         skip_group_check=True)
                        for j2 in range(j + 1, TT):
                            last = pe.matmul(sb_bank[j][:, (j2 - j) * P:], neg_ones, sb_soft[:, SBO[j2]:SBO[j2 + 1]],
                                             start=False, stop=True, skip_group_check=True)
                        last.then_inc(S["sb_summed"], 1)
                elif what == "sb_out":
                    h = i[0]
                    pe.wait_ge(S["sb_att"], 3 * (h + 1))
                    for j in range(TT):
                        wait_emptied(pe, "sbv", 0, j)
                    if h:
                        pe.wait_ge(S["sb_ready"], h)
                    for j in range(TT):
                        last = pe.matmul(pa[3][:, j * P:SEQ], sb_v[:, j, h * DH:(h + 1) * DH],
                                         sb_att[:, SBO[j]:SBO[j + 1]], start=j == 0, stop=j == TT - 1,
                                         skip_group_check=True)
                    last.then_inc(S["sb_oT"], 1)
                elif what == "decay_logits":
                    wait_emptied(pe, "ab", 0, 0)
                    pe.wait_ge(S["sb_att"], 3 * H)
                    pe.wait_ge(S["sb_ready"], H)
                    for t in range(TT):
                        last = pe.transpose(pa[0][:, t * P:(t + 1) * P], work[:, 6, t * P:(t + 1) * P], ident)
                    last.then_inc(S["ab_T_done"], 1)
                    pe.wait_ge(S["glog_ready"], 1)
                    gl_all = glog.rearrange("p t c -> p (t c)")
                    pe.matmul(pa[1][:, 0:TT * H], tri_inc, gl_all, start=True, stop=True)
                    pe.matmul(pa[2][:, 0:TT * H], tri_after, gl_all, start=True, stop=True)\
                      .then_inc(S["decay_sums"], 1)
                elif what == "mem_scores":
                    h = i[0]
                    pe.wait_ge(S["decay_tok"], 1)
                    if h:
                        pe.wait_ge(S["ms_exp"], TT * h)
                        pe.wait_ge(S["ms_ready"], h)
                    for t in range(TT):
                        last = pe.matmul(pa[t // 2][:, (t % 2) * N_MEM:(t % 2 + 1) * N_MEM],
                                         memq_T[:, h, t * P:(t + 1) * P], memk_T[:, h, :], start=t % 2 == 0,
                                         stop=True, skip_group_check=True)
                    last.then_inc(S["ms_scored"], 1)
                elif what == "mem_T":
                    h = i[0]
                    pe.wait_ge(S["ms_prob"], h + 1)
                    if h:
                        pe.wait_ge(S["ms_pT"], 2 * h)
                    for m in range(MT):
                        for t in range(TT):
                            last = pe.transpose(pa[2 + m][:, t * P:(t + 1) * P],
                                                work[:, t // 2, (t % 2) * N_MEM + m * P:(t % 2) * N_MEM + (m + 1) * P],
                                                ident)
                    last.then_inc(S["ms_T"], 1)
                elif what == "mem_out":
                    h = i[0]
                    pe.wait_ge(S["ms_pT"], 2 * (h + 1))
                    for m in range(MT):
                        wait_emptied(pe, "memv", 0, m)
                        last = pe.matmul(pa[0][:, :], mem_v[:, m, h * DH:(h + 1) * DH], work[:, 2 + m, :],
                                         start=m == 0, stop=m == MT - 1)
                    last.then_inc(S["ms_oT"], 1)
                elif what == "gdn_tok":
                    t = i[0]
                    pe.wait_ge(S["ms_ready"], H)
                    if t:
                        pe.wait_ge(S["g_ready"], t)
                        pe.wait_ge(S["g_state"], 2 * t)
                    for n, part in enumerate((1, 0, 2)):
                        pe.wait_ge(S["g_silu"], 3 * t + n + 1)
                        for h in range(H):
                            last = pe.transpose(pah[n][:, h, :], slab_C[:, part * H + h, t * P:(t + 1) * P], ident)
                        last.then_inc(S["g_tok"], 1)
                    for h in range(H):
                        last = pe.matmul(pah[3][:, h, :], glog[:, t, h:h + 1].to_broadcast([P, P]), tri_inc,
                                         start=True, stop=True)
                    last.then_inc(S["g_last"], 1)
                elif what == "gdn_chan":
                    t = i[0]
                    pe.wait_ge(S["g_scaled"], t + 1)
                    pe.wait_ge(S["g_decay"], t + 1)
                    four(pah[0], g_kn, None, transpose=True)
                    four(pah[1], g_kb, None, transpose=True)
                    four(pah[2], g_qn, None, transpose=True)
                    four(pah[3], g_qd, None, transpose=True).then_inc(S["g_chan"], 1)
                elif what == "gdn_gram":
                    t = i[0]
                    pe.wait_ge(S["g_chan_act"], 2 * (t + 1))
                    pe.wait_ge(S["g_chan_dve"], 2 * (t + 1))
                    four(pah[0], g_kT, g_kbT)
                    four(pah[1], g_kT, g_qT).then_inc(S["g_grams"], 1)
                elif what == "inv_T":
                    t, n = i
                    pe.wait_ge(S["i_Tt"], 6 * t + n + 1)
                    four(pah[2], g_Tt, None, transpose=True).then_inc(S["i_T"], 1)
                elif what == "inv_X":
                    t, n = i
                    pe.wait_ge(S["i_T_copied"], 5 * t + n + 1)
                    pe.wait_ge(S["i_C"], 5 * t + n + 1)
                    four(pah[0], g_C[n % 2], g_T).then_inc(S["i_X"], 1)
                elif what == "inv_P":
                    t, n = i
                    pe.wait_ge(S["i_X_copied"], 5 * t + n + 1)
                    four(pah[1], g_X, g_Tt).then_inc(S["i_P"], 1)
                elif what == "gdn_uw":
                    t = i[0]
                    pe.wait_ge(S["i_Tt"], 6 * (t + 1))
                    four(pah[0], g_Tt, g_vb)
                    four(pah[2], g_kbg, g_Tt).then_inc(S["g_uw"], 1)
                elif what == "gdn_read":
                    t, c = i
                    r = slice(c * CHUNK, (c + 1) * CHUNK)
                    if c == 0:
                        pe.wait_ge(S["g_u"], t + 1)
                        pe.wait_ge(S["g_w"], t + 1)
                    if t == 0 and c == 0:
                        pe.wait_ge(S["state_zero"], 1)
                    else:
                        pe.wait_ge(S["g_state"], 2 * t + c)
                    for h in range(H):
                        last = pe.matmul(pah[0][r, h, :], g_wT[:, h, r], g_state[:, h, :], start=True, stop=True)
                    last.then_inc(S["g_read"], 1)
                elif what == "gdn_update":
                    t, c = i
                    r = slice(c * CHUNK, (c + 1) * CHUNK)
                    pe.wait_ge(S["g_vnew"], 2 * t + c + 1)
                    for h in range(H):
                        pe.matmul(pah[1][r, h, :], g_qdT[:, h, r], g_state[:, h, :], start=True, stop=False)
                        pe.matmul(pah[1][r, h, :], g_at[r, h, r], g_vnew[r, h, :], start=False, stop=True)
                    for h in range(H):
                        last = pe.matmul(pah[2][:, h, :], g_kdec[r, h, :], g_vnew[r, h, :], start=True, stop=True)
                    last.then_inc(S["g_upd"], 1)
                elif what == "gdn_out":
                    t = i[0]
                    pe.wait_ge(S["g_o_scaled"], t + 1)
                    four(pah[3], g_o, None, transpose=True).then_inc(S["g_oT"], 1)
                elif what == "mix_T":
                    t = i[0]
                    for half in range(2):
                        wait_mixed(pe, 4 + half, t)
                    if t >= 2:
                        pe.wait_ge(S["mixT_ready"], 2 * (t - 1))
                    else:
                        pe.wait_ge(S["g_ready"], TT)
                    for half in range(2):
                        for k in range(KU):
                            last = pe.transpose(pah[2 * (t % 2) + half][:, k, :],
                                                slab_S[:, 2 * t + half, k * P:(k + 1) * P], ident)
                        last.then_inc(S["mixT_done"], 1)

            with pe.Fori(0, QUARTERS) as q:
                for n in range(LOOP_UNITS):
                    slot = (NU + n) % 2
                    pe.wait_ge(S["w_ready"], NU + n + 1 + q * LOOP_UNITS)
                    up, half = n < 4, n % 2
                    if n == 0:
                        pe.wait_ge(S["act_ready"], 2 * (TT + MT + TT))
                    for j in range(TT):
                        if half == 0:
                            pe.wait_ge(bank_free[j], BANK_USES[j] + n // 2 + q * (LOOP_UNITS // 2))
                        if n >= 4 and n < 6 and j == 0:
                            pe.wait_ge(S["up_ready"], KU * (half + 1) + q * (2 * KU))
                        for k in range(KU):
                            kt = KU * half + k
                            w = weights(slot, KU * UW, k * UW, (k + 1) * UW)
                            if up:
                                last = product(banks[j][:, :], [v[:, j * P:(j + 1) * P] for v in w],
                                               [act_B[:, part, kt, :] for part in range(2)], kt == 0, kt == KT - 1)
                            else:
                                last = product(banks[j][:, :],
                                               [act_A[:, part, kt, j * P:(j + 1) * P] for part in range(2)], w,
                                               kt == 0, kt == KT - 1)
                        last.then_inc(S["chunk_done"], 1)

        @block.scalar
        def _(act):
            at, order = [0], [0]

            def link(ins):
                order[0] += 1
                ins.then_inc(S["act_order"], 1)
                act.wait_ge(S["act_order"], order[0])

            with nc.allow_non_contiguous_dma(reason="small parameters"):
                for dst, src in ((g1, norm1_g), (gm, mem_norm_g), (g2, norm2_g)):
                    act.dma_start(dst, src[0].rearrange("(t p) -> p t", p=P)).then_inc(S["par_small"], 16)
                for dst, src in ((g_gdn, gdn_norm_g), (g_sbq, sb_q_norm_g), (g_sbk, sb_k_norm_g),
                                 (g_mq, mem_q_norm_g), (g_mk, mem_k_norm_g)):
                    act.dma_start(dst, src[0].rearrange("(p a) -> p a", a=1)).then_inc(S["par_small"], 16)
                for dst, src in ((alog, a_log), (dtb, dt_bias)):
                    act.dma_start(dst, src[0].partition_broadcast(P)).then_inc(S["par_small"], 16)
                for w in range(CONV):
                    act.dma_start(conv_c[:, w, :], conv_w[0, w].rearrange("(c p) -> p c", p=P)).then_inc(S["par_conv"], 16)

            def evacuate(p):
                unit, j, bank = UNITS[p["unit"]], p["j"], p["bank"]
                name = unit["stage"]
                act.wait_ge(S["chunk_done"], p["chunk"] + 1)
                src = banks[bank][:, :]
                if name in HEAD_STAGE:
                    m = HEAD_STAGE[name] + j
                    if m >= 2:
                        act.wait_ge(S["head_scaled"], m - 1)
                    act.activation(slab_Z[:, m % 2, :], src, ACT.Copy)
                    act.activation(slab_Z[:, 2 + m % 2, :], src, ACT.Square).then_inc(bank_free[bank], 1)
                elif name == "sbv":
                    act.activation(sb_v[:, j, :], src, ACT.Copy).then_inc(bank_free[bank], 1)
                elif name == "memv":
                    act.activation(mem_v[:, j, :], src, ACT.Copy).then_inc(bank_free[bank], 1)
                elif name == "conv":
                    act.activation(slab_C[:, unit["i"] * H + j, :], src, ACT.Copy,
                                   scale=conv_c[:, CONV - 1, unit["i"] * H + j:unit["i"] * H + j + 1])\
                       .then_inc(S["conv_tap"], 1)
                elif name == "ab":
                    act.activation(work[:, 6, :], src, ACT.Copy).then_inc(bank_free[bank], 1)
                elif name == "z":
                    act.activation(slab_Z[:, j, :], src, ACT.Copy).then_inc(bank_free[bank], 1)
                elif name == "gate":
                    if unit["i"]:
                        wait_mixed(act, unit["i"] - 1, j)
                    act.activation(gate_t[:, j, :], src, ACT.Tanh, scale=0.5).then_inc(bank_free[bank], 1)

            act.wait_ge(S["par_small"], 160)
            for what, *i in TIMELINE:
                if what == "dense":
                    for _ in range(i[0]):
                        p = PIECES[at[0]]
                        at[0] += 1
                        if p["closes_chunk"] and UNITS[p["unit"]]["last"]:
                            evacuate(p)
                elif what == "norm":
                    n = i[0]
                    if n < TT:
                        act.wait_ge(S[f"x_landed{n}"], 16)
                    elif n < TT + MT:
                        act.wait_ge(S[f"m_landed{n - TT}"], 16)
                    else:
                        for half in range(2):
                            wait_emptied(act, "wo", half, n - TT - MT)
                    if n >= 2:
                        act.wait_ge(S["norm_T_done"], 2 * (n - 1))
                    act.activation(work[:, 2 * (n % 2):2 * (n % 2) + 2, :], norm_source(n), ACT.Square,
                                   accum_out=ssx[:, n:n + 1]).then_inc(S["norm_ss"], 1)
                elif what == "norm_T":
                    n = i[0]
                    for half in range(2):
                        act.wait_ge(S["norm_gained"], 2 * n + half + 1)
                        act.activation(norm_dest(n, half, 0), heads_of(work[:, 4 + half, :]), ACT.Copy)\
                           .then_inc(S["norm_hi"], 1)
                elif what == "heads_T":
                    m = i[0]
                    dst, t, gain = HEADS[m]
                    if m == 0:
                        act.wait_ge(S["gain_scaled"], 1)
                    act.wait_ge(S["head_T_done"], m + 1)
                    act.activation(dst[:, :, t * P:(t + 1) * P], pah[m % 4], ACT.Copy, scale=gain)\
                       .then_inc(S["head_ready"], 1)
                elif what == "sb_scores":
                    h = i[0]
                    for j, width in ((0, SEQ), (1, SEQ - P), (2, SEQ - P)):
                        act.wait_ge(S["sb_scored"], TT * h + (j + 1 if j < 2 else TT))
                        act.activation(sb_exps[:, SBO[j]:SBO[j] + width], pa[j][:, 0:width], ACT.Abs)\
                           .then_inc(S["sb_abs"], 1)
                    act.wait_ge(S["sb_abs"], 3 * (h + 1))
                    act.activation(sb_exps, sb_exps, ACT.Exp, scale=-1.0).then_inc(S["sb_exp"], 1)
                    act.wait_ge(S["sb_exp"], h + 1)
                    act.activation(sb_exps, sb_exps, ACT.Ln, bias=1.0).then_inc(S["sb_ln"], 1)
                elif what == "sb_suffix":
                    h = i[0]
                    if h:
                        act.wait_ge(S["sb_oT"], h)
                    for n, (j, width) in enumerate(((0, SEQ), (1, SEQ - P), (2, SEQ - P))):
                        act.wait_ge(S["sb_summed"], TT * h + (j + 1 if j < 2 else TT))
                        act.activation(sb_att[:, SBO[j]:SBO[j] + width], pa[j][:, 0:width], ACT.Exp)\
                           .then_inc(S["sb_att"], 1)
                elif what == "sb_out":
                    h = i[0]
                    act.wait_ge(S["sb_oT"], h + 1)
                    act.activation(act_B[:, 0, h, :], pa[3][:, :], ACT.Copy).then_inc(S["sb_hi"], 1)
                elif what == "decay_logits":
                    act.wait_ge(S["ab_tok"], 1)
                    link(act.activation(gcum, tg, ACT.Abs))
                    act.activation(gcum, gcum, ACT.Exp, scale=-1.0).then_inc(S["ab_exp"], 1)
                    act.wait_ge(S["ab_exp"], 1)
                    act.activation(gcum, gcum, ACT.Ln, bias=1.0)
                    act.activation(alog, alog, ACT.Exp)
                    act.activation(beta, ab[:, :, H:2 * H], ACT.Exp, scale=-1.0).then_inc(S["ab_ln"], 1)
                    act.wait_ge(S["decay_sums"], 1)
                    act.activation(eg, pa[1][:, 0:TT * H].rearrange("p (t c) -> p t c", c=H), ACT.Exp)
                    act.activation(e2, pa[2][:, 0:TT * H].rearrange("p (t c) -> p t c", c=H), ACT.Exp)\
                       .then_inc(S["decay_exps"], 1)
                elif what == "mem_scores":
                    h = i[0]
                    act.wait_ge(S["ms_max"], h + 1)
                    for t in range(TT):
                        act.activation(work[:, t // 2, (t % 2) * N_MEM:(t % 2 + 1) * N_MEM],
                                       pa[t // 2][:, (t % 2) * N_MEM:(t % 2 + 1) * N_MEM], ACT.Exp,
                                       bias=mx[:, t:t + 1], accum_out=rs[:, t:t + 1]).then_inc(S["ms_exp"], 1)
                elif what == "mem_T":
                    h = i[0]
                    act.wait_ge(S["ms_T"], h + 1)
                    if h:
                        act.wait_ge(S["ms_oT"], h)
                    for m in range(MT):
                        act.activation(work[:, 2 + m, :], pa[2 + m][:, :], ACT.Copy).then_inc(S["ms_pT"], 1)
                elif what == "mem_out":
                    h = i[0]
                    act.wait_ge(S["ms_oT"], h + 1)
                    act.activation(act_B[:, 0, H + h, :], pa[0][:, :], ACT.Copy).then_inc(S["ms_hi"], 1)
                elif what == "gdn_tok":
                    t = i[0]
                    for n, part in enumerate((1, 0, 2)):
                        if n == 0:
                            for part2 in range(3):
                                for h in range(H):
                                    wait_emptied(act, "conv", part2, h)
                            act.wait_ge(S["ms_ready"], H)
                            if t:
                                act.wait_ge(S["g_ready"], t)
                        act.activation((g_kn, g_t1, g_t2)[n], slab_C[:, part * H:(part + 1) * H, t * P:(t + 1) * P],
                                       ACT.Tanh, scale=0.5).then_inc(S["g_tanh"], 1)
                    for n in range(2):
                        act.wait_ge(S["g_tok"], 3 * t + n + 1)
                        act.wait_ge(S["g_silu"], 3 * t + 2 + n)
                        act.activation((g_t1, g_t2)[n], pah[n], ACT.Square).then_inc(S["g_sq"], 1)
                    act.wait_ge(S["g_last"], t + 1)
                    act.activation(gl, pah[3][:, :, CHUNK - 1::CHUNK], ACT.Exp).then_inc(S["g_lastx"], 1)
                    act.wait_ge(S["g_decay_sub"], t + 1)
                    act.activation(g_lt, g_lt, ACT.Exp).then_inc(S["g_decay"], 1)
                elif what == "gdn_chan":
                    t = i[0]
                    act.wait_ge(S["g_chan"], t + 1)
                    act.activation(g_kT, pah[0], ACT.Copy).then_inc(S["g_chan_act"], 1)
                    act.activation(g_qT, pah[2], ACT.Copy).then_inc(S["g_chan_act"], 1)
                elif what == "inv_T":
                    t, n = i
                    act.wait_ge(S["i_T"], 5 * t + n + 1)
                    act.activation(g_T, pah[2], ACT.Copy).then_inc(S["i_T_copied"], 1)
                elif what == "inv_X":
                    t, n = i
                    act.wait_ge(S["i_X"], 5 * t + n + 1)
                    act.activation(g_X, pah[0], ACT.Copy).then_inc(S["i_X_copied"], 1)
                elif what == "gdn_uw":
                    t = i[0]
                    act.wait_ge(S["g_uw"], t + 1)
                    act.activation(g_u, pah[0], ACT.Copy).then_inc(S["g_u"], 1)
                elif what == "gdn_out":
                    t = i[0]
                    wait_emptied(act, "z", 0, t)
                    act.wait_ge(S["g_vnew"], 2 * (t + 1))
                    act.activation(g_u, heads_of(slab_Z[:, t, :]), ACT.Tanh, scale=0.5).then_inc(S["g_zt"], 1)
                    act.wait_ge(S["g_upd"], 2 * (t + 1))
                    act.activation(g_X, pah[1], ACT.Square).then_inc(S["g_o_sq"], 1)
                    act.wait_ge(S["g_o_gained"], t + 1)
                    act.activation(act_B[:, 0, 0:H, t * P:(t + 1) * P], g_X, ACT.Copy).then_inc(S["g_o_hi"], 1)
                elif what == "mix_T":
                    t = i[0]
                    for half in range(2):
                        act.wait_ge(S["mixT_done"], 2 * t + half + 1)
                        act.activation(act_A[:, 0, KU * half:KU * half + KU, t * P:(t + 1) * P],
                                       pah[2 * (t % 2) + half], ACT.Copy).then_inc(S["mixT_hi"], 1)

            with act.Fori(0, QUARTERS) as q:
                for n in range(2 * KU):
                    j = n % KU
                    act.wait_ge(S["chunk_done"], CHUNKS + (2 * (n // KU) + 1) * TT + j + 1 + q * LOOP_CHUNKS)
                    b, uses = (n - 2) % KU, BANK_USES[(n - 2) % KU] + (n - 2) // KU + 1
                    act.wait_ge(bank_free[b], uses + q * 4)
                    act.activation(work[:, n % 2, :], banks[j][:, :], ACT.Relu).then_inc(S["up_relu"], 1)
                    act.wait_ge(S["up_relu"], n + 1 + q * (2 * KU))
                    act.activation(act_A[:, 0, n, :], work[:, n % 2, :], ACT.Square).then_inc(S["up_hi"], 1)

        @block.vector
        def _(dve):
            at, order = [0], [0]

            def link(ins):
                order[0] += 1
                ins.then_inc(S["dve_order"], 1)
                dve.wait_ge(S["dve_order"], order[0])

            def rsqrt(dst, src, mult, add):
                n = src.shape[1]
                v, a = nt_v[:, 0:n], nt_a[:, 0:n]
                link(dve.tensor_scalar(v, src, mult, add, ALU.mult, ALU.add))
                link(dve.tensor_scalar(a.bitcast(I32), v.bitcast(I32), 1, None, ALU.logical_shift_right))
                link(dve.tensor_scalar(dst.bitcast(I32), a.bitcast(I32), -1.0, float(0x5F3759DF), ALU.mult, ALU.add))
                for _ in range(3):
                    link(dve.tensor_tensor(a, dst, dst, ALU.mult))
                    link(dve.scalar_tensor_tensor(out=a, in0=a, scalar=-0.5, in1=v, op0=ALU.mult, op1=ALU.mult))
                    link(dve.scalar_tensor_tensor(out=dst, in0=a, scalar=1.5, in1=dst, op0=ALU.add, op1=ALU.mult))

            def evacuate(p):
                unit, j, bank = UNITS[p["unit"]], p["j"], p["bank"]
                name, src = unit["stage"], banks[p["bank"]]
                if name in HEAD_STAGE:
                    m = HEAD_STAGE[name] + j
                    wait_emptied(dve, name, 0, j)
                    ss, r = ssh[:, 0:H], rsh[:, 0:H]
                    link(dve.reduce_sum(ss, heads_of(slab_Z[:, 2 + m % 2, :]), axis=AX.X))
                    rsqrt(r, ss, 1.0 / DH, EPS)
                    if m >= 2:
                        dve.wait_ge(S["head_T_done"], m - 1)
                    dve.tensor_tensor(heads_of(work[:, 6 + m % 2, :]), heads_of(slab_Z[:, m % 2, :]), per_head(r),
                                      ALU.mult).then_inc(S["head_scaled"], 1)
                elif name == "conv":
                    c = unit["i"] * H + j
                    y = slab_C[:, c, :]
                    dve.wait_ge(S["conv_tap"], c + 1)
                    for tap in range(1, CONV):
                        w = conv_c[:, CONV - 1 - tap, c:c + 1]
                        ins = dve.scalar_tensor_tensor(out=y[:, tap:], in0=src[:, 0:SEQ - tap], scalar=w,
                                                       in1=y[:, tap:], op0=ALU.mult, op1=ALU.add)
                        if tap < CONV - 1:
                            link(ins)
                    ins.then_inc(bank_free[bank], 1)
                elif name == "branch":
                    mix = slab_S[:, 2 * j + unit["i"] % 2, :]
                    dve.wait_ge(S["chunk_done"], p["chunk"] + 1)
                    wait_emptied(dve, "gate", unit["i"], j)
                    dst = mix if unit["i"] < 2 else gate_t[:, j, :]
                    ins = dve.scalar_tensor_tensor(out=dst, in0=gate_t[:, j, :], scalar=1.0, in1=src[:, :],
                                                   op0=ALU.add, op1=ALU.mult)
                    ins.then_inc(bank_free[bank], 1)
                    if unit["i"] >= 2:
                        dve.wait_ge(bank_free[bank], p["use"])
                        dve.tensor_tensor(mix, mix, gate_t[:, j, :], ALU.add).then_inc(S["mixed"], 1)
                elif name == "wo":
                    dve.wait_ge(S["chunk_done"], p["chunk"] + 1)
                    dve.wait_ge(S["x_again"], 16 * TT)
                    x1 = slab_C[:, 2 * j + unit["i"], :]
                    dve.scalar_tensor_tensor(out=x1, in0=src[:, :], scalar=0.5, in1=x1, op0=ALU.mult, op1=ALU.add)\
                       .then_inc(bank_free[bank], 1)

            dve.wait_ge(S["masks_ready"], 1)
            dve.wait_ge(S["par_small"], 160)
            dve.wait_ge(S["par_conv"], 16 * CONV)
            link(dve.tensor_scalar(g_sbq, g_sbq, SCALE, None, ALU.mult))
            dve.tensor_scalar(g_mq, g_mq, SCALE, None, ALU.mult).then_inc(S["gain_scaled"], 1)
            for what, *i in TIMELINE:
                if what == "dense":
                    for _ in range(i[0]):
                        p = PIECES[at[0]]
                        at[0] += 1
                        if p["closes_chunk"] and UNITS[p["unit"]]["last"]:
                            evacuate(p)
                elif what == "norm":
                    n = i[0]
                    dve.wait_ge(S["norm_ss"], n + 1)
                    r = rsx[:, n % 2:n % 2 + 1]
                    rsqrt(r, ssx[:, n:n + 1], 1.0 / D, EPS)
                    dve.tensor_scalar(work[:, 2 * (n % 2):2 * (n % 2) + 2, :], norm_source(n), r, None, ALU.mult)\
                       .then_inc(S["norm_scaled"], 1)
                elif what == "norm_T":
                    n = i[0]
                    gain = g1 if n < TT else gm if n < TT + MT else g2
                    for half in range(2):
                        dve.wait_ge(S["norm_T_done"], 2 * n + half + 1)
                        if n:
                            dve.wait_ge(S["act_ready"], 2 * n + half - 1)
                        dve.tensor_tensor(heads_of(work[:, 4 + half, :]), pah[2 * (n % 2) + half],
                                          gain[:, KU * half:KU * half + KU].unsqueeze(2).to_broadcast([P, KU, P]),
                                          ALU.mult).then_inc(S["norm_gained"], 1)
                        dve.wait_ge(S["norm_hi"], 2 * n + half + 1)
                        dve.tensor_tensor(norm_dest(n, half, 1), heads_of(work[:, 4 + half, :]),
                                          norm_dest(n, half, 0).bitcast(F32), ALU.subtract)\
                           .then_inc(S["act_ready"], 1)
                elif what == "sb_scores":
                    h = i[0]
                    widths = ((0, SEQ), (1, SEQ - P), (2, SEQ - P))
                    dve.wait_ge(S["sb_ln"], h + 1)
                    if h:
                        dve.wait_ge(S["sb_summed"], TT * h)
                    for j, width in widths:
                        dve.scalar_tensor_tensor(out=sb_soft[:, SBO[j]:SBO[j] + width], in0=pa[j][:, 0:width],
                                                 scalar=0.0, in1=sb_exps[:, SBO[j]:SBO[j] + width], op0=ALU.max,
                                                 op1=ALU.add).then_inc(S["sb_soft"], 1)
                elif what == "sb_out":
                    h = i[0]
                    dve.wait_ge(S["sb_hi"], h + 1)
                    dve.tensor_tensor(act_B[:, 1, h, :], pa[3][:, :], act_B[:, 0, h, :].bitcast(F32), ALU.subtract)\
                       .then_inc(S["sb_ready"], 1)
                elif what == "decay_logits":
                    dve.wait_ge(S["ab_T_done"], 1)
                    link(dve.tensor_copy(ab, pa[0][:, :].rearrange("p (t c) -> p t c", c=P)[:, :, 0:2 * H]))
                    dve.tensor_tensor(tg, ab[:, :, 0:H], dtb.unsqueeze(1).to_broadcast([P, TT, H]), ALU.add)\
                       .then_inc(S["ab_tok"], 1)
                    dve.wait_ge(S["ab_ln"], 1)
                    link(dve.scalar_tensor_tensor(out=glog, in0=tg, scalar=0.0, in1=gcum, op0=ALU.max, op1=ALU.add))
                    dve.scalar_tensor_tensor(out=glog, in0=glog, scalar=-1.0,
                                             in1=alog.unsqueeze(1).to_broadcast([P, TT, H]), op0=ALU.mult,
                                             op1=ALU.mult).then_inc(S["glog_ready"], 1)
                    link(dve.tensor_scalar(beta, beta, 1.0, None, ALU.add))
                    link(dve.reciprocal(beta, beta))
                    dve.wait_ge(S["decay_sums"], 1)
                    dve.wait_ge(S["decay_exps"], 1)
                    dve.tensor_copy(gcum, pa[1][:, 0:TT * H].rearrange("p (t c) -> p t c", c=H))\
                       .then_inc(S["decay_tok"], 1)
                elif what == "mem_scores":
                    h = i[0]
                    dve.wait_ge(S["ms_scored"], h + 1)
                    if h:
                        dve.wait_ge(S["ms_exp"], TT * h)
                    for n in range(TT // 2):
                        dve.reduce_max(rs[:, 2 * n:2 * n + 2], pa[n][:, :].rearrange("p (t m) -> p t m", m=N_MEM),
                                       axis=AX.X).then_inc(S["ms_top"], 1)
                    dve.wait_ge(S["ms_top"], 2 * (h + 1))
                    dve.tensor_scalar(mx, rs, -1.0, None, ALU.mult).then_inc(S["ms_max"], 1)
                    dve.wait_ge(S["ms_exp"], TT * (h + 1))
                    link(dve.reciprocal(mx, rs))
                    probs = work[:, 0:2, :].rearrange("p a (b m) -> p (a b) m", m=N_MEM)
                    dve.tensor_tensor(probs, probs, mx.unsqueeze(2).to_broadcast([P, TT, N_MEM]), ALU.mult)\
                       .then_inc(S["ms_prob"], 1)
                elif what == "mem_out":
                    h = i[0]
                    dve.wait_ge(S["ms_hi"], h + 1)
                    dve.tensor_tensor(act_B[:, 1, H + h, :], pa[0][:, :], act_B[:, 0, H + h, :].bitcast(F32),
                                      ALU.subtract).then_inc(S["ms_ready"], 1)
                elif what == "gdn_tok":
                    t = i[0]
                    if t == 0:
                        dve.memset(g_state, 0.0).then_inc(S["state_zero"], 1)
                    for n, part in enumerate((1, 0, 2)):
                        c = slab_C[:, part * H:(part + 1) * H, t * P:(t + 1) * P]
                        for h in range(1):
                            dve.wait_ge(S["g_tanh"], 3 * t + n + 1)
                            dve.scalar_tensor_tensor(out=c, in0=(g_kn, g_t1, g_t2)[n], scalar=1.0, in1=c,
                                                     op0=ALU.add, op1=ALU.mult).then_inc(S["g_silu"], 1)
                    dve.wait_ge(S["g_last"], t + 1)
                    dve.wait_ge(S["g_lastx"], t + 1)
                    link(dve.tensor_tensor(g_lt, pah[3], per_head(gcum[:, t, :]), ALU.subtract))
                    dve.tensor_scalar(g_lt, g_lt, 0.0, None, ALU.min).then_inc(S["g_decay_sub"], 1)
                    for n, sq in enumerate((g_t1, g_t2)):
                        dve.wait_ge(S["g_sq"], 2 * t + n + 1)
                        link(dve.reduce_sum(ssqk[:, n * H:(n + 1) * H], sq, axis=AX.X))
                    rsqrt(rqk, ssqk, 1.0, 4.0 * EPS)
                    rk, rq = rqk[:, 0:H], rqk[:, H:2 * H]
                    link(dve.tensor_scalar(rq, rq, SCALE, None, ALU.mult))
                    link(dve.tensor_tensor(sc_kb, rk, beta[:, t, :], ALU.mult))
                    link(dve.tensor_tensor(sc_kbg, sc_kb, eg[:, t, :], ALU.mult))
                    link(dve.tensor_tensor(sc_kdec, rk, e2[:, t, :], ALU.mult))
                    link(dve.tensor_scalar(sc_vb, beta[:, t, :], 0.5, None, ALU.mult))
                    link(dve.tensor_tensor(sc_qd, rq, eg[:, t, :], ALU.mult))
                    dve.wait_ge(S["g_tok"], 3 * (t + 1))
                    for dst, n, scale in ((g_kn, 0, rk), (g_kb, 0, sc_kb), (g_qn, 1, rq), (g_qd, 1, sc_qd),
                                          (g_kbg, 0, sc_kbg), (g_kdec, 0, sc_kdec), (g_vb, 2, sc_vb)):
                        ins = dve.tensor_tensor(dst, pah[n], per_head(scale), ALU.mult)
                    ins.then_inc(S["g_scaled"], 1)
                elif what == "gdn_chan":
                    t = i[0]
                    dve.wait_ge(S["g_chan"], t + 1)
                    dve.tensor_copy(g_kbT, pah[1]).then_inc(S["g_chan_dve"], 1)
                    dve.tensor_copy(g_qdT, pah[3]).then_inc(S["g_chan_dve"], 1)
                elif what == "gdn_gram":
                    t = i[0]
                    dve.wait_ge(S["g_grams"], t + 1)
                    link(dve.tensor_tensor(g_at, pah[1], g_lt, ALU.mult))
                    link(dve.tensor_tensor(g_lt, pah[0], g_lt, ALU.mult))
                    link(dve.tensor_tensor(g_Tt, g_lt, all_heads(lvl[0]), ALU.mult))
                    dve.scalar_tensor_tensor(out=g_Tt, in0=g_Tt, scalar=-1.0, in1=all_heads(ident), op0=ALU.mult,
                                             op1=ALU.add).then_inc(S["i_Tt"], 1)
                    dve.tensor_tensor(g_C[0], g_lt, all_heads(lvl[1]), ALU.mult).then_inc(S["i_C"], 1)
                    dve.tensor_tensor(g_at, g_at, all_heads(tri_inc), ALU.mult).then_inc(S["g_tri"], 1)
                elif what == "inv_P":
                    t, n = i
                    if n + 1 < len(LEVELS):
                        dve.tensor_tensor(g_C[(n + 1) % 2], g_lt, all_heads(lvl[n + 2]), ALU.mult)\
                           .then_inc(S["i_C"], 1)
                    dve.wait_ge(S["i_P"], 5 * t + n + 1)
                    dve.tensor_tensor(g_Tt, g_Tt, pah[1], ALU.subtract).then_inc(S["i_Tt"], 1)
                elif what == "gdn_uw":
                    t = i[0]
                    dve.wait_ge(S["g_uw"], t + 1)
                    dve.tensor_copy(g_wT, pah[2]).then_inc(S["g_w"], 1)
                elif what == "gdn_read":
                    t, c = i
                    r = slice(c * CHUNK, (c + 1) * CHUNK)
                    dve.wait_ge(S["g_read"], 2 * t + c + 1)
                    dve.wait_ge(S["g_u"], t + 1)
                    dve.tensor_tensor(g_vnew[r], g_u[r], pah[0][r], ALU.subtract).then_inc(S["g_vnew"], 1)
                elif what == "gdn_update":
                    t, c = i
                    dve.wait_ge(S["g_upd"], 2 * t + c + 1)
                    link(dve.tensor_tensor(g_state, g_state, per_head(gl[:, :, c]), ALU.mult))
                    dve.tensor_tensor(g_state, g_state, pah[2], ALU.add).then_inc(S["g_state"], 1)
                elif what == "gdn_out":
                    t = i[0]
                    z = heads_of(slab_Z[:, t, :])
                    dve.wait_ge(S["g_zt"], t + 1)
                    link(dve.scalar_tensor_tensor(out=z, in0=g_u, scalar=1.0, in1=z, op0=ALU.add, op1=ALU.mult))
                    dve.wait_ge(S["g_o_sq"], t + 1)
                    link(dve.reduce_sum(sso, g_X, axis=AX.X))
                    rsqrt(rso, sso, 1.0 / DH, EPS)
                    link(dve.tensor_scalar(rso, rso, 0.5, None, ALU.mult))
                    link(dve.tensor_tensor(g_o, pah[1], per_head(rso), ALU.mult))
                    dve.tensor_tensor(g_o, g_o, z, ALU.mult).then_inc(S["g_o_scaled"], 1)
                    dve.wait_ge(S["g_oT"], t + 1)
                    if t == 0:
                        for j in range(TT):
                            wait_mixed(dve, 1, j)
                    dve.tensor_scalar(g_X, pah[3], g_gdn, None, ALU.mult).then_inc(S["g_o_gained"], 1)
                    dve.wait_ge(S["g_o_hi"], t + 1)
                    dve.tensor_tensor(act_B[:, 1, 0:H, t * P:(t + 1) * P], g_X,
                                      act_B[:, 0, 0:H, t * P:(t + 1) * P].bitcast(F32), ALU.subtract)\
                       .then_inc(S["g_ready"], 1)
                elif what == "mix_T":
                    t = i[0]
                    for half in range(2):
                        dve.wait_ge(S["mixT_hi"], 2 * t + half + 1)
                        dst = act_A[:, :, KU * half:KU * half + KU, t * P:(t + 1) * P]
                        dve.tensor_tensor(dst[:, 1], pah[2 * (t % 2) + half], dst[:, 0].bitcast(F32), ALU.subtract)\
                           .then_inc(S["mixT_ready"], 1)

            with dve.Fori(0, QUARTERS) as q:
                for n in range(2 * KU):
                    dve.wait_ge(S["up_relu"], n + 1 + q * (2 * KU))
                    dve.scalar_tensor_tensor(out=work[:, 2 + n % 2, :], in0=banks[n % KU][:, :], scalar=0.0,
                                             in1=work[:, n % 2, :], op0=ALU.max, op1=ALU.mult)\
                       .then_inc(bank_free[n % KU], 1)
                    dve.wait_ge(bank_free[n % KU], BANK_USES[n % KU] + n // KU + 1 + q * 4)
                    dve.wait_ge(S["up_hi"], n + 1 + q * (2 * KU))
                    dve.tensor_tensor(act_A[:, 1, n, :], work[:, 2 + n % 2, :], act_A[:, 0, n, :].bitcast(F32),
                                      ALU.subtract).then_inc(S["up_ready"], 1)
                for n in range(2 * TT):
                    half, j = n // TT, n % TT
                    x1 = slab_C[:, 2 * j + half, :]
                    dve.wait_ge(S["chunk_done"], CHUNKS + (5 + 2 * half) * TT + j + 1 + q * LOOP_CHUNKS)
                    dve.tensor_tensor(x1, banks[j][:, :], x1, ALU.add).then_inc(bank_free[j], 1)


_INS = ["x", "mem", "norm1_g", "w_in", "conv_w", "a_log", "dt_bias", "gdn_norm_g", "sb_q_norm_g", "sb_k_norm_g",
        "mem_norm_g", "w_mem_kv", "mem_q_norm_g", "mem_k_norm_g", "w_br_gdn", "w_br_sb", "w_br_mem", "w_o",
        "norm2_g", "w_up", "w_down"]


def kernel(**inputs):
    import concourse.bacc as bacc
    from concourse.bass_utils import run_bass_kernel_spmd

    nc = bacc.Bacc("TRN2", target_bir_lowering=False, num_devices=1)
    arrays, args = {}, []
    for name in _INS:
        a = np.ascontiguousarray(inputs[name])
        arrays[f"in_{name}"] = a
        args.append(nc.dram_tensor(f"in_{name}", a.shape, mybir.dt.from_np(a.dtype), kind="ExternalInput").ap())
    shape = arrays["in_x"].shape
    args.append(nc.dram_tensor("layer_out", shape, mybir.dt.float32, kind="ExternalOutput").ap())
    hybrid_layer_kernel(nc, *args)
    return run_bass_kernel_spmd(nc, [arrays], core_ids=[0]).results[0]["layer_out"]
```

```python
import numpy as np

import concourse.bass as bass
from concourse import mybir
from contextlib import ExitStack


def hybrid_layer_kernel(nc, x, mem, norm1_g, w_in, conv_w, a_log, dt_bias, gdn_norm_g, sb_q_norm_g,
                        sb_k_norm_g, mem_norm_g, w_mem_kv, mem_q_norm_g, mem_k_norm_g, w_br_gdn,
                        w_br_sb, w_br_mem, w_o, norm2_g, w_up, w_down, out):
    F32, F32R, I32 = mybir.dt.float32, mybir.dt.float32r, mybir.dt.int32
    ALU, ACT, AX = mybir.AluOpType, mybir.ActivationFunctionType, mybir.AxisListType

    P = 128
    SEQ, D = x.shape[1], x.shape[2]
    N_MEM = mem.shape[1]
    H, DH, CHUNK = 4, 128, 64
    HW = H * DH
    EPS = 1e-6
    TT, KT = SEQ // P, D // P
    MT = N_MEM // P
    FF = w_up.shape[2]
    KU = 2
    KH = 4
    SLOTS = 4
    UW = 512
    QUARTERS = FF // D
    SCALE = float(DH) ** -0.5
    MASKED = -1e30
    CONV = conv_w.shape[1]

    C_GDN, C_Z = 0, 3 * HW
    C_AB = C_Z + HW
    C_SB = C_AB + 2 * H
    C_MEMQ = C_SB + 3 * HW
    C_GATE = C_MEMQ + HW

    win = w_in[0].rearrange("(t p) n -> p t n", p=P)
    wkv = w_mem_kv[0].rearrange("(t p) n -> p t n", p=P)
    wbr = [w[0].rearrange("(t p) n -> p t n", p=P) for w in (w_br_sb, w_br_mem, w_br_gdn)]
    wo = w_o[0].rearrange("(t p) n -> p t n", p=P)
    wup = w_up[0].rearrange("(t p) n -> p t n", p=P)
    wdown = w_down[0].rearrange("(t p) n -> p t n", p=P)

    UNITS = []

    def stage(name, i, w, col, act, kts, tiles, kind="tok", bank0=0, kt0=(0, 0), width=UW, ku=KU):
        for n, k in enumerate(range(0, kts, ku)):
            UNITS.append(dict(stage=name, i=i, src=w[:, k:k + ku, col:col + width], act=act[k // KH], kt0=kt0[k // KH] + k % KH,
                              first=n == 0, last=k + ku == kts, kind=kind,
                              outs=[(bank0 + j, j) for j in range(tiles)]))

    stage("sbq", 0, win, C_SB, "AA", KT, TT, kt0=(0, KH))
    stage("sbk", 0, win, C_SB + HW, "AA", KT, TT, kt0=(0, KH))
    stage("sbv", 0, win, C_SB + 2 * HW, "AA", KT, TT, kt0=(0, KH))
    stage("memq", 0, win, C_MEMQ, "AA", KT, TT, kt0=(0, KH))
    stage("memk", 0, wkv, 0, "BB", KT, MT, kt0=(0, KH))
    stage("memv", 0, wkv, HW, "BB", KT, MT, bank0=MT, kt0=(0, KH))
    for part in range(3):
        stage("conv", part, win, C_GDN + part * HW, "AA", KT, H, kind="chan", kt0=(0, KH))
    stage("ab", 0, win, C_AB, "AA", KT, 1, kind="chan", kt0=(0, KH), width=P, ku=KT)
    stage("z", 0, win, C_Z, "AA", KT, TT, kt0=(0, KH))
    GATE_OF = (1, 2, 0)
    BR_KT0 = (0, H, 0)
    for br in range(3):
        for half in range(2):
            stage("gate", 2 * br + half, win, C_GATE + GATE_OF[br] * D + half * UW, "AA", KT, TT, kt0=(0, KH))
            stage("branch", 2 * br + half, wbr[br], half * UW, "B", H, TT, kt0=(BR_KT0[br],))
    for half in range(2):
        stage("wo", half, wo, half * UW, "BA", KT, TT, kt0=(KH, 0))
    NU = len(UNITS)

    PIECES, BANK_USES = [], [0] * TT
    order = [(u, n) for n in range(TT) for u in range(2)]
    order += [(u, n) for u in range(2, NU) for n in range(len(UNITS[u]["outs"]))]
    for u, n in order:
        unit = UNITS[u]
        bank, j = unit["outs"][n]
        BANK_USES[bank] += unit["first"]
        ahead = {0: [-1, 0], 1: [], 2: [1, 2]}.get(u, [u]) if n == 0 else []
        PIECES.append(dict(unit=u, bank=bank, j=j, opens_unit=n == 0, use=BANK_USES[bank], done=len(PIECES) + 1,
                           ahead=ahead))
        unit["done"] = len(PIECES)
    EMPTIED = {(UNITS[p["unit"]]["stage"], UNITS[p["unit"]]["i"], p["j"]): (p["bank"], p["use"]) for p in PIECES}
    GU = KT // KU
    LOOP_GROUPS = 4
    LOOP_UNITS = LOOP_GROUPS * GU
    LOOP_PIECES = LOOP_UNITS * TT

    TIMELINE = []
    placed = [0]

    def pieces_of(stage_name, i):
        return [n for n, p in enumerate(PIECES)
                if (UNITS[p["unit"]]["stage"], UNITS[p["unit"]]["i"]) == (stage_name, i)]

    limit = [min(pieces_of("branch", 4))]

    def dense(n):
        n = max(0, min(n, limit[0] - placed[0]))
        placed[0] += n
        if n:
            TIMELINE.append(("dense", n))

    def dense_to(stage_name, i=0):
        dense(max(pieces_of(stage_name, i)) + 1 - placed[0])

    def step(name, *i):
        TIMELINE.append((name, *i))

    step("params")
    step("norm", 0, 1)
    step("norm_T", 0)
    step("norm", 1, 2)
    step("norm_T", 1)
    dense(2)
    step("norm", 2, 4)
    step("norm_T", 2)
    dense(2)
    step("norm_T", 3)
    dense(2 * TT)
    step("norm", TT, TT + MT)
    dense(3)
    for i in range(TT, TT + MT):
        step("norm_T", i)
        dense(2)
    heads = 0
    dense_to("sbq")
    for name, tiles, then in (("sbq", TT, "sbk"), ("sbk", TT, "sbv"), ("memq", TT, "memk"), ("memk", MT, "memv")):
        dense_to(name)
        dense(4 if name == "memk" else 6)
        for _ in range(tiles):
            step("heads_T", heads)
            dense(1 if then.startswith("mem") else 2)
            heads += 1
        dense_to(then)
    dense_to("memv")
    for h in range(H):
        step("sb_scores", h)
        dense(5)
        step("sb_suffix", h)
        dense(4)
        step("sb_out", h)
        dense(2)
    dense_to("conv", 2)
    for part in (1, 0, 2):
        step("silu", part)
    dense_to("ab")
    step("decay_logits")
    dense(3)
    step("decay_sums")
    dense(2)
    step("qk_squares")
    step("mem_scores", 0)
    dense(2)
    step("qk_norms")
    for h in range(H):
        if h + 1 < H:
            step("mem_scores", h + 1)
        dense(2)
        step("mem_T", h)
        dense(2)
        step("mem_out", h)
        dense(1)
    LEVELS = [2, 4, 8, 16, 32]
    tile_steps = [(1, "gdn_gram"), (1, "gdn_out"), (5, "inv_T"), (1, "inv_X", 0), (1, "gdn_oT"), (2, "inv_P", 0)]
    for lv in range(1, len(LEVELS)):
        tile_steps.append((1, "inv_X", lv))
        if lv == 1:
            tile_steps.append((0, "gdn_kT"))
        if lv == 2:
            tile_steps.append((0, "gdn_vT"))
        tile_steps.append((1, "inv_P", lv))
    tile_steps += [(1, "gdn_uw"), (1.5, "gdn_read", 0), (1, "gdn_update", 0), (1.5, "gdn_read", 1),
                   (1, "gdn_update", 1)]
    after = [(1, "gdn_gram"), (0, "gdn_out"), (5, "gdn_oT")]
    start, paced = placed[0], 0
    total = sum(TT * s[0] for s in tile_steps) + sum(s[0] for s in after)
    for t in range(TT + 1):
        for weight, name, *i in tile_steps if t < TT else after:
            paced += weight
            dense(start + int((limit[0] - start) * paced / total + 1e-6) - placed[0])
            if name == "gdn_out":
                if t:
                    step("gdn_out", t - 1)
            elif name == "gdn_oT":
                if t == 2:
                    assert placed[0] > max(pieces_of("branch", 1))
                if t > 1:
                    step("gdn_oT", t - 2)
            elif t < TT:
                step(name, t, *i)
    step("gdn_oT", TT - 1)
    limit[0] = len(PIECES)
    dense_to("branch", 4)
    for t in range(TT):
        dense(3)
        step("mix_T", 0, t)
    dense_to("branch", 5)
    dense(TT)
    for t in range(TT):
        step("mix_T", 1, t)
        dense(1)
    dense_to("wo", 0)
    for t in range(TT):
        dense(3)
        step("x1_T", 0, t)
    dense_to("wo", 1)
    for t in range(TT):
        step("x1_T", 1, t)
        step("x1_norm", t)
    assert placed[0] == len(PIECES)

    ctx = ExitStack()
    with ctx:
        def sb(name, shape, dt=F32):
            return ctx.enter_context(nc.sbuf_tensor(name, shape, dt))

        w_raw = sb("w_raw", [P, SLOTS, KU * UW])
        w_hi = sb("w_hi", [P, SLOTS, KU * UW], F32R)
        w_lo = sb("w_lo", [P, SLOTS, KU * UW], F32R)
        act_A = sb("act_A", [P, 2, KT, SEQ], F32R)
        act_B = sb("act_B", [P, 2, KT, SEQ], F32R)
        ACTS = {"A": act_A, "B": act_B}
        MIX, MLP_IN, MIDDLE = ((act_B, KH), (act_A, 0)), ((act_A, KH), (act_B, 0)), ((act_A, 0), (act_B, KH))
        slab_S = sb("slab_S", [P, 12, UW])
        slab_C = sb("slab_C", [P, 12, UW])
        slab_M = sb("slab_M", [P, 8, UW])
        slab_Z = sb("slab_Z", [P, TT, UW])
        work = sb("work", [P, 8, UW])
        sbq_T, sbk_T, sb_v = slab_S[:, 0:4, :], slab_S[:, 4:8, :], slab_S[:, 8:12, :]
        gate_t = slab_S[:, 8:12, :]
        memq_T = slab_M[:, 0:4, :]
        memk_T = slab_M[:, 4:6, :].rearrange("p a (b m) -> p (a b) m", m=N_MEM)
        mem_v = slab_M[:, 6:8, :]

        mats = sb("mats", [P, 12, P])
        ident, neg_ones, tri_inc, tri_after, neg_tri, neg_big = (mats[:, i, :] for i in range(6))
        lvl = [mats[:, 6 + i, :] for i in range(6)]
        small = sb("small", [P, 440])
        used = [0]

        def cols(n):
            used[0] += n
            return small[:, used[0] - n:used[0]]

        g1, gm, g2 = cols(KT), cols(KT), cols(KT)
        g_gdn, g_sbq, g_sbk, g_mq, g_mk = cols(1), cols(1), cols(1), cols(1), cols(1)
        conv_c = cols(CONV * 3 * H).rearrange("p (w c) -> p w c", w=CONV)
        NPAR = used[0]
        params = small[:, 0:NPAR]
        alog, dtb = cols(H), cols(H)
        ssx, rsx, mlp_scale = cols(TT + MT + TT), cols(TT + MT), cols(TT)
        nt_v, nt_a = cols(TT * H), cols(TT * H)
        ssh, rsh = cols(TT * H), cols(TT * H)
        ab = cols(TT * 2 * H).rearrange("p (t c) -> p t c", c=2 * H)
        tg = cols(TT * H).rearrange("p (t c) -> p t c", c=H)
        glog = cols(TT * H).rearrange("p (t c) -> p t c", c=H)
        beta = cols(TT * H).rearrange("p (t c) -> p t c", c=H)
        gcum = cols(TT * H).rearrange("p (t c) -> p t c", c=H)
        eg = cols(TT * H).rearrange("p (t c) -> p t c", c=H)
        e2 = cols(TT * H).rearrange("p (t c) -> p t c", c=H)
        bb, rq2, rq_half = (cols(TT * H).rearrange("p (t c) -> p t c", c=H) for _ in range(3))
        k_norm, k_dec, k_beta_decay, v_beta = tg, e2, eg, beta
        gl = cols(2 * H).rearrange("p (h c) -> p h c", c=2)
        sso, rso = cols(H), cols(H)
        mx, rs = [cols(TT), cols(TT)], [cols(TT), cols(TT)]

        banks = [ctx.enter_context(nc.psum_tensor(f"sum{i}", [P, UW], F32)) for i in range(TT)]
        pa = [ctx.enter_context(nc.psum_tensor(f"mixer{i}", [P, UW], F32)) for i in range(4)]

        def heads_of(ap):
            return ap.rearrange("p (h d) -> p h d", h=H)

        def per_head(c):
            return c.unsqueeze(2).to_broadcast([P, H, DH])

        def all_heads(m):
            return m.unsqueeze(1).to_broadcast([P, H, P])

        names = """w_high w_ready piece_done
            par_rows par_T_done par_decay params_ready masks_step ident_ready masks_ready x_landed0 x_landed1 x_landed2 x_landed3 m_landed0 m_landed1
            x_again stored
            norm_ss norm_factor norm_scaled norm_T_done norm_gained norm_hi act_ready
            gain_scaled head_scaled head_T_done head_ready
            conv_tap ab_T_done ab_tok ab_exp ab_ln glog_ready
            decay_sums decay_exps decay_tok
            sb_scored sb_abs sb_exp sb_ln sb_soft sb_summed sb_att sb_oT sb_hi sb_ready
            tanh_done silu_done qk_squared qk_summed qk_read factors_ready
            ms_scored ms_top ms_max ms_exp ms_prob ms_T ms_pT ms_oT ms_hi ms_ready
            mixed
            z_tanh g_bcast g_grams g_beta_row g_eg_row g_last g_decay_sub g_decay g_row_used g_masked g_q_dec
            g_kT_done g_vT_done g_k_scaled g_v_scaled i_T i_T_ready i_X i_X_copied i_P i_Pt i_Tt i_C g_uw g_w g_read
            g_qs g_vnew g_upd g_o_sum g_state g_o_sq g_o_scaled g_oT g_o_hi g_ready state_zero
            mixT_done mixT_hi mixT_ready x1T_done x1T_gained x1T_hi x1T_ready x1_ss mlp_scaled
            up_relu up_hi up_ready dve_order act_order""".split()
        S = {n: ctx.enter_context(nc.semaphore(n)) for n in names}
        raw_landed = [ctx.enter_context(nc.semaphore(f"raw_landed{i}")) for i in range(SLOTS)]
        bank_free = [ctx.enter_context(nc.semaphore(f"bank_free{i}")) for i in range(TT)]
        block = ctx.enter_context(nc.Block())

        def wait_emptied(eng, name, i, j):
            bank, use = EMPTIED[name, i, j]
            eng.wait_ge(bank_free[bank], use)

        def wait_mixed(eng, i, j):
            if i < 2:
                wait_emptied(eng, "branch", i, j)
            else:
                eng.wait_ge(S["mixed"], TT * (i - 2) + j + 1)

        def norm_source(i):
            return slab_C[:, 2 * i:2 * i + 2, :]

        def norm_gained(i, half):
            return heads_of(work[:, 4 + 2 * (i % 2) + half, :])

        def norm_dest(i, half, part):
            buf, t = (act_A, i) if i < TT else (act_B, i - TT)
            return buf[:, part, KH * half:KH * half + KH, t * P:(t + 1) * P]

        def held(places, half, part, cols=slice(None)):
            buf, kt = places[half]
            return buf[:, part, kt:kt + KH, cols]

        HEADS = ([(sbq_T, t, g_sbq) for t in range(TT)] + [(sbk_T, t, g_sbk) for t in range(TT)] +
                 [(memq_T, t, g_mq) for t in range(TT)] + [(memk_T, t, g_mk) for t in range(MT)])
        HEAD_STAGE = {"sbq": 0, "sbk": TT, "memq": 2 * TT, "memk": 3 * TT}
        SBO = [0, SEQ, 2 * SEQ - P, 3 * SEQ - 3 * P, 4 * SEQ - 6 * P]
        SBW = SBO[TT]
        sb_flat = work.rearrange("p a n -> p (a n)")
        sb_soft, sb_exps, sb_att = (sb_flat[:, i * SBW:(i + 1) * SBW] for i in range(3))
        sb_bank = [pa[0][:, 0:SEQ], pa[1][:, 0:SEQ - P], pa[2][:, 0:SEQ - 2 * P], pa[2][:, SEQ - 2 * P:SEQ - P]]
        ms_probs = [work[:, 4 * n:4 * n + 2, :] for n in range(2)]
        (g_kbg, g_decayed, g_lower, g_at, g_eg, g_state, g_Tt, g_T, g_X, g_C0, g_C1, g_wT, g_vnew, g_o,
         g_sq) = [heads_of(slab_M[:, i, :]) for i in range(8)] + [heads_of(work[:, i, :]) for i in range(7)]
        g_C = [g_C0, g_C1]

        def conv_tile(part, t):
            return slab_C[:, part * H:(part + 1) * H, t * P:(t + 1) * P]

        pah = [heads_of(p[:, :]) for p in pa]

        def o_bank(t):
            return pah[3]

        def load(sp, u, src, freed):
            kts, width = src.shape[1], src.shape[2]
            if freed is not None:
                sp.wait_ge(S["w_ready"], freed)
            sp.dma_start(w_raw[:, u % SLOTS, 0:kts * width].rearrange("p (t n) -> p t n", t=kts), src)\
              .then_inc(raw_landed[u % SLOTS], 16)

        @block.sync
        def _(sp):
            for i in range(TT):
                sp.dma_start(norm_source(i), x[0, i * P:(i + 1) * P, :].rearrange("p (a n) -> p a n", a=2))\
                  .then_inc(S[f"x_landed{i}"], 16)
                if i:
                    load(sp, i - 1, UNITS[i - 1]["src"], None)
            load(sp, TT - 1, UNITS[TT - 1]["src"], None)
            for i in range(MT):
                sp.dma_start(norm_source(TT + i), mem[0, i * P:(i + 1) * P, :].rearrange("p (a n) -> p a n", a=2))\
                  .then_inc(S[f"m_landed{i}"], 16)
            with nc.allow_non_contiguous_dma(reason="small parameters"):
                for dst, src in ((alog, a_log), (dtb, dt_bias)):
                    sp.dma_start(dst, src[0].partition_broadcast(P)).then_inc(S["par_decay"], 16)
            for u in range(SLOTS, NU):
                if UNITS[u]["stage"] == "branch" and UNITS[u]["first"] and UNITS[u]["i"] == 5:
                    sp.wait_ge(S["g_upd"], 2 * TT)
                    for t in range(TT):
                        sp.dma_start(norm_source(t), x[0, t * P:(t + 1) * P, :].rearrange("p (a n) -> p a n", a=2))\
                          .then_inc(S["x_again"], 16)
                load(sp, u, UNITS[u]["src"], u - SLOTS + 1)
            with sp.Fori(0, QUARTERS) as q:
                for n in range(LOOP_UNITS):
                    group, k = n // GU, KU * (n % GU)
                    if group < 2:
                        src = wup[:, k:k + KU, bass.ds(q * D + group * UW, UW)]
                    else:
                        src = wdown[:, bass.ds(q * KT + k, KU), (group - 2) * UW:(group - 1) * UW]
                    load(sp, NU + n, src, NU + n - SLOTS + 1 + q * LOOP_UNITS)
            for half in range(2):
                for t in range(TT):
                    sp.wait_ge(bank_free[t], BANK_USES[t] + (QUARTERS - 1) * LOOP_GROUPS + 3 + half)
                    sp.dma_start(out[0, t * P:(t + 1) * P, half * UW:(half + 1) * UW], slab_C[:, 2 * t + half, :])\
                      .then_inc(S["stored"], 16)
            sp.wait_ge(S["stored"], 16 * 2 * TT)

        @block.gpsimd
        def _(pool):
            sel = [0]

            def then(ins):
                sel[0] += 1
                ins.then_inc(S["masks_step"], 1)
                pool.wait_ge(S["masks_step"], sel[0])

            def blocks(dst, size, value):
                v = dst.rearrange("p (b s) -> p b s", s=size)
                then(pool.memset(dst, value))
                then(pool.affine_select(out=v, in_=v, compare_op=ALU.is_ge, fill=0.0, base=0,
                                        pattern=[[-size, P // size], [0, size]], channel_multiplier=1))
                then(pool.affine_select(out=v, in_=v, compare_op=ALU.is_ge, fill=0.0, base=size - 1,
                                        pattern=[[size, P // size], [0, size]], channel_multiplier=-1))

            def triangle(dst, base, step_p, step_f, fill=0.0):
                then(pool.affine_select(out=dst, in_=dst, compare_op=ALU.is_ge, fill=fill, base=base,
                                        pattern=[[step_f, P]], channel_multiplier=step_p))

            then(pool.memset(ident, 1.0))
            triangle(ident, 0, 1, -1)
            triangle(ident, 0, -1, 1)
            pool.sem_inc(S["ident_ready"], 1)

            def masks(n):
                if n == 0:
                    then(pool.memset(neg_ones, -1.0))
                    then(pool.memset(neg_tri, -1.0))
                    triangle(neg_tri, 0, 1, -1)
                    then(pool.memset(neg_big, 0.0))
                    triangle(neg_big, -1, -1, 1, fill=MASKED)
                elif n == 1:
                    blocks(tri_inc, CHUNK, 1.0)
                    triangle(tri_inc, 0, -1, 1)
                    blocks(tri_after, CHUNK, 1.0)
                    triangle(tri_after, -1, 1, -1)
                elif n < 8:
                    blocks(lvl[n - 2], 2 << (n - 2), 1.0)
                elif n == 8:
                    for m in range(5, 0, -1):
                        then(pool.tensor_tensor(lvl[m], lvl[m], lvl[m - 1], ALU.subtract))
                elif n == 9:
                    for m in range(6):
                        triangle(lvl[m], -1, -1, 1)
                    pool.sem_inc(S["masks_ready"], 1)

            def low_part(u, n, count):
                slot = u % SLOTS
                pool.wait_ge(S["w_high"], count)
                pool.tensor_tensor(w_lo[:, slot, 0:n], w_raw[:, slot, 0:n], w_hi[:, slot, 0:n].bitcast(F32),
                                   ALU.subtract).then_inc(S["w_ready"], 1)

            for u, unit in enumerate(UNITS):
                low_part(u, unit["src"].shape[1] * unit["src"].shape[2], u + 1)
                if u >= SLOTS - 1:
                    masks(u - SLOTS + 1)
            with pool.Fori(0, QUARTERS) as q:
                for n in range(LOOP_UNITS):
                    low_part(NU + n, KU * UW, NU + n + 1 + q * LOOP_UNITS)

        @block.tensor
        def _(pe):
            at = [0]

            def product(dst, lhs, rhs, first, last):
                pe.matmul(dst, lhs[0], rhs[0], start=first, stop=False)
                pe.matmul(dst, lhs[0], rhs[1], start=False, stop=False)
                return pe.matmul(dst, lhs[1], rhs[0], start=False, stop=last)

            def weights(slot, n, a, b):
                v = [w[:, slot, 0:n] for w in (w_hi, w_lo)]
                return [w[:, a:b] for w in v]

            def piece(p):
                unit = UNITS[p["unit"]]
                slot, j, act = p["unit"] % SLOTS, p["j"], ACTS[unit["act"]]
                kts, width = unit["src"].shape[1], unit["src"].shape[2]
                if p["opens_unit"]:
                    pe.wait_ge(S["w_ready"], p["unit"] + 1)
                if unit["first"] and p["use"] > 1:
                    pe.wait_ge(bank_free[p["bank"]], p["use"] - 1)
                if unit["stage"] == "sbq" and unit["first"]:
                    pe.wait_ge(S["act_ready"], 2 * (j + 1))
                if unit["stage"] == "memk" and p["opens_unit"]:
                    pe.wait_ge(S["act_ready"], 2 * (TT + MT))
                if unit["stage"] == "branch" and p["opens_unit"]:
                    pe.wait_ge(S[("sb_ready", "ms_ready", "g_ready")[unit["i"] // 2]], H)
                if unit["stage"] == "wo":
                    half = (unit["act"], unit["kt0"] // KH) != ("B", 1)
                    pe.wait_ge(S["mixT_ready"], half * TT + j + 1)
                for k in range(kts):
                    w = weights(slot, kts * width, k * width, (k + 1) * width)
                    opens, closes = unit["first"] and k == 0, unit["last"] and k == kts - 1
                    kt = unit["kt0"] + k
                    if unit["kind"] == "tok":
                        a = [act[:, part, kt, j * P:(j + 1) * P] for part in range(2)]
                        last = product(banks[p["bank"]][:, :], a, w, opens, closes)
                    else:
                        a = [act[:, part, kt, :] for part in range(2)]
                        last = product(banks[p["bank"]][:, :], [v[:, j * P:(j + 1) * P] for v in w], a, opens, closes)
                last.then_inc(S["piece_done"], 1)

            def four(dst, lhs, rhs, transpose=False):
                for h in range(H):
                    if transpose:
                        last = pe.transpose(dst[:, h, :], lhs[:, h, :], ident)
                    else:
                        last = pe.matmul(dst[:, h, :], lhs[:, h, :], rhs[:, h, :], start=True, stop=True)
                return last

            pe.wait_ge(S["ident_ready"], 1)
            for what, *i in TIMELINE:
                if what == "dense":
                    for _ in range(i[0]):
                        piece(PIECES[at[0]])
                        at[0] += 1
                elif what == "params":
                    pe.wait_ge(S["par_rows"], 16 * 9)
                    pe.transpose(pa[3][:, 0:NPAR], work[0:NPAR, 3, 0:P], ident[0:NPAR, 0:NPAR])\
                      .then_inc(S["par_T_done"], 1)
                elif what == "norm_T":
                    n = i[0]
                    pe.wait_ge(S["norm_scaled"], n + 1)
                    if n == 1:
                        pe.wait_ge(S["params_ready"], 1)
                    xn = norm_source(n)
                    for half in range(2):
                        if n >= 2:
                            pe.wait_ge(S["norm_gained"], 2 * (n - 2) + half + 1)
                        for k in range(KH):
                            last = pe.transpose(pah[2 * (n % 2) + half][:, k, :], xn[:, half, k * P:(k + 1) * P], ident)
                        last.then_inc(S["norm_T_done"], 1)
                elif what == "heads_T":
                    m = i[0]
                    pe.wait_ge(S["head_scaled"], m + 1)
                    if m < 4:
                        pe.wait_ge(S["norm_gained"], 2 * (TT + MT))
                    else:
                        pe.wait_ge(S["head_ready"], m - 3)
                    four(pah[m % 4], heads_of(work[:, m % 4, :]), None, transpose=True)\
                        .then_inc(S["head_T_done"], 1)
                elif what == "sb_scores":
                    h = i[0]
                    pe.wait_ge(S["masks_ready"], 1)
                    pe.wait_ge(S["head_ready"], 3 * TT + MT)
                    if h:
                        pe.wait_ge(S["sb_att"], 3 * h)
                    for j in range(TT):
                        alone = j < 3
                        pe.matmul(sb_bank[j], sbk_T[:, h, j * P:(j + 1) * P], sbq_T[:, h, j * P:SEQ],
                                  start=alone, stop=False, skip_group_check=True)
                        pe.matmul(sb_bank[j][:, 0:P], ident, neg_big, start=False, stop=True,
                                  skip_group_check=True).then_inc(S["sb_scored"], 1)
                elif what == "sb_suffix":
                    h = i[0]
                    pe.wait_ge(S["sb_soft"], 3 * (h + 1))
                    for j in range(TT):
                        last = pe.matmul(sb_bank[j], neg_tri, sb_soft[:, SBO[j]:SBO[j + 1]], start=False, stop=True,
                                         skip_group_check=True)
                        for j2 in range(j + 1, TT):
                            last = pe.matmul(sb_bank[j][:, (j2 - j) * P:], neg_ones, sb_soft[:, SBO[j2]:SBO[j2 + 1]],
                                             start=False, stop=True, skip_group_check=True)
                        last.then_inc(S["sb_summed"], 1)
                elif what == "sb_out":
                    h = i[0]
                    pe.wait_ge(S["sb_att"], 3 * (h + 1))
                    for j in range(TT):
                        wait_emptied(pe, "sbv", 0, j)
                    if h:
                        pe.wait_ge(S["sb_ready"], h)
                    for j in range(TT):
                        last = pe.matmul(pa[3][:, j * P:SEQ], sb_v[:, j, h * DH:(h + 1) * DH],
                                         sb_att[:, SBO[j]:SBO[j + 1]], start=j == 0, stop=j == TT - 1,
                                         skip_group_check=True)
                    last.then_inc(S["sb_oT"], 1)
                elif what == "decay_logits":
                    wait_emptied(pe, "ab", 0, 0)
                    pe.wait_ge(S["sb_att"], 3 * H)
                    pe.wait_ge(S["sb_ready"], H)
                    for t in range(TT):
                        last = pe.transpose(pa[0][:, t * P:(t + 1) * P], work[:, 6, t * P:(t + 1) * P], ident)
                    last.then_inc(S["ab_T_done"], 1)
                elif what == "decay_sums":
                    pe.wait_ge(S["glog_ready"], 1)
                    gl_all = glog.rearrange("p t c -> p (t c)")
                    pe.matmul(pa[1][:, 0:TT * H], tri_inc, gl_all, start=True, stop=True)
                    pe.matmul(pa[2][:, 0:TT * H], tri_after, gl_all, start=True, stop=True)\
                      .then_inc(S["decay_sums"], 1)
                elif what == "qk_squares":
                    for n in range(2):
                        pe.wait_ge(S["qk_squared"], n + 1)
                        for t in range(TT):
                            for h in range(H):
                                c = (n * TT + t) * H + h
                                last = pe.matmul(pa[3][:, c:c + 1], slab_S[:, n * H + h, t * P:(t + 1) * P],
                                                 neg_ones[:, 0:1], start=True, stop=True)
                    last.then_inc(S["qk_summed"], 1)
                elif what == "mem_scores":
                    h = i[0]
                    pe.wait_ge(S["decay_tok"], 1)
                    if h:
                        pe.wait_ge(S["ms_exp"], TT * h)
                    for t in range(TT):
                        last = pe.matmul(pa[t // 2][:, (t % 2) * N_MEM:(t % 2 + 1) * N_MEM],
                                         memq_T[:, h, t * P:(t + 1) * P], memk_T[:, h, :], start=t % 2 == 0,
                                         stop=True, skip_group_check=True)
                    last.then_inc(S["ms_scored"], 1)
                elif what == "mem_T":
                    h = i[0]
                    pe.wait_ge(S["ms_prob"], h + 1)
                    if h:
                        pe.wait_ge(S["ms_ready"], h)
                    else:
                        pe.wait_ge(S["qk_read"], 1)
                    probs = ms_probs[h % 2]
                    for m in range(MT):
                        for t in range(TT):
                            first = (t % 2) * N_MEM + m * P
                            last = pe.transpose(pa[2 + m][:, t * P:(t + 1) * P], probs[:, t // 2, first:first + P], ident)
                    last.then_inc(S["ms_T"], 1)
                elif what == "mem_out":
                    h = i[0]
                    pe.wait_ge(S["ms_pT"], 2 * (h + 1))
                    for m in range(MT):
                        wait_emptied(pe, "memv", 0, m)
                        last = pe.matmul(pa[2][:, :], mem_v[:, m, h * DH:(h + 1) * DH], work[:, 2 + m, :],
                                         start=m == 0, stop=m == MT - 1)
                    last.then_inc(S["ms_oT"], 1)
                elif what == "gdn_gram":
                    t = i[0]
                    pe.wait_ge(S["ms_ready"], H)
                    pe.wait_ge(S["factors_ready"], 1)
                    if t:
                        pe.wait_ge(S["g_state"], 2 * t)
                        pe.wait_ge(S["g_vnew"], 2 * t)
                    kT, qT = conv_tile(1, t), conv_tile(0, t)
                    for h in range(H):
                        last = pe.matmul(pah[3][:, h, :], glog[:, t, h:h + 1].to_broadcast([P, P]), tri_inc,
                                         start=True, stop=True)
                    last.then_inc(S["g_bcast"], 1)
                    four(pah[2], kT, qT)
                    four(pah[0], kT, kT).then_inc(S["g_grams"], 1)
                    pe.wait_ge(S["g_row_used"], t + 1)
                    for h in range(H):
                        last = pe.matmul(pah[3][:, h, :], bb[:, t, h:h + 1].to_broadcast([P, P]), ident,
                                         start=True, stop=True)
                    last.then_inc(S["g_beta_row"], 1)
                elif what == "inv_T":
                    t = i[0]
                    pe.wait_ge(S["i_Tt"], 6 * t + 1)
                    four(pah[2], g_Tt, None, transpose=True).then_inc(S["i_T"], 1)
                elif what == "inv_X":
                    t, n = i
                    pe.wait_ge(S["i_T_ready"], 5 * t + n + 1)
                    pe.wait_ge(S["i_C"], 5 * t + n + 1)
                    four(pah[0], g_C[n % 2], g_T).then_inc(S["i_X"], 1)
                elif what == "inv_P":
                    t, n = i
                    pe.wait_ge(S["i_X_copied"], 5 * t + n + 1)
                    pe.wait_ge(S["i_Tt"], 6 * t + n + 1)
                    if n + 1 < len(LEVELS):
                        four(pah[2], g_Tt, g_X).then_inc(S["i_Pt"], 1)
                    if t and n == 0:
                        pe.wait_ge(S["g_o_scaled"], t)
                    four(pah[1], g_X, g_Tt).then_inc(S["i_P"], 1)
                elif what == "gdn_kT":
                    t = i[0]
                    if t > 1:
                        pe.wait_ge(S["g_ready"], t - 1)
                    four(pah[3], conv_tile(1, t), None, transpose=True).then_inc(S["g_kT_done"], 1)
                elif what == "gdn_vT":
                    t = i[0]
                    pe.wait_ge(S["g_k_scaled"], t + 1)
                    four(pah[3], conv_tile(2, t), None, transpose=True).then_inc(S["g_vT_done"], 1)
                elif what == "gdn_uw":
                    t = i[0]
                    pe.wait_ge(S["i_Tt"], 6 * (t + 1))
                    pe.wait_ge(S["g_v_scaled"], t + 1)
                    four(pah[2], g_kbg, g_Tt).then_inc(S["g_uw"], 1)
                    for h in range(H):
                        pe.matmul(pah[0][:, h, :], g_Tt[:, h, :], conv_tile(2, t)[:, h, :], start=h == 0, stop=False,
                                  skip_group_check=True)
                elif what == "gdn_read":
                    t, c = i
                    r = slice(c * CHUNK, (c + 1) * CHUNK)
                    if c == 0:
                        pe.wait_ge(S["g_w"], t + 1)
                    if t == 0 and c == 0:
                        pe.wait_ge(S["state_zero"], 1)
                    else:
                        pe.wait_ge(S["g_state"], 2 * t + c)
                    for h in range(H):
                        last = pe.matmul(pah[0][r, h, :], g_wT[:, h, r], g_state[:, h, :], start=False, stop=True,
                                         skip_group_check=True)
                    last.then_inc(S["g_read"], 1)
                    if c == 0:
                        pe.wait_ge(S["g_q_dec"], t + 1)
                    for h in range(H):
                        last = pe.matmul(pah[1][r, h, :], conv_tile(0, t)[:, h, r], g_state[:, h, :], start=h == 0,
                                         stop=False, skip_group_check=True)
                    last.then_inc(S["g_qs"], 1)
                elif what == "gdn_update":
                    t, c = i
                    r = slice(c * CHUNK, (c + 1) * CHUNK)
                    pe.wait_ge(S["g_vnew"], 2 * t + c + 1)
                    for h in range(H):
                        last = pe.matmul(pah[2][:, h, :], conv_tile(1, t)[r, h, :], g_vnew[r, h, :], start=True,
                                         stop=True)
                    last.then_inc(S["g_upd"], 1)
                    for h in range(H):
                        last = pe.matmul(pah[1][r, h, :], g_at[r, h, r], g_vnew[r, h, :], start=False, stop=True,
                                         skip_group_check=True)
                    last.then_inc(S["g_o_sum"], 1)
                elif what == "gdn_oT":
                    t = i[0]
                    pe.wait_ge(S["g_o_scaled"], t + 1)
                    if t < TT - 2:
                        pe.wait_ge(S["i_Tt"], 6 * (t + 2) + 1)
                    elif t == TT - 1:
                        pe.wait_ge(S["g_ready"], TT - 1)
                    four(o_bank(t), heads_of(slab_Z[:, t, :]), None, transpose=True).then_inc(S["g_oT"], 1)
                elif what == "mix_T":
                    half, t = i
                    n = half * TT + t
                    wait_mixed(pe, 4 + half, t)
                    if n >= 4:
                        pe.wait_ge(S["mixT_ready"], n - 3)
                    else:
                        pe.wait_ge(S["g_ready"], TT)
                    for k in range(KH):
                        last = pe.transpose(pah[n % 4][:, k, :], slab_S[:, 2 * t + half, k * P:(k + 1) * P], ident)
                    last.then_inc(S["mixT_done"], 1)
                elif what == "x1_T":
                    half, t = i
                    n = half * TT + t
                    wait_emptied(pe, "wo", half, t)
                    if n >= 4:
                        pe.wait_ge(S["x1T_gained"], n - 3)
                    else:
                        pe.wait_ge(S["mixT_ready"], 2 * TT)
                    for k in range(KH):
                        last = pe.transpose(pah[n % 4][:, k, :], slab_C[:, 2 * t + half, k * P:(k + 1) * P], ident)
                    last.then_inc(S["x1T_done"], 1)

            with pe.Fori(0, QUARTERS) as q:
                for n in range(LOOP_UNITS):
                    u, group, kp = NU + n, n // GU, n % GU
                    pe.wait_ge(S["w_ready"], u + 1 + q * LOOP_UNITS)
                    if group == 0:
                        pe.wait_ge(S["x1T_ready"], TT * (1 + kp // (GU // 2)))
                    if group == 2:
                        pe.wait_ge(S["up_ready"], KU * (kp + 1) + q * KT)
                    for j in range(TT):
                        if kp == 0:
                            pe.wait_ge(bank_free[j], BANK_USES[j] + group + q * LOOP_GROUPS)
                        for k in range(KU):
                            kt = KU * kp + k
                            w = weights(u % SLOTS, KU * UW, k * UW, (k + 1) * UW)
                            if group < 2:
                                a = [held(MLP_IN, kt // KH, part)[:, kt % KH, :] for part in range(2)]
                                last = product(banks[j][:, :], [v[:, j * P:(j + 1) * P] for v in w], a, kt == 0,
                                               kt == KT - 1)
                            else:
                                a = [held(MIDDLE, kt // KH, part, slice(j * P, (j + 1) * P))[:, kt % KH, :]
                                     for part in range(2)]
                                last = product(banks[j][:, :], a, w, kt == 0, kt == KT - 1)
                        last.then_inc(S["piece_done"], 1)

        @block.scalar
        def _(act):
            at, order = [0], [0]

            def link(ins):
                order[0] += 1
                ins.then_inc(S["act_order"], 1)
                act.wait_ge(S["act_order"], order[0])

            row = 0
            for src in (norm1_g, mem_norm_g, norm2_g, gdn_norm_g, sb_q_norm_g, sb_k_norm_g, mem_q_norm_g,
                        mem_k_norm_g, conv_w):
                src = src[0].rearrange("w (c p) -> (w c) p", p=P) if src is conv_w else\
                    src[0].rearrange("(t p) -> t p", p=P)
                act.dma_start(work[row:row + src.shape[0], 3, 0:P], src).then_inc(S["par_rows"], 16)
                row += src.shape[0]

            def evacuate(p):
                unit, j, bank = UNITS[p["unit"]], p["j"], p["bank"]
                name = unit["stage"]
                act.wait_ge(S["piece_done"], p["done"])
                src = banks[bank][:, :]
                if name in HEAD_STAGE:
                    m = HEAD_STAGE[name] + j
                    if m >= 4:
                        act.wait_ge(S["head_T_done"], m - 3)
                    else:
                        act.wait_ge(S["params_ready"], 1)
                    act.activation(work[:, m % 4, :], src, ACT.Copy)
                    act.activation(slab_Z[:, m % 4, :], src, ACT.Square).then_inc(bank_free[bank], 1)
                elif name == "sbv":
                    act.activation(sb_v[:, j, :], src, ACT.Copy).then_inc(bank_free[bank], 1)
                elif name == "memv":
                    act.activation(mem_v[:, j, :], src, ACT.Copy).then_inc(bank_free[bank], 1)
                elif name == "conv":
                    act.activation(slab_C[:, unit["i"] * H + j, :], src, ACT.Copy,
                                   scale=conv_c[:, CONV - 1, unit["i"] * H + j:unit["i"] * H + j + 1])\
                       .then_inc(S["conv_tap"], 1)
                elif name == "ab":
                    act.activation(work[:, 6, :], src, ACT.Copy).then_inc(bank_free[bank], 1)
                elif name == "z":
                    act.activation(slab_Z[:, j, :], src, ACT.Tanh, scale=0.5).then_inc(S["z_tanh"], 1)
                elif name == "gate":
                    if unit["i"]:
                        wait_mixed(act, unit["i"] - 1, j)
                    else:
                        act.wait_ge(S["silu_done"], 3)
                    act.activation(gate_t[:, j, :], src, ACT.Tanh, scale=0.5).then_inc(bank_free[bank], 1)

            def high_part(u, n, landed, freed):
                slot = u % SLOTS
                act.wait_ge(raw_landed[slot], landed)
                if freed is not None:
                    act.wait_ge(S["piece_done"], freed)
                act.activation(w_hi[:, slot, 0:n], w_raw[:, slot, 0:n], ACT.Copy).then_inc(S["w_high"], 1)

            def high_part_ahead(u):
                u += SLOTS - 1
                n = UNITS[u]["src"].shape[1] * UNITS[u]["src"].shape[2] if u < NU else KU * UW
                high_part(u, n, 16 * (u // SLOTS + 1), UNITS[u - SLOTS]["done"] if u >= SLOTS else None)

            for what, *i in TIMELINE:
                if what == "dense":
                    for _ in range(i[0]):
                        p = PIECES[at[0]]
                        at[0] += 1
                        for u in p["ahead"]:
                            high_part_ahead(u)
                        if UNITS[p["unit"]]["last"]:
                            evacuate(p)
                elif what == "norm":
                    for n in range(*i):
                        act.wait_ge(S[f"x_landed{n}" if n < TT else f"m_landed{n - TT}"], 16)
                        act.activation(slab_S[:, 2 * n:2 * n + 2, :], norm_source(n), ACT.Square,
                                       accum_out=ssx[:, n:n + 1]).then_inc(S["norm_ss"], 1)
                    if i[0] < 2:
                        high_part_ahead(i[0] - SLOTS + 1)
                    for n in range(*i):
                        act.wait_ge(S["norm_factor"], n + 1)
                        act.activation(norm_source(n), norm_source(n), ACT.Copy, scale=rsx[:, n:n + 1])\
                           .then_inc(S["norm_scaled"], 1)
                elif what == "norm_T":
                    n = i[0]
                    for half in range(2):
                        act.wait_ge(S["norm_gained"], 2 * n + half + 1)
                        act.activation(norm_dest(n, half, 0), norm_gained(n, half), ACT.Copy)\
                           .then_inc(S["norm_hi"], 1)
                elif what == "heads_T":
                    m = i[0]
                    dst, t, gain = HEADS[m]
                    if m == 0:
                        act.wait_ge(S["gain_scaled"], 1)
                    act.wait_ge(S["head_T_done"], m + 1)
                    act.activation(dst[:, :, t * P:(t + 1) * P], pah[m % 4], ACT.Copy, scale=gain)\
                       .then_inc(S["head_ready"], 1)
                elif what == "sb_scores":
                    h = i[0]
                    for j, width in ((0, SEQ), (1, SEQ - P), (2, SEQ - P)):
                        act.wait_ge(S["sb_scored"], TT * h + (j + 1 if j < 2 else TT))
                        act.activation(sb_exps[:, SBO[j]:SBO[j] + width], pa[j][:, 0:width], ACT.Abs)\
                           .then_inc(S["sb_abs"], 1)
                    act.wait_ge(S["sb_abs"], 3 * (h + 1))
                    act.activation(sb_exps, sb_exps, ACT.Exp, scale=-1.0).then_inc(S["sb_exp"], 1)
                    act.wait_ge(S["sb_exp"], h + 1)
                    act.activation(sb_exps, sb_exps, ACT.Ln, bias=1.0).then_inc(S["sb_ln"], 1)
                elif what == "sb_suffix":
                    h = i[0]
                    if h:
                        act.wait_ge(S["sb_oT"], h)
                    for n, (j, width) in enumerate(((0, SEQ), (1, SEQ - P), (2, SEQ - P))):
                        act.wait_ge(S["sb_summed"], TT * h + (j + 1 if j < 2 else TT))
                        act.activation(sb_att[:, SBO[j]:SBO[j] + width], pa[j][:, 0:width], ACT.Exp)\
                           .then_inc(S["sb_att"], 1)
                elif what == "sb_out":
                    h = i[0]
                    act.wait_ge(S["sb_oT"], h + 1)
                    act.activation(act_B[:, 0, h, :], pa[3][:, :], ACT.Copy).then_inc(S["sb_hi"], 1)
                elif what == "decay_logits":
                    act.wait_ge(S["ab_tok"], 1)
                    link(act.activation(gcum, tg, ACT.Abs))
                    act.activation(gcum, gcum, ACT.Exp, scale=-1.0).then_inc(S["ab_exp"], 1)
                    act.wait_ge(S["ab_exp"], 1)
                    act.activation(gcum, gcum, ACT.Ln, bias=1.0)
                    act.activation(alog, alog, ACT.Exp)
                    act.activation(beta, ab[:, :, H:2 * H], ACT.Exp, scale=-1.0).then_inc(S["ab_ln"], 1)
                elif what == "silu":
                    part = i[0]
                    n = (1, 0, 2).index(part)
                    for h in range(H):
                        wait_emptied(act, "conv", part, h)
                    act.activation(slab_S[:, n * H:(n + 1) * H, :], slab_C[:, part * H:(part + 1) * H, :], ACT.Tanh,
                                   scale=0.5).then_inc(S["tanh_done"], 1)
                elif what == "qk_squares":
                    for n, part in enumerate((1, 0)):
                        act.wait_ge(S["silu_done"], n + 1)
                        act.activation(slab_S[:, n * H:(n + 1) * H, :], slab_C[:, part * H:(part + 1) * H, :],
                                       ACT.Square).then_inc(S["qk_squared"], 1)
                elif what == "decay_sums":
                    act.wait_ge(S["decay_sums"], 1)
                    act.activation(eg, pa[1][:, 0:TT * H].rearrange("p (t c) -> p t c", c=H), ACT.Exp)
                    act.activation(e2, pa[2][:, 0:TT * H].rearrange("p (t c) -> p t c", c=H), ACT.Exp)\
                       .then_inc(S["decay_exps"], 1)
                elif what == "mem_scores":
                    h = i[0]
                    act.wait_ge(S["ms_max"], h + 1)
                    if h >= 2:
                        act.wait_ge(S["ms_T"], h - 1)
                    for t in range(TT):
                        part = slice((t % 2) * N_MEM, (t % 2 + 1) * N_MEM)
                        act.activation(ms_probs[h % 2][:, t // 2, part], pa[t // 2][:, part], ACT.Exp,
                                       bias=mx[h % 2][:, t:t + 1], accum_out=rs[h % 2][:, t:t + 1])\
                           .then_inc(S["ms_exp"], 1)
                elif what == "mem_T":
                    h = i[0]
                    act.wait_ge(S["ms_T"], h + 1)
                    if h:
                        act.wait_ge(S["ms_oT"], h)
                    for m in range(MT):
                        act.activation(work[:, 2 + m, :], pa[2 + m][:, :], ACT.Copy).then_inc(S["ms_pT"], 1)
                elif what == "mem_out":
                    h = i[0]
                    act.wait_ge(S["ms_oT"], h + 1)
                    act.activation(act_B[:, 0, H + h, :], pa[2][:, :], ACT.Copy).then_inc(S["ms_hi"], 1)
                elif what == "gdn_gram":
                    t = i[0]
                    act.wait_ge(S["ms_ready"], H)
                    act.wait_ge(S["g_decay_sub"], t + 1)
                    if t:
                        act.wait_ge(S["g_state"], 2 * t)
                    act.activation(gl, pah[3][:, :, CHUNK - 1::CHUNK], ACT.Exp).then_inc(S["g_last"], 1)
                    if t:
                        act.wait_ge(S["g_q_dec"], t)
                    act.activation(g_eg, pah[3], ACT.Exp).then_inc(S["g_row_used"], 1)
                    act.activation(g_decayed, g_decayed, ACT.Exp).then_inc(S["g_decay"], 1)
                elif what == "inv_T":
                    t = i[0]
                    act.wait_ge(S["i_T"], t + 1)
                    act.activation(g_T, pah[2], ACT.Copy).then_inc(S["i_T_ready"], 1)
                elif what == "inv_X":
                    t, n = i
                    act.wait_ge(S["i_X"], 5 * t + n + 1)
                    if t + n:
                        act.wait_ge(S["i_P"], 5 * t + n)
                    act.activation(g_X, pah[0], ACT.Copy).then_inc(S["i_X_copied"], 1)
                elif what == "gdn_uw":
                    t = i[0]
                    act.wait_ge(S["g_uw"], t + 1)
                    act.activation(g_wT, pah[2], ACT.Copy, scale=-1.0).then_inc(S["g_w"], 1)
                elif what == "gdn_read":
                    t, c = i
                    r = slice(c * CHUNK, (c + 1) * CHUNK)
                    act.wait_ge(S["g_read"], 2 * t + c + 1)
                    act.activation(g_vnew[r], pah[0][r], ACT.Copy).then_inc(S["g_vnew"], 1)
                elif what == "gdn_out":
                    t = i[0]
                    act.wait_ge(S["g_o_sum"], 2 * (t + 1))
                    act.activation(g_sq, pah[1], ACT.Square).then_inc(S["g_o_sq"], 1)
                elif what == "gdn_oT":
                    t = i[0]
                    act.wait_ge(S["g_oT"], t + 1)
                    if t == 0:
                        for j in range(TT):
                            wait_mixed(act, 1, j)
                    act.activation(act_B[:, 0, 0:H, t * P:(t + 1) * P], o_bank(t), ACT.Copy, scale=g_gdn)\
                       .then_inc(S["g_o_hi"], 1)
                elif what == "mix_T":
                    half, t = i
                    n = half * TT + t
                    act.wait_ge(S["mixT_done"], n + 1)
                    act.activation(held(MIX, half, 0, slice(t * P, (t + 1) * P)), pah[n % 4], ACT.Copy)\
                       .then_inc(S["mixT_hi"], 1)
                elif what == "x1_T":
                    half, t = i
                    n = half * TT + t
                    act.wait_ge(S["x1T_gained"], n + 1)
                    act.activation(held(MLP_IN, half, 0, slice(t * P, (t + 1) * P)), heads_of(work[:, n % 2, :]),
                                   ACT.Copy).then_inc(S["x1T_hi"], 1)
                elif what == "x1_norm":
                    t = i[0]
                    n = TT + MT + t
                    for half in range(2):
                        wait_emptied(act, "wo", half, t)
                    act.activation(work[:, 4:6, :], norm_source(t), ACT.Square, accum_out=ssx[:, n:n + 1])\
                       .then_inc(S["x1_ss"], 1)

            def relus(q, group):
                for j in range(TT):
                    n = TT * group + j
                    act.wait_ge(S["piece_done"], len(PIECES) + (GU * (group + 1) - 1) * TT + j + 1 + q * LOOP_PIECES)
                    b, uses = (n - 2) % TT, BANK_USES[(n - 2) % TT] + (n - 2) // TT + 1
                    act.wait_ge(bank_free[b], uses + q * LOOP_GROUPS)
                    act.activation(work[:, n % 2, :], banks[j][:, :], ACT.Relu).then_inc(S["up_relu"], 1)
                    act.wait_ge(S["up_relu"], n + 1 + q * KT)
                    act.activation(held(MIDDLE, group, 0)[:, j, :], work[:, n % 2, :], ACT.Square)\
                       .then_inc(S["up_hi"], 1)

            def quarter(q, units):
                ahead = SLOTS - 1

                def high_parts(a, b):
                    for n in range(a, min(b, units)):
                        u = NU + ahead + n
                        freed = len(PIECES) + (ahead + n - SLOTS + 1) * TT
                        high_part(u, KU * UW, 16 * (u // SLOTS + 1) + q * (16 * LOOP_UNITS // SLOTS),
                                  freed + q * LOOP_PIECES)

                high_parts(0, GU)
                relus(q, 0)
                high_parts(GU, 2 * GU)
                relus(q, 1)
                high_parts(2 * GU, LOOP_UNITS)

            with act.Fori(0, QUARTERS - 1) as q:
                quarter(q, LOOP_UNITS)
            quarter(QUARTERS - 1, LOOP_UNITS - (SLOTS - 1))

        @block.vector
        def _(dve):
            at, order = [0], [0]

            def link(ins):
                order[0] += 1
                ins.then_inc(S["dve_order"], 1)
                dve.wait_ge(S["dve_order"], order[0])

            def rsqrt(dst, src, mult, add, v=None, a=None, src_read=None):
                n = src.shape[1]
                if v is None:
                    v, a = nt_v[:, 0:n], nt_a[:, 0:n]
                link(dve.tensor_scalar(v, src, mult, add, ALU.mult, ALU.add))
                if src_read is not None:
                    dve.sem_inc(src_read, 1)
                link(dve.tensor_scalar(a.bitcast(I32), v.bitcast(I32), 1, None, ALU.logical_shift_right))
                link(dve.tensor_scalar(dst.bitcast(I32), a.bitcast(I32), -1.0, float(0x5F3759DF), ALU.mult, ALU.add))
                for _ in range(3):
                    link(dve.tensor_tensor(a, dst, dst, ALU.mult))
                    link(dve.scalar_tensor_tensor(out=a, in0=a, scalar=-0.5, in1=v, op0=ALU.mult, op1=ALU.mult))
                    link(dve.scalar_tensor_tensor(out=dst, in0=a, scalar=1.5, in1=dst, op0=ALU.add, op1=ALU.mult))

            def evacuate(p):
                unit, j, bank = UNITS[p["unit"]], p["j"], p["bank"]
                name, src = unit["stage"], banks[p["bank"]]
                if name in HEAD_STAGE:
                    m = HEAD_STAGE[name] + j
                    wait_emptied(dve, name, 0, j)
                    ins = dve.reduce_sum(ssh[:, j * H:(j + 1) * H], heads_of(slab_Z[:, m % 4, :]), axis=AX.X)
                    if (j + 1) * P == (SEQ if name != "memk" else N_MEM):
                        link(ins)
                        rsqrt(rsh[:, 0:(j + 1) * H], ssh[:, 0:(j + 1) * H], 1.0 / DH, EPS)
                        for n in range(j + 1):
                            copy = heads_of(work[:, (m - j + n) % 4, :])
                            dve.tensor_tensor(copy, copy, per_head(rsh[:, n * H:(n + 1) * H]), ALU.mult)\
                               .then_inc(S["head_scaled"], 1)
                elif name == "conv":
                    c = unit["i"] * H + j
                    y = slab_C[:, c, :]
                    dve.wait_ge(S["conv_tap"], c + 1)
                    for tap in range(1, CONV):
                        w = conv_c[:, CONV - 1 - tap, c:c + 1]
                        ins = dve.scalar_tensor_tensor(out=y[:, tap:], in0=src[:, 0:SEQ - tap], scalar=w,
                                                       in1=y[:, tap:], op0=ALU.mult, op1=ALU.add)
                        if tap < CONV - 1:
                            link(ins)
                    ins.then_inc(bank_free[bank], 1)
                elif name == "z":
                    z = slab_Z[:, j, :]
                    dve.wait_ge(S["z_tanh"], j + 1)
                    dve.scalar_tensor_tensor(out=z, in0=z, scalar=1.0, in1=src[:, :], op0=ALU.add, op1=ALU.mult)\
                       .then_inc(bank_free[bank], 1)
                elif name == "branch":
                    mix = slab_S[:, 2 * j + unit["i"] % 2, :]
                    dve.wait_ge(S["piece_done"], p["done"])
                    wait_emptied(dve, "gate", unit["i"], j)
                    dst = mix if unit["i"] < 2 else gate_t[:, j, :]
                    ins = dve.scalar_tensor_tensor(out=dst, in0=gate_t[:, j, :], scalar=1.0, in1=src[:, :],
                                                   op0=ALU.add, op1=ALU.mult)
                    ins.then_inc(bank_free[bank], 1)
                    if unit["i"] >= 2:
                        dve.wait_ge(bank_free[bank], p["use"])
                        dve.tensor_tensor(mix, mix, gate_t[:, j, :], ALU.add).then_inc(S["mixed"], 1)
                elif name == "wo":
                    dve.wait_ge(S["piece_done"], p["done"])
                    dve.wait_ge(S["x_again"], 16 * TT)
                    x1 = slab_C[:, 2 * j + unit["i"], :]
                    dve.scalar_tensor_tensor(out=x1, in0=src[:, :], scalar=0.5, in1=x1, op0=ALU.mult, op1=ALU.add)\
                       .then_inc(bank_free[bank], 1)

            for what, *i in TIMELINE:
                if what == "dense":
                    for _ in range(i[0]):
                        p = PIECES[at[0]]
                        at[0] += 1
                        if UNITS[p["unit"]]["last"]:
                            evacuate(p)
                elif what == "norm":
                    dve.wait_ge(S["norm_ss"], i[1])
                    rsqrt(rsx[:, i[0]:i[1]], ssx[:, i[0]:i[1]], 1.0 / D, EPS)
                    dve.sem_inc(S["norm_factor"], i[1] - i[0])
                elif what == "norm_T":
                    n = i[0]
                    if n == 0:
                        dve.wait_ge(S["par_T_done"], 1)
                        dve.tensor_copy(params, pa[3][:, 0:NPAR]).then_inc(S["params_ready"], 1)
                        dve.wait_ge(S["params_ready"], 1)
                        dve.tensor_scalar(g_sbq, g_sbq, SCALE, None, ALU.mult)
                        dve.tensor_scalar(g_mq, g_mq, SCALE, None, ALU.mult).then_inc(S["gain_scaled"], 1)
                    gain = g1 if n < TT else gm
                    for half in range(2):
                        dve.wait_ge(S["norm_T_done"], 2 * n + half + 1)
                        if n > 1:
                            dve.wait_ge(S["act_ready"], 2 * (n - 2) + half + 1)
                        dve.tensor_tensor(norm_gained(n, half), pah[2 * (n % 2) + half],
                                          gain[:, KH * half:KH * half + KH].unsqueeze(2).to_broadcast([P, KH, P]),
                                          ALU.mult).then_inc(S["norm_gained"], 1)
                    for half in range(2):
                        dve.wait_ge(S["norm_hi"], 2 * n + half + 1)
                        dve.tensor_tensor(norm_dest(n, half, 1), norm_gained(n, half),
                                          norm_dest(n, half, 0).bitcast(F32), ALU.subtract)\
                           .then_inc(S["act_ready"], 1)
                elif what == "sb_scores":
                    h = i[0]
                    widths = ((0, SEQ), (1, SEQ - P), (2, SEQ - P))
                    dve.wait_ge(S["sb_ln"], h + 1)
                    if h:
                        dve.wait_ge(S["sb_summed"], TT * h)
                    for j, width in widths:
                        dve.scalar_tensor_tensor(out=sb_soft[:, SBO[j]:SBO[j] + width], in0=pa[j][:, 0:width],
                                                 scalar=0.0, in1=sb_exps[:, SBO[j]:SBO[j] + width], op0=ALU.max,
                                                 op1=ALU.add).then_inc(S["sb_soft"], 1)
                elif what == "sb_out":
                    h = i[0]
                    dve.wait_ge(S["sb_hi"], h + 1)
                    dve.tensor_tensor(act_B[:, 1, h, :], pa[3][:, :], act_B[:, 0, h, :].bitcast(F32), ALU.subtract)\
                       .then_inc(S["sb_ready"], 1)
                elif what == "decay_logits":
                    dve.wait_ge(S["ab_T_done"], 1)
                    dve.wait_ge(S["par_decay"], 32)
                    link(dve.tensor_copy(ab, pa[0][:, :].rearrange("p (t c) -> p t c", c=P)[:, :, 0:2 * H]))
                    dve.tensor_tensor(tg, ab[:, :, 0:H], dtb.unsqueeze(1).to_broadcast([P, TT, H]), ALU.add)\
                       .then_inc(S["ab_tok"], 1)
                    dve.wait_ge(S["ab_ln"], 1)
                    link(dve.scalar_tensor_tensor(out=glog, in0=tg, scalar=0.0, in1=gcum, op0=ALU.max, op1=ALU.add))
                    dve.scalar_tensor_tensor(out=glog, in0=glog, scalar=-1.0,
                                             in1=alog.unsqueeze(1).to_broadcast([P, TT, H]), op0=ALU.mult,
                                             op1=ALU.mult).then_inc(S["glog_ready"], 1)
                    link(dve.tensor_scalar(beta, beta, 1.0, None, ALU.add))
                    link(dve.reciprocal(beta, beta))
                elif what == "decay_sums":
                    dve.wait_ge(S["decay_sums"], 1)
                    dve.wait_ge(S["decay_exps"], 1)
                    dve.tensor_copy(gcum, pa[1][:, 0:TT * H].rearrange("p (t c) -> p t c", c=H))\
                       .then_inc(S["decay_tok"], 1)
                elif what == "silu":
                    part = i[0]
                    n = (1, 0, 2).index(part)
                    c = slab_C[:, part * H:(part + 1) * H, :]
                    dve.wait_ge(S["tanh_done"], n + 1)
                    dve.scalar_tensor_tensor(out=c, in0=slab_S[:, n * H:(n + 1) * H, :], scalar=1.0, in1=c,
                                             op0=ALU.add, op1=ALU.mult).then_inc(S["silu_done"], 1)
                elif what == "qk_norms":
                    dve.wait_ge(S["qk_summed"], 1)
                    n = TT * H
                    v, a, r = (work[:, 7, i * 2 * n:(i + 1) * 2 * n] for i in range(3))
                    rsqrt(r, pa[3][:, 0:2 * n], -1.0, 4.0 * EPS, v, a, src_read=S["qk_read"])
                    r3 = r.rearrange("p (t c) -> p t c", c=H)
                    rk, rq = r3[:, 0:TT, :], r3[:, TT:2 * TT, :]
                    dve.tensor_copy(k_norm, rk)
                    dve.tensor_scalar(rq_half, rq, 0.5 * SCALE, None, ALU.mult)
                    dve.scalar_tensor_tensor(out=rq2, in0=rq, scalar=SCALE * SCALE, in1=rq, op0=ALU.mult, op1=ALU.mult)
                    dve.tensor_tensor(k_dec, rk, e2, ALU.mult)
                    link(dve.tensor_tensor(bb, rk, beta, ALU.mult))
                    dve.tensor_tensor(k_beta_decay, bb, eg, ALU.mult)
                    dve.tensor_scalar(v_beta, beta, 0.5, None, ALU.mult).then_inc(S["factors_ready"], 1)
                elif what == "mem_scores":
                    h = i[0]
                    dve.wait_ge(S["ms_scored"], h + 1)
                    if h:
                        dve.wait_ge(S["ms_exp"], TT * h)
                    top, total = mx[h % 2], rs[h % 2]
                    for n in range(TT // 2):
                        dve.reduce_max(total[:, 2 * n:2 * n + 2], pa[n][:, :].rearrange("p (t m) -> p t m", m=N_MEM),
                                       axis=AX.X).then_inc(S["ms_top"], 1)
                    dve.wait_ge(S["ms_top"], 2 * (h + 1))
                    dve.tensor_scalar(top, total, -1.0, None, ALU.mult).then_inc(S["ms_max"], 1)
                    dve.wait_ge(S["ms_exp"], TT * (h + 1))
                    link(dve.reciprocal(top, total))
                    probs = ms_probs[h % 2].rearrange("p a (b m) -> p (a b) m", m=N_MEM)
                    dve.tensor_tensor(probs, probs, top.unsqueeze(2).to_broadcast([P, TT, N_MEM]), ALU.mult)\
                       .then_inc(S["ms_prob"], 1)
                elif what == "mem_out":
                    h = i[0]
                    dve.wait_ge(S["ms_hi"], h + 1)
                    dve.tensor_tensor(act_B[:, 1, H + h, :], pa[2][:, :], act_B[:, 0, H + h, :].bitcast(F32),
                                      ALU.subtract).then_inc(S["ms_ready"], 1)
                elif what == "gdn_gram":
                    t = i[0]
                    if t == 0:
                        dve.wait_ge(S["ms_oT"], H)
                        dve.memset(g_state, 0.0).then_inc(S["state_zero"], 1)
                    dve.wait_ge(S["g_bcast"], t + 1)
                    for h in range(H):
                        ins = dve.tensor_scalar(g_decayed[:, h, :], pah[3][:, h, :], gcum[:, t, h:h + 1], 0.0,
                                                ALU.subtract, ALU.min)
                    ins.then_inc(S["g_decay_sub"], 1)
                    dve.wait_ge(S["g_decay"], t + 1)
                    for h in range(H):
                        ins = dve.scalar_tensor_tensor(out=g_decayed[:, h, :], in0=g_decayed[:, h, :],
                                                       scalar=k_norm[:, t, h:h + 1], in1=tri_inc, op0=ALU.mult,
                                                       op1=ALU.mult)
                    link(ins)
                    dve.wait_ge(S["g_beta_row"], t + 1)
                    link(dve.tensor_tensor(g_lower, g_decayed, pah[3], ALU.mult))
                    dve.wait_ge(S["g_grams"], t + 1)
                    link(dve.tensor_tensor(g_lower, g_lower, pah[0], ALU.mult))
                    link(dve.tensor_tensor(g_Tt, g_lower, all_heads(lvl[0]), ALU.mult))
                    if t:
                        dve.wait_ge(S["g_o_sum"], 2 * t)
                    dve.tensor_tensor(g_at, g_decayed, pah[2], ALU.mult)
                    dve.scalar_tensor_tensor(out=g_Tt, in0=g_Tt, scalar=-1.0, in1=all_heads(ident), op0=ALU.mult,
                                             op1=ALU.add).then_inc(S["i_Tt"], 1)
                    dve.tensor_tensor(g_C[0], g_lower, all_heads(lvl[1]), ALU.mult).then_inc(S["i_C"], 1)
                    dve.wait_ge(S["g_row_used"], t + 1)
                    q = conv_tile(0, t)
                    dve.tensor_tensor(q, q, g_eg, ALU.mult).then_inc(S["g_q_dec"], 1)
                elif what == "gdn_kT":
                    t = i[0]
                    dve.wait_ge(S["g_kT_done"], t + 1)
                    dve.tensor_tensor(g_kbg, pah[3], per_head(k_beta_decay[:, t, :]), ALU.mult)
                    dve.tensor_tensor(conv_tile(1, t), pah[3], per_head(k_dec[:, t, :]), ALU.mult)\
                       .then_inc(S["g_k_scaled"], 1)
                elif what == "gdn_vT":
                    t = i[0]
                    dve.wait_ge(S["g_vT_done"], t + 1)
                    dve.tensor_tensor(conv_tile(2, t), pah[3], per_head(v_beta[:, t, :]), ALU.mult)\
                       .then_inc(S["g_v_scaled"], 1)
                elif what == "inv_P":
                    t, n = i
                    if n + 1 < len(LEVELS):
                        dve.tensor_tensor(g_C[(n + 1) % 2], g_lower, all_heads(lvl[n + 2]), ALU.mult)\
                           .then_inc(S["i_C"], 1)
                        dve.wait_ge(S["i_Pt"], 4 * t + n + 1)
                        dve.wait_ge(S["i_T_ready"], 5 * t + n + 1)
                        dve.tensor_tensor(g_T, g_T, pah[2], ALU.subtract).then_inc(S["i_T_ready"], 1)
                    dve.wait_ge(S["i_P"], 5 * t + n + 1)
                    dve.tensor_tensor(g_Tt, g_Tt, pah[1], ALU.subtract).then_inc(S["i_Tt"], 1)
                elif what == "gdn_read":
                    t, c = i
                    dve.wait_ge(S["g_qs"], 2 * t + c + 1)
                    link(dve.tensor_tensor(g_state, g_state, per_head(gl[:, :, c]), ALU.mult))
                elif what == "gdn_update":
                    t, c = i
                    dve.wait_ge(S["g_upd"], 2 * t + c + 1)
                    dve.tensor_tensor(g_state, g_state, pah[2], ALU.add).then_inc(S["g_state"], 1)
                elif what == "gdn_out":
                    t = i[0]
                    dve.wait_ge(S["g_o_sq"], t + 1)
                    link(dve.reduce_sum(sso, g_sq, axis=AX.X))
                    link(dve.tensor_tensor(sso, sso, rq2[:, t, :], ALU.mult))
                    rsqrt(rso, sso, 1.0 / DH, EPS)
                    link(dve.tensor_tensor(rso, rso, rq_half[:, t, :], ALU.mult))
                    link(dve.tensor_tensor(g_o, pah[1], per_head(rso), ALU.mult))
                    z = heads_of(slab_Z[:, t, :])
                    dve.tensor_tensor(z, g_o, z, ALU.mult).then_inc(S["g_o_scaled"], 1)
                elif what == "gdn_oT":
                    t = i[0]
                    hi, lo = (act_B[:, part, 0:H, t * P:(t + 1) * P] for part in range(2))
                    dve.wait_ge(S["g_o_hi"], t + 1)
                    dve.scalar_tensor_tensor(out=lo, in0=o_bank(t), scalar=g_gdn, in1=hi.bitcast(F32), op0=ALU.mult,
                                             op1=ALU.subtract).then_inc(S["g_ready"], 1)
                elif what == "mix_T":
                    half, t = i
                    n = half * TT + t
                    tokens = slice(t * P, (t + 1) * P)
                    dve.wait_ge(S["mixT_hi"], n + 1)
                    dve.tensor_tensor(held(MIX, half, 1, tokens), pah[n % 4], held(MIX, half, 0, tokens).bitcast(F32),
                                      ALU.subtract).then_inc(S["mixT_ready"], 1)
                elif what == "x1_T":
                    half, t = i
                    n = half * TT + t
                    tokens = slice(t * P, (t + 1) * P)
                    dve.wait_ge(S["x1T_done"], n + 1)
                    dve.tensor_tensor(heads_of(work[:, n % 2, :]), pah[n % 4],
                                      g2[:, KH * half:KH * half + KH].unsqueeze(2).to_broadcast([P, KH, P]),
                                      ALU.mult).then_inc(S["x1T_gained"], 1)
                    dve.wait_ge(S["x1T_hi"], n + 1)
                    dve.wait_ge(S["x1T_gained"], n + 1)
                    dve.tensor_tensor(held(MLP_IN, half, 1, tokens), heads_of(work[:, n % 2, :]),
                                      held(MLP_IN, half, 0, tokens).bitcast(F32), ALU.subtract)\
                       .then_inc(S["x1T_ready"], 1)
                elif what == "x1_norm":
                    t = i[0]
                    n = TT + MT + t
                    dve.wait_ge(S["x1_ss"], t + 1)
                    link(dve.tensor_scalar(rsx[:, 0:1], ssx[:, n:n + 1], 1.0 / D, EPS, ALU.mult, ALU.add))
                    dve.reciprocal(mlp_scale[:, t:t + 1], rsx[:, 0:1]).then_inc(S["mlp_scaled"], 1)

            dve.wait_ge(S["mlp_scaled"], TT)
            with dve.Fori(0, QUARTERS) as q:
                for n in range(KT):
                    group, j = n // TT, n % TT
                    dve.wait_ge(S["up_relu"], n + 1 + q * KT)
                    dve.scalar_tensor_tensor(out=work[:, 2 + n % 2, :], in0=banks[j][:, :], scalar=0.0,
                                             in1=work[:, n % 2, :], op0=ALU.max, op1=ALU.mult)\
                       .then_inc(bank_free[j], 1)
                    dve.wait_ge(bank_free[j], BANK_USES[j] + group + 1 + q * LOOP_GROUPS)
                    dve.wait_ge(S["up_hi"], n + 1 + q * KT)
                    dve.tensor_tensor(held(MIDDLE, group, 1)[:, j, :], work[:, 2 + n % 2, :],
                                      held(MIDDLE, group, 0)[:, j, :].bitcast(F32), ALU.subtract)\
                       .then_inc(S["up_ready"], 1)
                for n in range(2 * TT):
                    half, j = n // TT, n % TT
                    x1 = slab_C[:, 2 * j + half, :]
                    dve.wait_ge(S["piece_done"],
                                len(PIECES) + (GU * (half + 3) - 1) * TT + j + 1 + q * LOOP_PIECES)
                    dve.scalar_tensor_tensor(out=x1, in0=banks[j][:, :], scalar=mlp_scale[:, j:j + 1], in1=x1,
                                             op0=ALU.mult, op1=ALU.add).then_inc(bank_free[j], 1)


_INS = ["x", "mem", "norm1_g", "w_in", "conv_w", "a_log", "dt_bias", "gdn_norm_g", "sb_q_norm_g", "sb_k_norm_g",
        "mem_norm_g", "w_mem_kv", "mem_q_norm_g", "mem_k_norm_g", "w_br_gdn", "w_br_sb", "w_br_mem", "w_o",
        "norm2_g", "w_up", "w_down"]


def kernel(**inputs):
    import concourse.bacc as bacc
    from concourse.bass_utils import run_bass_kernel_spmd

    nc = bacc.Bacc("TRN2", target_bir_lowering=False, num_devices=1)
    arrays, args = {}, []
    for name in _INS:
        a = np.ascontiguousarray(inputs[name])
        arrays[f"in_{name}"] = a
        args.append(nc.dram_tensor(f"in_{name}", a.shape, mybir.dt.from_np(a.dtype), kind="ExternalInput").ap())
    shape = arrays["in_x"].shape
    args.append(nc.dram_tensor("layer_out", shape, mybir.dt.float32, kind="ExternalOutput").ap())
    hybrid_layer_kernel(nc, *args)
    return run_bass_kernel_spmd(nc, [arrays], core_ids=[0]).results[0]["layer_out"]
```

```python
import numpy as np

import concourse.bass as bass
from concourse import mybir
from contextlib import ExitStack


def hybrid_layer_kernel(nc, x, mem, norm1_g, w_in, conv_w, a_log, dt_bias, gdn_norm_g, sb_q_norm_g,
                        sb_k_norm_g, mem_norm_g, w_mem_kv, mem_q_norm_g, mem_k_norm_g, w_br_gdn,
                        w_br_sb, w_br_mem, w_o, norm2_g, w_up, w_down, out):
    F32, F32R, BF16, I32 = mybir.dt.float32, mybir.dt.float32r, mybir.dt.bfloat16, mybir.dt.int32
    ALU, ACT, AX = mybir.AluOpType, mybir.ActivationFunctionType, mybir.AxisListType

    P = 128
    SEQ, D = x.shape[1], x.shape[2]
    N_MEM = mem.shape[1]
    H, DH, CHUNK = 4, 128, 64
    HW = H * DH
    EPS = 1e-6
    TT, KT = SEQ // P, D // P
    MT = N_MEM // P
    FF = w_up.shape[2]
    KU = 2
    KH = 4
    SLOTS = 4
    UW = 512
    QUARTERS = FF // D
    SCALE = float(DH) ** -0.5
    MASKED = -1e30
    CONV = conv_w.shape[1]

    C_GDN, C_Z = 0, 3 * HW
    C_AB = C_Z + HW
    C_SB = C_AB + 2 * H
    C_MEMQ = C_SB + 3 * HW
    C_GATE = C_MEMQ + HW

    win = w_in[0].rearrange("(t p) n -> p t n", p=P)
    wkv = w_mem_kv[0].rearrange("(t p) n -> p t n", p=P)
    wbr = [w[0].rearrange("(t p) n -> p t n", p=P) for w in (w_br_sb, w_br_mem, w_br_gdn)]
    wo = w_o[0].rearrange("(t p) n -> p t n", p=P)
    wup = w_up[0].rearrange("(t p) n -> p t n", p=P)
    wdown = w_down[0].rearrange("(t p) n -> p t n", p=P)

    UNITS = []

    def stage(name, i, w, col, act, kts, tiles, kind="tok", bank0=0, kt0=(0, 0), width=UW, ku=KU):
        for n, k in enumerate(range(0, kts, ku)):
            UNITS.append(dict(stage=name, i=i, src=w[:, k:k + ku, col:col + width], act=act[k // KH],
                              kt0=kt0[k // KH] + k % KH,
                              first=n == 0, last=k + ku == kts, kind=kind,
                              outs=[(bank0 + j, j) for j in range(tiles)]))

    stage("sbq", 0, win, C_SB, "AA", KT, TT, kt0=(0, KH))
    stage("sbk", 0, win, C_SB + HW, "AA", KT, TT, kt0=(0, KH))
    stage("sbv", 0, win, C_SB + 2 * HW, "AA", KT, TT, kt0=(0, KH))
    stage("memq", 0, win, C_MEMQ, "AA", KT, TT, kt0=(0, KH))
    stage("memk", 0, wkv, 0, "BB", KT, MT, kt0=(0, KH))
    stage("memv", 0, wkv, HW, "BB", KT, MT, bank0=MT, kt0=(0, KH))
    for part in range(3):
        stage("conv", part, win, C_GDN + part * HW, "AA", KT, H, kind="chan", kt0=(0, KH))
    stage("ab", 0, win, C_AB, "AA", KT, 1, kind="chan", kt0=(0, KH), width=P, ku=KT)
    stage("z", 0, win, C_Z, "AA", KT, TT, kt0=(0, KH))
    GATE_OF = (1, 2, 0)
    BR_KT0 = (0, H, 0)
    for br in range(3):
        for half in range(2):
            stage("gate", 2 * br + half, win, C_GATE + GATE_OF[br] * D + half * UW, "AA", KT, UW // P, kind="chan",
                  kt0=(0, KH))
            stage("branch", 2 * br + half, wbr[br], half * UW, "B", H, UW // P, kind="chan", kt0=(BR_KT0[br],))
    for half in range(2):
        stage("wo", half, wo, half * UW, "BA", KT, TT, kt0=(KH, 0))
    NU = len(UNITS)

    PIECES, BANK_USES = [], [0] * TT
    order = [(u, n) for n in range(TT) for u in range(2)]
    order += [(u, n) for u in range(2, NU) for n in range(len(UNITS[u]["outs"]))]
    for u, n in order:
        unit = UNITS[u]
        bank, j = unit["outs"][n]
        BANK_USES[bank] += unit["first"]
        ahead = {0: [-1, 0], 1: [], 2: [1, 2]}.get(u, [u]) if n == 0 else []
        PIECES.append(dict(unit=u, bank=bank, j=j, opens_unit=n == 0, use=BANK_USES[bank], done=len(PIECES) + 1,
                           ahead=ahead))
        unit["done"] = len(PIECES)
    EMPTIED = {(UNITS[p["unit"]]["stage"], UNITS[p["unit"]]["i"], p["j"]): (p["bank"], p["use"]) for p in PIECES}
    GU = KT // KU
    LOOP_GROUPS = 4
    LOOP_UNITS = LOOP_GROUPS * GU
    LOOP_PIECES = LOOP_UNITS * TT

    TIMELINE = []
    placed = [0]

    def pieces_of(stage_name, i):
        return [n for n, p in enumerate(PIECES)
                if (UNITS[p["unit"]]["stage"], UNITS[p["unit"]]["i"]) == (stage_name, i)]

    limit = [min(pieces_of("branch", 4))]

    def dense(n):
        n = max(0, min(n, limit[0] - placed[0]))
        placed[0] += n
        if n:
            TIMELINE.append(("dense", n))

    def dense_to(stage_name, i=0):
        dense(max(pieces_of(stage_name, i)) + 1 - placed[0])

    def step(name, *i):
        TIMELINE.append((name, *i))

    step("norm_squares", 0, 2)
    step("norm", 0, 1)
    step("norm", 1, 2)
    step("params", 0)
    step("norm_T", 0)
    step("norm_squares", 2, TT)
    step("norm_T", 1)
    step("norm", 2, TT)
    dense(4)
    step("norm_T", 2)
    step("norm_T", 3)
    dense(2 * TT)
    step("params", 1)
    step("norm_squares", TT, TT + MT)
    step("norm", TT, TT + MT)
    dense(3)
    for i in range(TT, TT + MT):
        step("norm_T", i)
        dense(2)
    heads = 0
    dense_to("sbq")
    for name, tiles, then in (("sbq", TT, "sbk"), ("sbk", TT, "sbv"), ("memq", TT, "memk"), ("memk", MT, "memv")):
        dense_to(name)
        dense(4 if name == "memk" else 6)
        for _ in range(tiles):
            step("heads_T", heads)
            dense(1 if then in ("memk", "memv") else 2)
            heads += 1
        dense_to(then)
    dense_to("memv")
    conv_tiles = 0

    def conv_taps(n):
        nonlocal conv_tiles
        while n and conv_tiles < 3 * H and placed[0] > max(pieces_of("conv", conv_tiles // H)):
            step("conv_taps", conv_tiles)
            conv_tiles += 1
            n -= 1
            if conv_tiles in (H, 2 * H):
                step("silu", conv_tiles // H - 1)

    dense(2)
    for h in range(H):
        step("sb_scores", h)
        dense(3)
        step("sb_soft", h)
        dense(1)
        step("sb_split", h)
        conv_taps(1)
        dense(3)
        step("sb_suffix", h)
        conv_taps(2)
        dense(3)
        step("sb_out", h)
        conv_taps(1)
        dense(2)
    dense_to("conv", 2)
    conv_taps(2)
    dense_to("ab")
    conv_taps(2)
    step("qk_squares")
    dense(2)
    step("decay_logits")
    dense(3)
    step("decay_sums")
    step("silu", 2)
    dense(1)
    step("qk_sums")
    step("mem_scores", 0)
    dense(2)
    step("qk_norms")
    for h in range(H):
        if h + 1 < H:
            step("mem_scores", h + 1)
        dense(2)
        step("mem_T", h)
        dense(3)
        step("mem_out", h)
    LEVELS = [2, 4, 8, 16, 32]
    tile_steps = [(3, "gdn_gram"), (1, "gdn_out"), (4, "inv_T"), (1, "inv_X", 0), (1, "gdn_oT"), (2, "inv_P", 0)]
    for lv in range(1, len(LEVELS)):
        tile_steps.append((1, "inv_X", lv))
        if lv == 1:
            tile_steps.append((0, "gdn_kT"))
        if lv == 2:
            tile_steps.append((0, "gdn_vT"))
        tile_steps.append((1, "inv_P", lv))
    tile_steps += [(1, "gdn_uw"), (1, "gdn_read", 0), (1, "gdn_update", 0), (1, "gdn_read", 1),
                   (1, "gdn_update", 1)]
    after = [(1, "gdn_out", TT - 1), (2, "gdn_oT", TT - 2), (5, "gdn_oT", TT - 1)]
    start, paced = placed[0], 0
    total = sum(TT * s[0] for s in tile_steps) + sum(s[0] for s in after) + 1

    def fill(weight):
        nonlocal paced
        paced += weight
        dense(start + int((limit[0] - start) * paced / total + 1e-6) - placed[0])

    for t in range(TT):
        for weight, name, *i in tile_steps:
            fill(weight)
            if name == "gdn_out":
                if t:
                    step("gdn_out", t - 1)
            elif name == "gdn_oT":
                if t == 2:
                    assert placed[0] > max(pieces_of("branch", 1))
                if t > 1:
                    step("gdn_oT", t - 2)
            else:
                step(name, t, *i)
    for weight, *last_steps in after:
        fill(weight)
        step(*last_steps)
    limit[0] = len(PIECES)
    dense_to("branch", 4)
    dense(2)
    step("mix_split", 0)
    dense_to("branch", 5)
    dense(2)
    step("mix_split", 1)
    dense_to("wo", 0)
    for t in range(TT):
        dense(3)
        step("x1_T", 0, t)
    dense_to("wo", 1)
    for t in range(TT):
        step("x1_T", 1, t)
        step("x1_norm", t)
    assert placed[0] == len(PIECES)

    ctx = ExitStack()
    with ctx:
        def sb(name, shape, dt=F32):
            return ctx.enter_context(nc.sbuf_tensor(name, shape, dt))

        w_raw = sb("w_raw", [P, SLOTS, KU * UW])
        w_hi = sb("w_hi", [P, SLOTS, KU * UW], F32R)
        w_lo = sb("w_lo", [P, SLOTS, KU * UW], F32R)
        act_A = sb("act_A", [P, 2, KT, SEQ], F32R)
        act_B = sb("act_B", [P, 2, KT, SEQ], F32R)
        ACTS = {"A": act_A, "B": act_B}
        MIX, MLP_IN, MIDDLE = ((act_B, KH), (act_A, 0)), ((act_A, KH), (act_B, 0)), ((act_A, 0), (act_B, KH))
        slab_S = sb("slab_S", [P, 12, UW])
        slab_C = sb("slab_C", [P, 12, UW])
        slab_M = sb("slab_M", [P, 8, UW])
        slab_Z = sb("slab_Z", [P, TT, UW])
        work = sb("work", [P, 8, UW])
        sbq_T, sbk_T, sb_v = slab_S[:, 0:4, :], slab_S[:, 4:8, :], slab_S[:, 8:12, :]
        gate_t = slab_S[:, 8:12, :]
        rows_g1, rows_more = work[0:KT, 3, 0:P], work[:, 3, P:2 * P]
        memq_T = slab_M[:, 0:4, :]
        memk_T = slab_M[:, 4:6, :].rearrange("p a (b m) -> p (a b) m", m=N_MEM)
        mem_v = slab_M[:, 6:8, :]

        mats = sb("mats", [P, 12, P])
        ident, neg_ones, tri_inc, tri_after, neg_tri, neg_big = (mats[:, i, :] for i in range(6))
        lvl = [mats[:, 6 + i, :] for i in range(6)]
        small = sb("small", [P, 440])
        used = [0]

        def cols(n):
            used[0] += n
            return small[:, used[0] - n:used[0]]

        g1, gm, g2 = cols(KT), cols(KT), cols(KT)
        g_gdn, g_sbq, g_sbk, g_mq, g_mk = cols(1), cols(1), cols(1), cols(1), cols(1)
        conv_c = cols(CONV * 3 * H).rearrange("p (w c) -> p w c", w=CONV)
        NPAR = used[0]
        params = (g1, small[:, KT:NPAR])
        alog, dtb = cols(H), cols(H)
        ssx, rsx, mlp_scale = cols(TT + MT + TT), cols(TT + MT), cols(TT)
        nt_v, nt_a = cols(TT * H), cols(TT * H)
        ssh, rsh = cols(TT * H), cols(TT * H)
        ab = cols(TT * 2 * H).rearrange("p (t c) -> p t c", c=2 * H)
        tg = cols(TT * H).rearrange("p (t c) -> p t c", c=H)
        glog = cols(TT * H).rearrange("p (t c) -> p t c", c=H)
        beta = cols(TT * H).rearrange("p (t c) -> p t c", c=H)
        gcum = cols(TT * H).rearrange("p (t c) -> p t c", c=H)
        eg = cols(TT * H).rearrange("p (t c) -> p t c", c=H)
        e2 = cols(TT * H).rearrange("p (t c) -> p t c", c=H)
        bb, rq2, rq_half = (cols(TT * H).rearrange("p (t c) -> p t c", c=H) for _ in range(3))
        k_norm, k_dec, k_beta_decay, v_beta = tg, e2, eg, beta
        gl = cols(2 * H).rearrange("p (h c) -> p h c", c=2)
        sso, rso = cols(H), cols(H)
        mx, rs = [cols(TT), cols(TT)], [cols(TT), cols(TT)]

        banks = [ctx.enter_context(nc.psum_tensor(f"sum{i}", [P, UW], F32)) for i in range(TT)]
        pa = [ctx.enter_context(nc.psum_tensor(f"mixer{i}", [P, UW], F32)) for i in range(4)]

        def heads_of(ap):
            return ap.rearrange("p (h d) -> p h d", h=H)

        def per_head(c):
            return c.unsqueeze(2).to_broadcast([P, H, DH])

        def all_heads(m):
            return m.unsqueeze(1).to_broadcast([P, H, P])

        names = """w_high w_ready piece_done
            par_g1 par_rows par_T_done par_decay params_ready masks_step ident_ready masks_ready
            x_landed0 x_landed1 x_landed2 x_landed3 m_landed0 m_landed1
            x_again stored
            norm_ss norm_factor norm_scaled norm_T_done norm_gained norm_hi act_ready
            gain_scaled head_scaled head_T_done head_ready
            conv_done ab_T_done ab_tok ab_exp ab_ln glog_ready
            decay_sums decay_exps decay_tok
            sb_masks sb_scored sb_abs sb_exp sb_ln sb_soft sb_after sb_high sb_low sb_summed sb_att sb_oT sb_hi sb_ready
            tanh_done silu_done qk_squared qk_summed qk_read factors_ready
            ms_scored ms_top ms_max ms_exp ms_prob ms_T ms_pT ms_oT ms_hi ms_ready
            mixed
            z_tanh g_bcast g_grams g_beta_row g_last g_decay_sub g_decay g_row_used g_q_dec
            g_kT_done g_vT_done g_k_scaled g_v_scaled i_T i_T_ready i_X i_X_copied i_P i_Pt i_Tt i_C g_uw g_w g_read
            g_qs g_vnew g_upd g_o_sum g_state g_o_sq g_o_scaled g_oT g_o_hi g_ready state_zero
            mix_hi mix_ready x1T_done x1T_gained x1T_hi x1T_ready x1_ss mlp_scaled
            up_relu up_hi up_ready dve_order act_order""".split()
        S = {n: ctx.enter_context(nc.semaphore(n)) for n in names}
        raw_landed = [ctx.enter_context(nc.semaphore(f"raw_landed{i}")) for i in range(SLOTS)]
        bank_free = [ctx.enter_context(nc.semaphore(f"bank_free{i}")) for i in range(TT)]
        block = ctx.enter_context(nc.Block())

        def wait_emptied(eng, name, i, j):
            bank, use = EMPTIED[name, i, j]
            eng.wait_ge(bank_free[bank], use)

        def wait_mixed(eng, i, j):
            if i < 2:
                wait_emptied(eng, "branch", i, j)
            else:
                eng.wait_ge(S["mixed"], TT * (i - 2) + j + 1)

        def norm_source(i):
            return slab_C[:, 2 * i:2 * i + 2, :]

        def norm_diag(n):
            return slab_M[:, n, 0:P]

        def norm_gained(i, half):
            return heads_of(work[:, 4 + 2 * (i % 2) + half, :])

        def norm_dest(i, half, part):
            buf, t = (act_A, i) if i < TT else (act_B, i - TT)
            return buf[:, part, KH * half:KH * half + KH, t * P:(t + 1) * P]

        def held(places, half, part, cols=slice(None)):
            buf, kt = places[half]
            return buf[:, part, kt:kt + KH, cols]

        HEADS = ([(sbq_T, t, g_sbq) for t in range(TT)] + [(sbk_T, t, g_sbk) for t in range(TT)] +
                 [(memq_T, t, g_mq) for t in range(TT)] + [(memk_T, t, g_mk) for t in range(MT)])
        HEAD_STAGE = {"sbq": 0, "sbk": TT, "memq": 2 * TT, "memk": 3 * TT}
        SBO = [0, SEQ, 2 * SEQ - P, 3 * SEQ - 3 * P, 4 * SEQ - 6 * P]
        SBW = SBO[TT]
        sb_flat = work.rearrange("p a n -> p (a n)")
        sb_soft, sb_exps, sb_att = (sb_flat[:, i * SBW:(i + 1) * SBW] for i in range(3))
        sb_split = [act_B[:, part, KH:2 * KH, :].rearrange("p a n -> p (a n)") for part in range(2)]
        SB_AFTER0, SB_AFTER1, SB_END = SBW, SBW + SEQ - P, SBW + 2 * SEQ - 3 * P
        sb_after = sb_exps[:, 0:SB_END - SBW]
        neg_tri_r, neg_ones_r = (m[:, SB_END:SB_END + P] for m in sb_split)
        ident_bf, neg_big_bf = (work[:, 7, 3 * P:].bitcast(BF16)[:, i * P:(i + 1) * P] for i in range(2))
        sb_bank = [pa[0][:, 0:SEQ], pa[1][:, 0:SEQ - P], pa[2][:, 0:SEQ - 2 * P], pa[2][:, SEQ - 2 * P:SEQ - P]]
        ms_probs = [work[:, 4 * n:4 * n + 2, :] for n in range(2)]
        (g_kbg, g_decayed, g_lower, g_at, g_eg, g_state, g_Tt, g_T, g_X, g_C0, g_C1, g_wT, g_vnew, g_o,
         g_sq) = [heads_of(slab_M[:, i, :]) for i in range(8)] + [heads_of(work[:, i, :]) for i in range(7)]
        g_C = [g_C0, g_C1]

        def conv_tile(part, t):
            return slab_C[:, part * H:(part + 1) * H, t * P:(t + 1) * P]

        pah = [heads_of(p[:, :]) for p in pa]

        def o_bank(t):
            return pah[3]

        def load(sp, u, src, freed):
            kts, width = src.shape[1], src.shape[2]
            if freed is not None:
                sp.wait_ge(S["w_ready"], freed)
            sp.dma_start(w_raw[:, u % SLOTS, 0:kts * width].rearrange("p (t n) -> p t n", t=kts), src)\
              .then_inc(raw_landed[u % SLOTS], 16)

        @block.sync
        def _(sp):
            def load_x(i):
                sp.dma_start(norm_source(i), x[0, i * P:(i + 1) * P, :].rearrange("p (a n) -> p a n", a=2))\
                  .then_inc(S[f"x_landed{i}"], 16)

            row = 0

            def load_rows(src, rows, landed):
                nonlocal row
                sp.dma_start(rows[row:row + src.shape[0], :], src).then_inc(landed, 16)
                row += src.shape[0]

            load_x(0)
            load_rows(norm1_g[0].rearrange("(t p) -> t p", p=P), rows_g1, S["par_g1"])
            load_x(1)
            load(sp, 0, UNITS[0]["src"], None)
            load(sp, 1, UNITS[1]["src"], None)
            load_x(2)
            load_x(3)
            for i in range(2, SLOTS):
                load(sp, i, UNITS[i]["src"], None)
            row = 0
            for src in (mem_norm_g, norm2_g, gdn_norm_g, sb_q_norm_g, sb_k_norm_g, mem_q_norm_g, mem_k_norm_g):
                load_rows(src[0].rearrange("(t p) -> t p", p=P), rows_more, S["par_rows"])
            load_rows(conv_w[0].rearrange("w (c p) -> (w c) p", p=P), rows_more, S["par_rows"])
            for i in range(MT):
                sp.dma_start(norm_source(TT + i), mem[0, i * P:(i + 1) * P, :].rearrange("p (a n) -> p a n", a=2))\
                  .then_inc(S[f"m_landed{i}"], 16)
            with nc.allow_non_contiguous_dma(reason="small parameters"):
                for dst, src in ((alog, a_log), (dtb, dt_bias)):
                    sp.dma_start(dst, src[0].partition_broadcast(P)).then_inc(S["par_decay"], 16)
            for u in range(SLOTS, NU):
                if UNITS[u]["stage"] == "branch" and UNITS[u]["first"] and UNITS[u]["i"] == 5:
                    sp.wait_ge(S["g_upd"], 2 * TT)
                    for t in range(TT):
                        sp.dma_start(norm_source(t), x[0, t * P:(t + 1) * P, :].rearrange("p (a n) -> p a n", a=2))\
                          .then_inc(S["x_again"], 16)
                load(sp, u, UNITS[u]["src"], u - SLOTS + 1)
            with sp.Fori(0, QUARTERS) as q:
                for n in range(LOOP_UNITS):
                    group, k = n // GU, KU * (n % GU)
                    if group < 2:
                        src = wup[:, k:k + KU, bass.ds(q * D + group * UW, UW)]
                    else:
                        src = wdown[:, bass.ds(q * KT + k, KU), (group - 2) * UW:(group - 1) * UW]
                    load(sp, NU + n, src, NU + n - SLOTS + 1 + q * LOOP_UNITS)
            for half in range(2):
                for t in range(TT):
                    sp.wait_ge(bank_free[t], BANK_USES[t] + (QUARTERS - 1) * LOOP_GROUPS + 3 + half)
                    sp.dma_start(out[0, t * P:(t + 1) * P, half * UW:(half + 1) * UW], slab_C[:, 2 * t + half, :])\
                      .then_inc(S["stored"], 16)
            sp.wait_ge(S["stored"], 16 * 2 * TT)

        @block.gpsimd
        def _(pool):
            sel = [0]

            def then(ins):
                sel[0] += 1
                ins.then_inc(S["masks_step"], 1)
                pool.wait_ge(S["masks_step"], sel[0])

            def blocks(dst, size, value):
                v = dst.rearrange("p (b s) -> p b s", s=size)
                then(pool.memset(dst, value))
                then(pool.affine_select(out=v, in_=v, compare_op=ALU.is_ge, fill=0.0, base=0,
                                        pattern=[[-size, P // size], [0, size]], channel_multiplier=1))
                then(pool.affine_select(out=v, in_=v, compare_op=ALU.is_ge, fill=0.0, base=size - 1,
                                        pattern=[[size, P // size], [0, size]], channel_multiplier=-1))

            def triangle(dst, base, step_p, step_f, fill=0.0):
                then(pool.affine_select(out=dst, in_=dst, compare_op=ALU.is_ge, fill=fill, base=base,
                                        pattern=[[step_f, P]], channel_multiplier=step_p))

            then(pool.memset(ident, 1.0))
            triangle(ident, 0, 1, -1)
            triangle(ident, 0, -1, 1)
            pool.sem_inc(S["ident_ready"], 1)

            def masks(n):
                if n == 0:
                    then(pool.memset(neg_ones, -1.0))
                    then(pool.memset(neg_tri, -1.0))
                    triangle(neg_tri, 0, 1, -1)
                    then(pool.memset(neg_big, 0.0))
                    triangle(neg_big, -1, -1, 1, fill=MASKED)
                elif n == 1:
                    blocks(tri_inc, CHUNK, 1.0)
                    triangle(tri_inc, 0, -1, 1)
                    blocks(tri_after, CHUNK, 1.0)
                    triangle(tri_after, -1, 1, -1)
                elif n < 8:
                    blocks(lvl[n - 2], 2 << (n - 2), 1.0)
                elif n == 8:
                    for m in range(5, 0, -1):
                        then(pool.tensor_tensor(lvl[m], lvl[m], lvl[m - 1], ALU.subtract))
                elif n == 9:
                    for m in range(6):
                        triangle(lvl[m], -1, -1, 1)
                    pool.sem_inc(S["masks_ready"], 1)

            def low_part(u, n, count):
                slot = u % SLOTS
                pool.wait_ge(S["w_high"], count)
                pool.tensor_tensor(w_lo[:, slot, 0:n], w_raw[:, slot, 0:n], w_hi[:, slot, 0:n].bitcast(F32),
                                   ALU.subtract).then_inc(S["w_ready"], 1)

            for u, unit in enumerate(UNITS):
                low_part(u, unit["src"].shape[1] * unit["src"].shape[2], u + 1)
                if u >= SLOTS - 1:
                    masks(u - SLOTS + 1)
            with pool.Fori(0, QUARTERS) as q:
                for n in range(LOOP_UNITS):
                    low_part(NU + n, KU * UW, NU + n + 1 + q * LOOP_UNITS)

        @block.tensor
        def _(pe):
            at = [0]

            def product(dst, lhs, rhs, first, last):
                pe.matmul(dst, lhs[0], rhs[0], start=first, stop=False)
                pe.matmul(dst, lhs[0], rhs[1], start=False, stop=False)
                return pe.matmul(dst, lhs[1], rhs[0], start=False, stop=last)

            def weights(slot, n, a, b):
                v = [w[:, slot, 0:n] for w in (w_hi, w_lo)]
                return [w[:, a:b] for w in v]

            def piece(p):
                unit = UNITS[p["unit"]]
                slot, j, act = p["unit"] % SLOTS, p["j"], ACTS[unit["act"]]
                kts, width = unit["src"].shape[1], unit["src"].shape[2]
                if p["opens_unit"]:
                    pe.wait_ge(S["w_ready"], p["unit"] + 1)
                if unit["first"] and p["use"] > 1:
                    pe.wait_ge(bank_free[p["bank"]], p["use"] - 1)
                if unit["stage"] == "sbq" and unit["first"]:
                    pe.wait_ge(S["act_ready"], 2 * (j + 1))
                if unit["stage"] == "memk" and p["opens_unit"]:
                    pe.wait_ge(S["act_ready"], 2 * (TT + MT))
                if unit["stage"] == "branch" and p["opens_unit"]:
                    pe.wait_ge(S[("sb_ready", "ms_ready", "g_ready")[unit["i"] // 2]], H)
                if unit["stage"] == "wo" and p["opens_unit"]:
                    half = (unit["act"], unit["kt0"] // KH) != ("B", 1)
                    pe.wait_ge(S["mix_ready"], half * KH + unit["kt0"] % KH + kts)
                for k in range(kts):
                    w = weights(slot, kts * width, k * width, (k + 1) * width)
                    opens, closes = unit["first"] and k == 0, unit["last"] and k == kts - 1
                    kt = unit["kt0"] + k
                    if unit["kind"] == "tok":
                        a = [act[:, part, kt, j * P:(j + 1) * P] for part in range(2)]
                        last = product(banks[p["bank"]][:, :], a, w, opens, closes)
                    else:
                        a = [act[:, part, kt, :] for part in range(2)]
                        last = product(banks[p["bank"]][:, :], [v[:, j * P:(j + 1) * P] for v in w], a, opens, closes)
                last.then_inc(S["piece_done"], 1)

            def four(dst, lhs, rhs, transpose=False):
                for h in range(H):
                    if transpose:
                        last = pe.transpose(dst[:, h, :], lhs[:, h, :], ident)
                    else:
                        last = pe.matmul(dst[:, h, :], lhs[:, h, :], rhs[:, h, :], start=True, stop=True)
                return last

            pe.wait_ge(S["ident_ready"], 1)
            for what, *i in TIMELINE:
                if what == "dense":
                    for _ in range(i[0]):
                        piece(PIECES[at[0]])
                        at[0] += 1
                elif what == "params":
                    if i[0] == 0:
                        pe.wait_ge(S["par_g1"], 16)
                        rows, n = rows_g1, KT
                    else:
                        pe.wait_ge(S["par_rows"], 16 * 8)
                        pe.wait_ge(S["act_ready"], 2 * TT)
                        rows, n = rows_more, NPAR - KT
                    pe.transpose(pa[3][:, 0:n], rows[0:n, :], ident[0:n, 0:n]).then_inc(S["par_T_done"], 1)
                elif what == "norm_T":
                    n = i[0]
                    if n < TT:
                        pe.wait_ge(S["norm_factor"], n + 1)
                    else:
                        pe.wait_ge(S["norm_scaled"], n - TT + 1)
                    if n == 1 or n == TT + 1:
                        pe.wait_ge(S["params_ready"], 1 + n // TT)
                    for half in range(2):
                        if n >= 2:
                            pe.wait_ge(S["norm_gained"], 2 * (n - 2) + half + 1)
                        for k in range(KH):
                            dst, tile = pah[2 * (n % 2) + half][:, k, :], norm_source(n)[:, half, k * P:(k + 1) * P]
                            if n < TT:
                                last = pe.matmul(dst, tile, norm_diag(n), start=True, stop=True)
                            else:
                                last = pe.transpose(dst, tile, ident)
                        last.then_inc(S["norm_T_done"], 1)
                elif what == "heads_T":
                    m = i[0]
                    pe.wait_ge(S["head_scaled"], m + 1)
                    if m < 4:
                        pe.wait_ge(S["norm_gained"], 2 * (TT + MT))
                    else:
                        pe.wait_ge(S["head_ready"], m - 3)
                    four(pah[m % 4], heads_of(work[:, m % 4, :]), None, transpose=True)\
                        .then_inc(S["head_T_done"], 1)
                elif what == "sb_scores":
                    h = i[0]
                    pe.wait_ge(S["sb_masks"], 1)
                    pe.wait_ge(S["head_ready"], 3 * TT + MT)
                    if h:
                        pe.wait_ge(S["sb_att"], 3 * h)
                    for j in range(TT):
                        alone = j < 3
                        pe.matmul(sb_bank[j], sbk_T[:, h, j * P:(j + 1) * P], sbq_T[:, h, j * P:SEQ],
                                  start=alone, stop=False, skip_group_check=True)
                        pe.matmul(sb_bank[j][:, 0:P], ident_bf, neg_big_bf, start=False, stop=True,
                                  skip_group_check=True).then_inc(S["sb_scored"], 1)
                elif what == "sb_suffix":
                    h = i[0]
                    def minus_sums(dst, ones, cols):
                        pe.matmul(dst, ones, sb_split[0][:, cols], start=False, stop=False, skip_group_check=True)
                        return pe.matmul(dst, ones, sb_split[1][:, cols], start=False, stop=True,
                                         skip_group_check=True)

                    pe.wait_ge(S["sb_low"], 2 * h + 1)
                    minus_sums(pa[0][:, 0:SEQ], neg_tri_r, slice(SBO[0], SBO[1]))
                    minus_sums(pa[1][:, 0:SEQ - P], neg_tri_r, slice(SBO[1], SBO[2]))
                    minus_sums(pa[2][:, 0:SEQ - P], neg_tri_r, slice(SBO[2], SBO[4]))
                    pe.wait_ge(S["sb_low"], 2 * h + 2)
                    minus_sums(pa[0][:, P:SEQ], neg_ones_r, slice(SB_AFTER0, SB_AFTER1)).then_inc(S["sb_summed"], 1)
                    minus_sums(pa[1][:, P:SEQ - P], neg_ones_r, slice(SB_AFTER1, SB_END))\
                        .then_inc(S["sb_summed"], 1)
                    minus_sums(pa[2][:, P:2 * P], neg_ones_r, slice(SBO[3], SBO[4]))\
                        .then_inc(S["sb_summed"], 1)
                elif what == "sb_out":
                    h = i[0]
                    pe.wait_ge(S["sb_att"], 3 * (h + 1))
                    for j in range(TT):
                        wait_emptied(pe, "sbv", 0, j)
                    if h:
                        pe.wait_ge(S["sb_ready"], h)
                    for j in range(TT):
                        last = pe.matmul(pa[3][:, j * P:SEQ], sb_v[:, j, h * DH:(h + 1) * DH],
                                         sb_att[:, SBO[j]:SBO[j + 1]], start=j == 0, stop=j == TT - 1,
                                         skip_group_check=True)
                    last.then_inc(S["sb_oT"], 1)
                elif what == "decay_logits":
                    wait_emptied(pe, "ab", 0, 0)
                    pe.wait_ge(S["sb_att"], 3 * H)
                    pe.wait_ge(S["sb_ready"], H)
                    for t in range(TT):
                        last = pe.transpose(pa[0][:, t * P:(t + 1) * P], work[:, 6, t * P:(t + 1) * P], ident)
                    last.then_inc(S["ab_T_done"], 1)
                elif what == "decay_sums":
                    pe.wait_ge(S["glog_ready"], 1)
                    gl_all = glog.rearrange("p t c -> p (t c)")
                    pe.matmul(pa[1][:, 0:TT * H], tri_inc, gl_all, start=True, stop=True)
                    pe.matmul(pa[2][:, 0:TT * H], tri_after, gl_all, start=True, stop=True)\
                      .then_inc(S["decay_sums"], 1)
                elif what == "qk_sums":
                    for n in range(2):
                        pe.wait_ge(S["qk_squared"], n + 1)
                        for t in range(TT):
                            for h in range(H):
                                c = (n * TT + t) * H + h
                                last = pe.matmul(pa[3][:, c:c + 1], slab_S[:, n * H + h, t * P:(t + 1) * P],
                                                 neg_ones[:, 0:1], start=True, stop=True)
                    last.then_inc(S["qk_summed"], 1)
                elif what == "mem_scores":
                    h = i[0]
                    pe.wait_ge(S["decay_tok"], 1)
                    if h:
                        pe.wait_ge(S["ms_exp"], TT * h)
                    for t in range(TT):
                        last = pe.matmul(pa[t // 2][:, (t % 2) * N_MEM:(t % 2 + 1) * N_MEM],
                                         memq_T[:, h, t * P:(t + 1) * P], memk_T[:, h, :], start=t % 2 == 0,
                                         stop=True, skip_group_check=True)
                    last.then_inc(S["ms_scored"], 1)
                elif what == "mem_T":
                    h = i[0]
                    pe.wait_ge(S["ms_prob"], h + 1)
                    if h:
                        pe.wait_ge(S["ms_ready"], h)
                    else:
                        pe.wait_ge(S["qk_read"], 1)
                    probs = ms_probs[h % 2]
                    for m in range(MT):
                        for t in range(TT):
                            first = (t % 2) * N_MEM + m * P
                            last = pe.transpose(pa[2 + m][:, t * P:(t + 1) * P], probs[:, t // 2, first:first + P], ident)
                    last.then_inc(S["ms_T"], 1)
                elif what == "mem_out":
                    h = i[0]
                    pe.wait_ge(S["ms_pT"], 2 * (h + 1))
                    for m in range(MT):
                        wait_emptied(pe, "memv", 0, m)
                        last = pe.matmul(pa[2][:, :], mem_v[:, m, h * DH:(h + 1) * DH], work[:, 2 + m, :],
                                         start=m == 0, stop=m == MT - 1)
                    last.then_inc(S["ms_oT"], 1)
                elif what == "gdn_gram":
                    t = i[0]
                    pe.wait_ge(S["ms_ready"], H)
                    pe.wait_ge(S["factors_ready"], 1)
                    if t:
                        pe.wait_ge(S["g_state"], 2 * t)
                        pe.wait_ge(S["g_vnew"], 2 * t)
                    kT, qT = conv_tile(1, t), conv_tile(0, t)
                    for h in range(H):
                        last = pe.matmul(pah[3][:, h, :], glog[:, t, h:h + 1].to_broadcast([P, P]), tri_inc,
                                         start=True, stop=True)
                    last.then_inc(S["g_bcast"], 1)
                    four(pah[2], kT, qT)
                    four(pah[0], kT, kT).then_inc(S["g_grams"], 1)
                    pe.wait_ge(S["g_row_used"], t + 1)
                    for h in range(H):
                        last = pe.matmul(pah[3][:, h, :], bb[:, t, h:h + 1].to_broadcast([P, P]), ident,
                                         start=True, stop=True)
                    last.then_inc(S["g_beta_row"], 1)
                elif what == "inv_T":
                    t = i[0]
                    pe.wait_ge(S["i_Tt"], 6 * t + 1)
                    four(pah[2], g_Tt, None, transpose=True).then_inc(S["i_T"], 1)
                elif what == "inv_X":
                    t, n = i
                    pe.wait_ge(S["i_T_ready"], 5 * t + n + 1)
                    pe.wait_ge(S["i_C"], 5 * t + n + 1)
                    four(pah[0], g_C[n % 2], g_T).then_inc(S["i_X"], 1)
                elif what == "inv_P":
                    t, n = i
                    pe.wait_ge(S["i_X_copied"], 5 * t + n + 1)
                    pe.wait_ge(S["i_Tt"], 6 * t + n + 1)
                    if n + 1 < len(LEVELS):
                        four(pah[2], g_Tt, g_X).then_inc(S["i_Pt"], 1)
                    if t and n == 0:
                        pe.wait_ge(S["g_o_scaled"], t)
                    four(pah[1], g_X, g_Tt).then_inc(S["i_P"], 1)
                elif what == "gdn_kT":
                    t = i[0]
                    if t > 1:
                        pe.wait_ge(S["g_ready"], t - 1)
                    four(pah[3], conv_tile(1, t), None, transpose=True).then_inc(S["g_kT_done"], 1)
                elif what == "gdn_vT":
                    t = i[0]
                    pe.wait_ge(S["g_k_scaled"], t + 1)
                    four(pah[3], conv_tile(2, t), None, transpose=True).then_inc(S["g_vT_done"], 1)
                elif what == "gdn_uw":
                    t = i[0]
                    pe.wait_ge(S["i_Tt"], 6 * (t + 1))
                    pe.wait_ge(S["g_v_scaled"], t + 1)
                    four(pah[2], g_kbg, g_Tt).then_inc(S["g_uw"], 1)
                    for h in range(H):
                        pe.matmul(pah[0][:, h, :], g_Tt[:, h, :], conv_tile(2, t)[:, h, :], start=h == 0, stop=False,
                                  skip_group_check=True)
                elif what == "gdn_read":
                    t, c = i
                    r = slice(c * CHUNK, (c + 1) * CHUNK)
                    if c == 0:
                        pe.wait_ge(S["g_w"], t + 1)
                    if t == 0 and c == 0:
                        pe.wait_ge(S["state_zero"], 1)
                    else:
                        pe.wait_ge(S["g_state"], 2 * t + c)
                    for h in range(H):
                        last = pe.matmul(pah[0][r, h, :], g_wT[:, h, r], g_state[:, h, :], start=False, stop=True,
                                         skip_group_check=True)
                    last.then_inc(S["g_read"], 1)
                    if c == 0:
                        pe.wait_ge(S["g_q_dec"], t + 1)
                    for h in range(H):
                        last = pe.matmul(pah[1][r, h, :], conv_tile(0, t)[:, h, r], g_state[:, h, :], start=h == 0,
                                         stop=False, skip_group_check=True)
                    last.then_inc(S["g_qs"], 1)
                elif what == "gdn_update":
                    t, c = i
                    r = slice(c * CHUNK, (c + 1) * CHUNK)
                    pe.wait_ge(S["g_vnew"], 2 * t + c + 1)
                    for h in range(H):
                        last = pe.matmul(pah[2][:, h, :], conv_tile(1, t)[r, h, :], g_vnew[r, h, :], start=True,
                                         stop=True)
                    last.then_inc(S["g_upd"], 1)
                    for h in range(H):
                        last = pe.matmul(pah[1][r, h, :], g_at[r, h, r], g_vnew[r, h, :], start=False, stop=True,
                                         skip_group_check=True)
                    last.then_inc(S["g_o_sum"], 1)
                elif what == "gdn_oT":
                    t = i[0]
                    pe.wait_ge(S["g_o_scaled"], t + 1)
                    if t < TT - 2:
                        pe.wait_ge(S["i_Tt"], 6 * (t + 2) + 1)
                    elif t == TT - 1:
                        pe.wait_ge(S["g_ready"], TT - 1)
                    four(o_bank(t), heads_of(slab_Z[:, t, :]), None, transpose=True).then_inc(S["g_oT"], 1)
                elif what == "x1_T":
                    half, t = i
                    n = half * TT + t
                    wait_emptied(pe, "wo", half, t)
                    if n >= 4:
                        pe.wait_ge(S["x1T_gained"], n - 3)
                    else:
                        pe.wait_ge(S["g_ready"], TT)
                    for k in range(KH):
                        last = pe.transpose(pah[n % 4][:, k, :], slab_C[:, 2 * t + half, k * P:(k + 1) * P], ident)
                    last.then_inc(S["x1T_done"], 1)

            with pe.Fori(0, QUARTERS) as q:
                for n in range(LOOP_UNITS):
                    u, group, kp = NU + n, n // GU, n % GU
                    pe.wait_ge(S["w_ready"], u + 1 + q * LOOP_UNITS)
                    if group == 0:
                        pe.wait_ge(S["x1T_ready"], TT * (1 + kp // (GU // 2)))
                    if group == 2:
                        pe.wait_ge(S["up_ready"], KU * (kp + 1) + q * KT)
                    for j in range(TT):
                        if kp == 0:
                            pe.wait_ge(bank_free[j], BANK_USES[j] + group + q * LOOP_GROUPS)
                        for k in range(KU):
                            kt = KU * kp + k
                            w = weights(u % SLOTS, KU * UW, k * UW, (k + 1) * UW)
                            if group < 2:
                                a = [held(MLP_IN, kt // KH, part)[:, kt % KH, :] for part in range(2)]
                                last = product(banks[j][:, :], [v[:, j * P:(j + 1) * P] for v in w], a, kt == 0,
                                               kt == KT - 1)
                            else:
                                a = [held(MIDDLE, kt // KH, part, slice(j * P, (j + 1) * P))[:, kt % KH, :]
                                     for part in range(2)]
                                last = product(banks[j][:, :], a, w, kt == 0, kt == KT - 1)
                        last.then_inc(S["piece_done"], 1)

        @block.scalar
        def _(act):
            at, order = [0], [0]

            def link(ins):
                order[0] += 1
                ins.then_inc(S["act_order"], 1)
                act.wait_ge(S["act_order"], order[0])

            def evacuate(p):
                unit, j, bank = UNITS[p["unit"]], p["j"], p["bank"]
                name = unit["stage"]
                act.wait_ge(S["piece_done"], p["done"])
                src = banks[bank][:, :]
                if name in HEAD_STAGE:
                    m = HEAD_STAGE[name] + j
                    if m >= 4:
                        act.wait_ge(S["head_T_done"], m - 3)
                    else:
                        act.wait_ge(S["params_ready"], 2)
                    act.activation(work[:, m % 4, :], src, ACT.Copy)
                    act.activation(slab_Z[:, m % 4, :], src, ACT.Square).then_inc(bank_free[bank], 1)
                elif name == "sbv":
                    act.activation(sb_v[:, j, :], src, ACT.Copy).then_inc(bank_free[bank], 1)
                elif name == "memv":
                    act.activation(mem_v[:, j, :], src, ACT.Copy).then_inc(bank_free[bank], 1)
                elif name == "conv":
                    if unit["i"]:
                        act.wait_ge(S["silu_done"], unit["i"])
                    act.activation(slab_Z[:, j, :], src, ACT.Copy)
                    act.activation(slab_C[:, unit["i"] * H + j, :], src, ACT.Copy,
                                   scale=conv_c[:, CONV - 1, unit["i"] * H + j:unit["i"] * H + j + 1])\
                       .then_inc(bank_free[bank], 1)
                elif name == "ab":
                    act.activation(work[:, 6, :], src, ACT.Copy).then_inc(bank_free[bank], 1)
                elif name == "z":
                    act.wait_ge(S["silu_done"], 3)
                    act.activation(slab_Z[:, j, :], src, ACT.Tanh, scale=0.5).then_inc(S["z_tanh"], 1)
                elif name == "gate":
                    if unit["i"]:
                        wait_mixed(act, unit["i"] - 1, j)
                    act.activation(gate_t[:, j, :], src, ACT.Tanh, scale=0.5).then_inc(bank_free[bank], 1)

            def high_part(u, n, landed, freed):
                slot = u % SLOTS
                act.wait_ge(raw_landed[slot], landed)
                if freed is not None:
                    act.wait_ge(S["piece_done"], freed)
                act.activation(w_hi[:, slot, 0:n], w_raw[:, slot, 0:n], ACT.Copy).then_inc(S["w_high"], 1)

            def high_part_ahead(u):
                u += SLOTS - 1
                n = UNITS[u]["src"].shape[1] * UNITS[u]["src"].shape[2] if u < NU else KU * UW
                high_part(u, n, 16 * (u // SLOTS + 1), UNITS[u - SLOTS]["done"] if u >= SLOTS else None)

            for what, *i in TIMELINE:
                if what == "dense":
                    for _ in range(i[0]):
                        p = PIECES[at[0]]
                        at[0] += 1
                        for u in p["ahead"]:
                            high_part_ahead(u)
                        if UNITS[p["unit"]]["last"]:
                            evacuate(p)
                elif what == "norm_squares":
                    for n in range(*i):
                        act.wait_ge(S[f"x_landed{n}" if n < TT else f"m_landed{n - TT}"], 16)
                        act.activation(slab_S[:, 2 * n:2 * n + 2, :], norm_source(n), ACT.Square,
                                       accum_out=ssx[:, n:n + 1]).then_inc(S["norm_ss"], 1)
                elif what == "norm":
                    if i[0] < 2:
                        high_part_ahead(i[0] - SLOTS + 1)
                    if i[0] == TT:
                        act.wait_ge(S["norm_factor"], TT + MT)
                        for n in range(*i):
                            act.activation(norm_source(n), norm_source(n), ACT.Copy, scale=rsx[:, n:n + 1])\
                               .then_inc(S["norm_scaled"], 1)
                elif what == "norm_T":
                    n = i[0]
                    for half in range(2):
                        act.wait_ge(S["norm_gained"], 2 * n + half + 1)
                        act.activation(norm_dest(n, half, 0), norm_gained(n, half), ACT.Copy)\
                           .then_inc(S["norm_hi"], 1)
                elif what == "heads_T":
                    m = i[0]
                    dst, t, gain = HEADS[m]
                    if m == 0:
                        act.wait_ge(S["gain_scaled"], 1)
                    act.wait_ge(S["head_T_done"], m + 1)
                    act.activation(dst[:, :, t * P:(t + 1) * P], pah[m % 4], ACT.Copy, scale=gain)\
                       .then_inc(S["head_ready"], 1)
                elif what == "sb_scores":
                    h = i[0]
                    if h == 0:
                        for j in range(MT):
                            wait_emptied(act, "memv", 0, j)
                        act.wait_ge(S["masks_ready"], 1)
                        act.activation(neg_tri_r, neg_tri, ACT.Copy)
                        act.activation(neg_ones_r, neg_ones, ACT.Copy)
                        act.activation(ident_bf, ident, ACT.Copy)
                        act.activation(neg_big_bf, neg_big, ACT.Copy).then_inc(S["sb_masks"], 1)
                    if h:
                        act.wait_ge(S["sb_low"], 2 * h)
                    for j, width in ((0, SEQ), (1, SEQ - P), (2, SEQ - P)):
                        act.wait_ge(S["sb_scored"], TT * h + (j + 1 if j < 2 else TT))
                        act.activation(sb_exps[:, SBO[j]:SBO[j] + width], pa[j][:, 0:width], ACT.Abs)\
                           .then_inc(S["sb_abs"], 1)
                    act.wait_ge(S["sb_abs"], 3 * (h + 1))
                    act.activation(sb_exps, sb_exps, ACT.Exp, scale=-1.0).then_inc(S["sb_exp"], 1)
                    act.wait_ge(S["sb_exp"], h + 1)
                    act.activation(sb_exps, sb_exps, ACT.Ln, bias=1.0).then_inc(S["sb_ln"], 1)
                elif what == "sb_split":
                    h = i[0]
                    act.wait_ge(S["sb_soft"], 3 * (h + 1))
                    act.activation(sb_split[0][:, 0:SBW], sb_soft, ACT.Copy).then_inc(S["sb_high"], 1)
                    act.wait_ge(S["sb_after"], h + 1)
                    act.activation(sb_split[0][:, SBW:SB_END], sb_after, ACT.Copy)\
                       .then_inc(S["sb_high"], 1)
                elif what == "sb_suffix":
                    h = i[0]
                    if h:
                        act.wait_ge(S["sb_oT"], h)
                    for n, (j, width) in enumerate(((0, SEQ), (1, SEQ - P), (2, SEQ - P))):
                        act.wait_ge(S["sb_summed"], 3 * h + n + 1)
                        act.activation(sb_att[:, SBO[j]:SBO[j] + width], pa[j][:, 0:width], ACT.Exp)\
                           .then_inc(S["sb_att"], 1)
                elif what == "sb_out":
                    h = i[0]
                    act.wait_ge(S["sb_oT"], h + 1)
                    act.activation(act_B[:, 0, h, :], pa[3][:, :], ACT.Copy).then_inc(S["sb_hi"], 1)
                elif what == "decay_logits":
                    act.wait_ge(S["ab_tok"], 1)
                    link(act.activation(gcum, tg, ACT.Abs))
                    act.activation(gcum, gcum, ACT.Exp, scale=-1.0).then_inc(S["ab_exp"], 1)
                    act.wait_ge(S["ab_exp"], 1)
                    act.activation(gcum, gcum, ACT.Ln, bias=1.0)
                    act.activation(alog, alog, ACT.Exp)
                    act.activation(beta, ab[:, :, H:2 * H], ACT.Exp, scale=-1.0).then_inc(S["ab_ln"], 1)
                elif what == "silu":
                    part = i[0]
                    act.wait_ge(S["conv_done"], H * (part + 1))
                    act.activation(slab_Z[:, :, :], slab_C[:, part * H:(part + 1) * H, :], ACT.Tanh,
                                   scale=0.5).then_inc(S["tanh_done"], 1)
                elif what == "qk_squares":
                    act.wait_ge(S["silu_done"], 2)
                    for n, part in enumerate((1, 0)):
                        act.activation(slab_S[:, n * H:(n + 1) * H, :], slab_C[:, part * H:(part + 1) * H, :],
                                       ACT.Square).then_inc(S["qk_squared"], 1)
                elif what == "decay_sums":
                    act.wait_ge(S["decay_sums"], 1)
                    act.activation(eg, pa[1][:, 0:TT * H].rearrange("p (t c) -> p t c", c=H), ACT.Exp)
                    act.activation(e2, pa[2][:, 0:TT * H].rearrange("p (t c) -> p t c", c=H), ACT.Exp)\
                       .then_inc(S["decay_exps"], 1)
                elif what == "mem_scores":
                    h = i[0]
                    act.wait_ge(S["ms_max"], h + 1)
                    if h >= 2:
                        act.wait_ge(S["ms_T"], h - 1)
                    for t in range(TT):
                        part = slice((t % 2) * N_MEM, (t % 2 + 1) * N_MEM)
                        act.activation(ms_probs[h % 2][:, t // 2, part], pa[t // 2][:, part], ACT.Exp,
                                       bias=mx[h % 2][:, t:t + 1], accum_out=rs[h % 2][:, t:t + 1])\
                           .then_inc(S["ms_exp"], 1)
                elif what == "mem_T":
                    h = i[0]
                    act.wait_ge(S["ms_T"], h + 1)
                    if h:
                        act.wait_ge(S["ms_oT"], h)
                    for m in range(MT):
                        act.activation(work[:, 2 + m, :], pa[2 + m][:, :], ACT.Copy).then_inc(S["ms_pT"], 1)
                elif what == "mem_out":
                    h = i[0]
                    act.wait_ge(S["ms_oT"], h + 1)
                    act.activation(act_B[:, 0, H + h, :], pa[2][:, :], ACT.Copy).then_inc(S["ms_hi"], 1)
                elif what == "gdn_gram":
                    t = i[0]
                    act.wait_ge(S["ms_ready"], H)
                    act.wait_ge(S["g_decay_sub"], t + 1)
                    if t:
                        act.wait_ge(S["g_state"], 2 * t)
                    act.activation(gl, pah[3][:, :, CHUNK - 1::CHUNK], ACT.Exp).then_inc(S["g_last"], 1)
                    if t:
                        act.wait_ge(S["g_q_dec"], t)
                    act.activation(g_eg, pah[3], ACT.Exp).then_inc(S["g_row_used"], 1)
                    act.activation(g_decayed, g_decayed, ACT.Exp).then_inc(S["g_decay"], 1)
                elif what == "inv_T":
                    t = i[0]
                    act.wait_ge(S["i_T"], t + 1)
                    act.activation(g_T, pah[2], ACT.Copy).then_inc(S["i_T_ready"], 1)
                elif what == "inv_X":
                    t, n = i
                    act.wait_ge(S["i_X"], 5 * t + n + 1)
                    if t + n:
                        act.wait_ge(S["i_P"], 5 * t + n)
                    act.activation(g_X, pah[0], ACT.Copy).then_inc(S["i_X_copied"], 1)
                elif what == "gdn_uw":
                    t = i[0]
                    act.wait_ge(S["g_uw"], t + 1)
                    act.activation(g_wT, pah[2], ACT.Copy, scale=-1.0).then_inc(S["g_w"], 1)
                elif what == "gdn_read":
                    t, c = i
                    r = slice(c * CHUNK, (c + 1) * CHUNK)
                    act.wait_ge(S["g_read"], 2 * t + c + 1)
                    act.activation(g_vnew[r], pah[0][r], ACT.Copy).then_inc(S["g_vnew"], 1)
                elif what == "gdn_out":
                    t = i[0]
                    act.wait_ge(S["g_o_sum"], 2 * (t + 1))
                    act.activation(g_sq, pah[1], ACT.Square).then_inc(S["g_o_sq"], 1)
                elif what == "gdn_oT":
                    t = i[0]
                    act.wait_ge(S["g_oT"], t + 1)
                    if t == 0:
                        for j in range(TT):
                            wait_mixed(act, 1, j)
                    act.activation(act_B[:, 0, 0:H, t * P:(t + 1) * P], o_bank(t), ACT.Copy, scale=g_gdn)\
                       .then_inc(S["g_o_hi"], 1)
                elif what == "mix_split":
                    half = i[0]
                    for k in range(KH):
                        wait_mixed(act, 4 + half, k)
                        act.activation(held(MIX, half, 0)[:, k, :], slab_S[:, KH * half + k, :], ACT.Copy)\
                           .then_inc(S["mix_hi"], 1)
                elif what == "x1_T":
                    half, t = i
                    n = half * TT + t
                    act.wait_ge(S["x1T_gained"], n + 1)
                    act.activation(held(MLP_IN, half, 0, slice(t * P, (t + 1) * P)), heads_of(work[:, n % 2, :]),
                                   ACT.Copy).then_inc(S["x1T_hi"], 1)
                elif what == "x1_norm":
                    t = i[0]
                    n = TT + MT + t
                    for half in range(2):
                        wait_emptied(act, "wo", half, t)
                    act.activation(work[:, 4:6, :], norm_source(t), ACT.Square, accum_out=ssx[:, n:n + 1])\
                       .then_inc(S["x1_ss"], 1)

            def relus(q, group):
                for j in range(TT):
                    n = TT * group + j
                    act.wait_ge(S["piece_done"], len(PIECES) + (GU * (group + 1) - 1) * TT + j + 1 + q * LOOP_PIECES)
                    b, uses = (n - 2) % TT, BANK_USES[(n - 2) % TT] + (n - 2) // TT + 1
                    act.wait_ge(bank_free[b], uses + q * LOOP_GROUPS)
                    act.activation(work[:, n % 2, :], banks[j][:, :], ACT.Relu).then_inc(S["up_relu"], 1)
                    act.wait_ge(S["up_relu"], n + 1 + q * KT)
                    act.activation(held(MIDDLE, group, 0)[:, j, :], work[:, n % 2, :], ACT.Square)\
                       .then_inc(S["up_hi"], 1)

            def quarter(q, units):
                ahead = SLOTS - 1

                def high_parts(a, b):
                    for n in range(a, min(b, units)):
                        u = NU + ahead + n
                        freed = len(PIECES) + (ahead + n - SLOTS + 1) * TT
                        high_part(u, KU * UW, 16 * (u // SLOTS + 1) + q * (16 * LOOP_UNITS // SLOTS),
                                  freed + q * LOOP_PIECES)

                high_parts(0, GU)
                relus(q, 0)
                high_parts(GU, 2 * GU)
                relus(q, 1)
                high_parts(2 * GU, LOOP_UNITS)

            with act.Fori(0, QUARTERS - 1) as q:
                quarter(q, LOOP_UNITS)
            quarter(QUARTERS - 1, LOOP_UNITS - (SLOTS - 1))

        @block.vector
        def _(dve):
            at, order = [0], [0]

            def link(ins):
                order[0] += 1
                ins.then_inc(S["dve_order"], 1)
                dve.wait_ge(S["dve_order"], order[0])

            def rsqrt(dst, src, mult, add, v=None, a=None, src_read=None):
                n = src.shape[1]
                if v is None:
                    v, a = nt_v[:, 0:n], nt_a[:, 0:n]
                link(dve.tensor_scalar(v, src, mult, add, ALU.mult, ALU.add))
                if src_read is not None:
                    dve.sem_inc(src_read, 1)
                link(dve.tensor_scalar(a.bitcast(I32), v.bitcast(I32), 1, None, ALU.logical_shift_right))
                link(dve.tensor_scalar(dst.bitcast(I32), a.bitcast(I32), -1.0, float(0x5F3759DF), ALU.mult, ALU.add))
                for _ in range(3):
                    link(dve.tensor_tensor(a, dst, dst, ALU.mult))
                    link(dve.scalar_tensor_tensor(out=a, in0=a, scalar=-0.5, in1=v, op0=ALU.mult, op1=ALU.mult))
                    link(dve.scalar_tensor_tensor(out=dst, in0=a, scalar=1.5, in1=dst, op0=ALU.add, op1=ALU.mult))

            def evacuate(p):
                unit, j, bank = UNITS[p["unit"]], p["j"], p["bank"]
                name, src = unit["stage"], banks[p["bank"]]
                if name in HEAD_STAGE:
                    m = HEAD_STAGE[name] + j
                    wait_emptied(dve, name, 0, j)
                    ins = dve.reduce_sum(ssh[:, j * H:(j + 1) * H], heads_of(slab_Z[:, m % 4, :]), axis=AX.X)
                    if (j + 1) * P == (SEQ if name != "memk" else N_MEM):
                        link(ins)
                        rsqrt(rsh[:, 0:(j + 1) * H], ssh[:, 0:(j + 1) * H], 1.0 / DH, EPS)
                        for n in range(j + 1):
                            copy = heads_of(work[:, (m - j + n) % 4, :])
                            dve.tensor_tensor(copy, copy, per_head(rsh[:, n * H:(n + 1) * H]), ALU.mult)\
                               .then_inc(S["head_scaled"], 1)
                elif name == "z":
                    z = slab_Z[:, j, :]
                    dve.wait_ge(S["z_tanh"], j + 1)
                    dve.scalar_tensor_tensor(out=z, in0=z, scalar=1.0, in1=src[:, :], op0=ALU.add, op1=ALU.mult)\
                       .then_inc(bank_free[bank], 1)
                elif name == "branch":
                    mix = slab_S[:, KH * (unit["i"] % 2) + j, :]
                    dve.wait_ge(S["piece_done"], p["done"])
                    wait_emptied(dve, "gate", unit["i"], j)
                    dst = mix if unit["i"] < 2 else gate_t[:, j, :]
                    ins = dve.scalar_tensor_tensor(out=dst, in0=gate_t[:, j, :], scalar=1.0, in1=src[:, :],
                                                   op0=ALU.add, op1=ALU.mult)
                    ins.then_inc(bank_free[bank], 1)
                    if unit["i"] >= 2:
                        dve.wait_ge(bank_free[bank], p["use"])
                        dve.tensor_tensor(mix, mix, gate_t[:, j, :], ALU.add).then_inc(S["mixed"], 1)
                elif name == "wo":
                    dve.wait_ge(S["piece_done"], p["done"])
                    dve.wait_ge(S["x_again"], 16 * TT)
                    x1 = slab_C[:, 2 * j + unit["i"], :]
                    dve.scalar_tensor_tensor(out=x1, in0=src[:, :], scalar=0.5, in1=x1, op0=ALU.mult, op1=ALU.add)\
                       .then_inc(bank_free[bank], 1)

            dve.wait_ge(S["ident_ready"], 1)
            for what, *i in TIMELINE:
                if what == "dense":
                    for _ in range(i[0]):
                        p = PIECES[at[0]]
                        at[0] += 1
                        if UNITS[p["unit"]]["last"]:
                            evacuate(p)
                elif what == "norm":
                    dve.wait_ge(S["norm_ss"], i[1])
                    rsqrt(rsx[:, i[0]:i[1]], ssx[:, i[0]:i[1]], 1.0 / D, EPS)
                    if i[0] == TT:
                        dve.sem_inc(S["norm_factor"], MT)
                    else:
                        for n in range(*i):
                            dve.tensor_scalar(norm_diag(n), ident, rsx[:, n:n + 1], None, ALU.mult)\
                               .then_inc(S["norm_factor"], 1)
                elif what == "params":
                    n = i[0]
                    dve.wait_ge(S["par_T_done"], n + 1)
                    dve.tensor_copy(params[n], pa[3][:, 0:params[n].shape[1]]).then_inc(S["params_ready"], 1)
                    if n:
                        dve.wait_ge(S["params_ready"], 2)
                        dve.tensor_scalar(g_sbq, g_sbq, SCALE, None, ALU.mult)
                        dve.tensor_scalar(g_mq, g_mq, SCALE, None, ALU.mult).then_inc(S["gain_scaled"], 1)
                elif what == "norm_T":
                    n = i[0]
                    if n == 0:
                        dve.wait_ge(S["params_ready"], 1)
                    gain = g1 if n < TT else gm
                    for half in range(2):
                        dve.wait_ge(S["norm_T_done"], 2 * n + half + 1)
                        if n > 1:
                            dve.wait_ge(S["act_ready"], 2 * (n - 2) + half + 1)
                        dve.tensor_tensor(norm_gained(n, half), pah[2 * (n % 2) + half],
                                          gain[:, KH * half:KH * half + KH].unsqueeze(2).to_broadcast([P, KH, P]),
                                          ALU.mult).then_inc(S["norm_gained"], 1)
                    for half in range(2):
                        dve.wait_ge(S["norm_hi"], 2 * n + half + 1)
                        dve.tensor_tensor(norm_dest(n, half, 1), norm_gained(n, half),
                                          norm_dest(n, half, 0).bitcast(F32), ALU.subtract)\
                           .then_inc(S["act_ready"], 1)
                elif what == "sb_soft":
                    h = i[0]
                    widths = ((0, SEQ), (1, SEQ - P), (2, SEQ - P))
                    dve.wait_ge(S["sb_ln"], h + 1)
                    if h:
                        dve.wait_ge(S["sb_summed"], 3 * h)
                    else:
                        for j in range(MT):
                            wait_emptied(dve, "memv", 0, j)
                    for j, width in widths:
                        dve.scalar_tensor_tensor(out=sb_soft[:, SBO[j]:SBO[j] + width], in0=pa[j][:, 0:width],
                                                 scalar=0.0, in1=sb_exps[:, SBO[j]:SBO[j] + width], op0=ALU.max,
                                                 op1=ALU.add).then_inc(S["sb_soft"], 1)
                    dve.wait_ge(S["sb_soft"], 3 * (h + 1))
                    after0, after1 = sb_after[:, 0:SEQ - P], sb_after[:, SEQ - P:]
                    dve.tensor_copy(after1[:, 0:P], sb_soft[:, SBO[2]:SBO[2] + P])
                    dve.tensor_copy(after0[:, 0:P], sb_soft[:, SBO[1]:SBO[1] + P])
                    link(dve.tensor_tensor(after1[:, P:], sb_soft[:, SBO[2] + P:SBO[3]], sb_soft[:, SBO[3]:SBO[4]],
                                           ALU.add))
                    dve.tensor_tensor(after0[:, P:], sb_soft[:, SBO[1] + P:SBO[2]], after1, ALU.add)\
                       .then_inc(S["sb_after"], 1)
                elif what == "sb_split":
                    h = i[0]
                    dve.wait_ge(S["sb_after"], h + 1)
                    for n, (part, sums) in enumerate(((slice(0, SBW), sb_soft), (slice(SBW, SB_END), sb_after))):
                        dve.wait_ge(S["sb_high"], 2 * h + n + 1)
                        dve.tensor_tensor(sb_split[1][:, part], sums, sb_split[0][:, part].bitcast(F32),
                                          ALU.subtract).then_inc(S["sb_low"], 1)
                elif what == "sb_out":
                    h = i[0]
                    dve.wait_ge(S["sb_hi"], h + 1)
                    dve.tensor_tensor(act_B[:, 1, h, :], pa[3][:, :], act_B[:, 0, h, :].bitcast(F32), ALU.subtract)\
                       .then_inc(S["sb_ready"], 1)
                elif what == "decay_logits":
                    dve.wait_ge(S["ab_T_done"], 1)
                    dve.wait_ge(S["par_decay"], 32)
                    link(dve.tensor_copy(ab, pa[0][:, :].rearrange("p (t c) -> p t c", c=P)[:, :, 0:2 * H]))
                    dve.tensor_tensor(tg, ab[:, :, 0:H], dtb.unsqueeze(1).to_broadcast([P, TT, H]), ALU.add)\
                       .then_inc(S["ab_tok"], 1)
                    dve.wait_ge(S["ab_ln"], 1)
                    link(dve.scalar_tensor_tensor(out=glog, in0=tg, scalar=0.0, in1=gcum, op0=ALU.max, op1=ALU.add))
                    dve.scalar_tensor_tensor(out=glog, in0=glog, scalar=-1.0,
                                             in1=alog.unsqueeze(1).to_broadcast([P, TT, H]), op0=ALU.mult,
                                             op1=ALU.mult).then_inc(S["glog_ready"], 1)
                    link(dve.tensor_scalar(beta, beta, 1.0, None, ALU.add))
                    link(dve.reciprocal(beta, beta))
                elif what == "decay_sums":
                    dve.wait_ge(S["decay_sums"], 1)
                    dve.wait_ge(S["decay_exps"], 1)
                    dve.tensor_copy(gcum, pa[1][:, 0:TT * H].rearrange("p (t c) -> p t c", c=H))\
                       .then_inc(S["decay_tok"], 1)
                elif what == "conv_taps":
                    c = i[0]
                    y, copy = slab_C[:, c, :], slab_Z[:, c % H, :]
                    wait_emptied(dve, "conv", c // H, c % H)
                    for tap in range(1, CONV):
                        ins = dve.scalar_tensor_tensor(out=y[:, tap:], in0=copy[:, 0:SEQ - tap],
                                                       scalar=conv_c[:, CONV - 1 - tap, c:c + 1], in1=y[:, tap:],
                                                       op0=ALU.mult, op1=ALU.add)
                        if tap < CONV - 1:
                            link(ins)
                    ins.then_inc(S["conv_done"], 1)
                elif what == "silu":
                    part = i[0]
                    c = slab_C[:, part * H:(part + 1) * H, :]
                    dve.wait_ge(S["tanh_done"], part + 1)
                    dve.scalar_tensor_tensor(out=c, in0=slab_Z[:, :, :], scalar=1.0, in1=c,
                                             op0=ALU.add, op1=ALU.mult).then_inc(S["silu_done"], 1)
                elif what == "qk_norms":
                    dve.wait_ge(S["qk_summed"], 1)
                    n = TT * H
                    v, a, r = (work[:, 7, i * 2 * n:(i + 1) * 2 * n] for i in range(3))
                    rsqrt(r, pa[3][:, 0:2 * n], -1.0, 4.0 * EPS, v, a, src_read=S["qk_read"])
                    r3 = r.rearrange("p (t c) -> p t c", c=H)
                    rk, rq = r3[:, 0:TT, :], r3[:, TT:2 * TT, :]
                    dve.tensor_copy(k_norm, rk)
                    dve.tensor_scalar(rq_half, rq, 0.5 * SCALE, None, ALU.mult)
                    dve.scalar_tensor_tensor(out=rq2, in0=rq, scalar=SCALE * SCALE, in1=rq, op0=ALU.mult, op1=ALU.mult)
                    dve.tensor_tensor(k_dec, rk, e2, ALU.mult)
                    link(dve.tensor_tensor(bb, rk, beta, ALU.mult))
                    dve.tensor_tensor(k_beta_decay, bb, eg, ALU.mult)
                    dve.tensor_scalar(v_beta, beta, 0.5, None, ALU.mult).then_inc(S["factors_ready"], 1)
                elif what == "mem_scores":
                    h = i[0]
                    dve.wait_ge(S["ms_scored"], h + 1)
                    if h:
                        dve.wait_ge(S["ms_exp"], TT * h)
                    top, total = mx[h % 2], rs[h % 2]
                    for n in range(TT // 2):
                        dve.reduce_max(total[:, 2 * n:2 * n + 2], pa[n][:, :].rearrange("p (t m) -> p t m", m=N_MEM),
                                       axis=AX.X).then_inc(S["ms_top"], 1)
                    dve.wait_ge(S["ms_top"], 2 * (h + 1))
                    dve.tensor_scalar(top, total, -1.0, None, ALU.mult).then_inc(S["ms_max"], 1)
                    dve.wait_ge(S["ms_exp"], TT * (h + 1))
                    link(dve.reciprocal(top, total))
                    probs = ms_probs[h % 2].rearrange("p a (b m) -> p (a b) m", m=N_MEM)
                    dve.tensor_tensor(probs, probs, top.unsqueeze(2).to_broadcast([P, TT, N_MEM]), ALU.mult)\
                       .then_inc(S["ms_prob"], 1)
                elif what == "mem_out":
                    h = i[0]
                    dve.wait_ge(S["ms_hi"], h + 1)
                    dve.tensor_tensor(act_B[:, 1, H + h, :], pa[2][:, :], act_B[:, 0, H + h, :].bitcast(F32),
                                      ALU.subtract).then_inc(S["ms_ready"], 1)
                elif what == "gdn_gram":
                    t = i[0]
                    if t == 0:
                        dve.wait_ge(S["ms_oT"], H)
                        dve.memset(g_state, 0.0).then_inc(S["state_zero"], 1)
                    dve.wait_ge(S["g_bcast"], t + 1)
                    for h in range(H):
                        ins = dve.tensor_scalar(g_decayed[:, h, :], pah[3][:, h, :], gcum[:, t, h:h + 1], 0.0,
                                                ALU.subtract, ALU.min)
                    ins.then_inc(S["g_decay_sub"], 1)
                    dve.wait_ge(S["g_decay"], t + 1)
                    for h in range(H):
                        ins = dve.scalar_tensor_tensor(out=g_decayed[:, h, :], in0=g_decayed[:, h, :],
                                                       scalar=k_norm[:, t, h:h + 1], in1=tri_inc, op0=ALU.mult,
                                                       op1=ALU.mult)
                    link(ins)
                    dve.wait_ge(S["g_beta_row"], t + 1)
                    link(dve.tensor_tensor(g_lower, g_decayed, pah[3], ALU.mult))
                    dve.wait_ge(S["g_grams"], t + 1)
                    link(dve.tensor_tensor(g_lower, g_lower, pah[0], ALU.mult))
                    link(dve.tensor_tensor(g_Tt, g_lower, all_heads(lvl[0]), ALU.mult))
                    if t:
                        dve.wait_ge(S["g_o_sum"], 2 * t)
                    dve.tensor_tensor(g_at, g_decayed, pah[2], ALU.mult)
                    dve.scalar_tensor_tensor(out=g_Tt, in0=g_Tt, scalar=-1.0, in1=all_heads(ident), op0=ALU.mult,
                                             op1=ALU.add).then_inc(S["i_Tt"], 1)
                    dve.tensor_tensor(g_C[0], g_lower, all_heads(lvl[1]), ALU.mult).then_inc(S["i_C"], 1)
                    dve.wait_ge(S["g_row_used"], t + 1)
                    q = conv_tile(0, t)
                    dve.tensor_tensor(q, q, g_eg, ALU.mult).then_inc(S["g_q_dec"], 1)
                elif what == "gdn_kT":
                    t = i[0]
                    dve.wait_ge(S["g_kT_done"], t + 1)
                    dve.tensor_tensor(g_kbg, pah[3], per_head(k_beta_decay[:, t, :]), ALU.mult)
                    dve.tensor_tensor(conv_tile(1, t), pah[3], per_head(k_dec[:, t, :]), ALU.mult)\
                       .then_inc(S["g_k_scaled"], 1)
                elif what == "gdn_vT":
                    t = i[0]
                    dve.wait_ge(S["g_vT_done"], t + 1)
                    dve.tensor_tensor(conv_tile(2, t), pah[3], per_head(v_beta[:, t, :]), ALU.mult)\
                       .then_inc(S["g_v_scaled"], 1)
                elif what == "inv_P":
                    t, n = i
                    if n + 1 < len(LEVELS):
                        dve.tensor_tensor(g_C[(n + 1) % 2], g_lower, all_heads(lvl[n + 2]), ALU.mult)\
                           .then_inc(S["i_C"], 1)
                        dve.wait_ge(S["i_Pt"], 4 * t + n + 1)
                        dve.wait_ge(S["i_T_ready"], 5 * t + n + 1)
                        dve.tensor_tensor(g_T, g_T, pah[2], ALU.subtract).then_inc(S["i_T_ready"], 1)
                    dve.wait_ge(S["i_P"], 5 * t + n + 1)
                    dve.tensor_tensor(g_Tt, g_Tt, pah[1], ALU.subtract).then_inc(S["i_Tt"], 1)
                elif what == "gdn_read":
                    t, c = i
                    dve.wait_ge(S["g_qs"], 2 * t + c + 1)
                    link(dve.tensor_tensor(g_state, g_state, per_head(gl[:, :, c]), ALU.mult))
                elif what == "gdn_update":
                    t, c = i
                    dve.wait_ge(S["g_upd"], 2 * t + c + 1)
                    dve.tensor_tensor(g_state, g_state, pah[2], ALU.add).then_inc(S["g_state"], 1)
                elif what == "gdn_out":
                    t = i[0]
                    dve.wait_ge(S["g_o_sq"], t + 1)
                    link(dve.reduce_sum(sso, g_sq, axis=AX.X))
                    link(dve.tensor_tensor(sso, sso, rq2[:, t, :], ALU.mult))
                    rsqrt(rso, sso, 1.0 / DH, EPS)
                    link(dve.tensor_tensor(rso, rso, rq_half[:, t, :], ALU.mult))
                    link(dve.tensor_tensor(g_o, pah[1], per_head(rso), ALU.mult))
                    z = heads_of(slab_Z[:, t, :])
                    dve.tensor_tensor(z, g_o, z, ALU.mult).then_inc(S["g_o_scaled"], 1)
                elif what == "gdn_oT":
                    t = i[0]
                    hi, lo = (act_B[:, part, 0:H, t * P:(t + 1) * P] for part in range(2))
                    dve.wait_ge(S["g_o_hi"], t + 1)
                    dve.scalar_tensor_tensor(out=lo, in0=o_bank(t), scalar=g_gdn, in1=hi.bitcast(F32), op0=ALU.mult,
                                             op1=ALU.subtract).then_inc(S["g_ready"], 1)
                elif what == "mix_split":
                    half = i[0]
                    for k in range(KH):
                        dve.wait_ge(S["mix_hi"], KH * half + k + 1)
                        dve.tensor_tensor(held(MIX, half, 1)[:, k, :], slab_S[:, KH * half + k, :],
                                          held(MIX, half, 0)[:, k, :].bitcast(F32), ALU.subtract)\
                           .then_inc(S["mix_ready"], 1)
                elif what == "x1_T":
                    half, t = i
                    n = half * TT + t
                    tokens = slice(t * P, (t + 1) * P)
                    dve.wait_ge(S["x1T_done"], n + 1)
                    dve.tensor_tensor(heads_of(work[:, n % 2, :]), pah[n % 4],
                                      g2[:, KH * half:KH * half + KH].unsqueeze(2).to_broadcast([P, KH, P]),
                                      ALU.mult).then_inc(S["x1T_gained"], 1)
                    dve.wait_ge(S["x1T_hi"], n + 1)
                    dve.wait_ge(S["x1T_gained"], n + 1)
                    dve.tensor_tensor(held(MLP_IN, half, 1, tokens), heads_of(work[:, n % 2, :]),
                                      held(MLP_IN, half, 0, tokens).bitcast(F32), ALU.subtract)\
                       .then_inc(S["x1T_ready"], 1)
                elif what == "x1_norm":
                    t = i[0]
                    n = TT + MT + t
                    dve.wait_ge(S["x1_ss"], t + 1)
                    link(dve.tensor_scalar(rsx[:, 0:1], ssx[:, n:n + 1], 1.0 / D, EPS, ALU.mult, ALU.add))
                    dve.reciprocal(mlp_scale[:, t:t + 1], rsx[:, 0:1]).then_inc(S["mlp_scaled"], 1)

            dve.wait_ge(S["mlp_scaled"], TT)
            with dve.Fori(0, QUARTERS) as q:
                for n in range(KT):
                    group, j = n // TT, n % TT
                    dve.wait_ge(S["up_relu"], n + 1 + q * KT)
                    dve.scalar_tensor_tensor(out=work[:, 2 + n % 2, :], in0=banks[j][:, :], scalar=0.0,
                                             in1=work[:, n % 2, :], op0=ALU.max, op1=ALU.mult)\
                       .then_inc(bank_free[j], 1)
                    dve.wait_ge(bank_free[j], BANK_USES[j] + group + 1 + q * LOOP_GROUPS)
                    dve.wait_ge(S["up_hi"], n + 1 + q * KT)
                    dve.tensor_tensor(held(MIDDLE, group, 1)[:, j, :], work[:, 2 + n % 2, :],
                                      held(MIDDLE, group, 0)[:, j, :].bitcast(F32), ALU.subtract)\
                       .then_inc(S["up_ready"], 1)
                for n in range(2 * TT):
                    half, j = n // TT, n % TT
                    x1 = slab_C[:, 2 * j + half, :]
                    dve.wait_ge(S["piece_done"],
                                len(PIECES) + (GU * (half + 3) - 1) * TT + j + 1 + q * LOOP_PIECES)
                    dve.scalar_tensor_tensor(out=x1, in0=banks[j][:, :], scalar=mlp_scale[:, j:j + 1], in1=x1,
                                             op0=ALU.mult, op1=ALU.add).then_inc(bank_free[j], 1)


_INS = ["x", "mem", "norm1_g", "w_in", "conv_w", "a_log", "dt_bias", "gdn_norm_g", "sb_q_norm_g", "sb_k_norm_g",
        "mem_norm_g", "w_mem_kv", "mem_q_norm_g", "mem_k_norm_g", "w_br_gdn", "w_br_sb", "w_br_mem", "w_o",
        "norm2_g", "w_up", "w_down"]


def kernel(**inputs):
    import concourse.bacc as bacc
    from concourse.bass_utils import run_bass_kernel_spmd

    nc = bacc.Bacc("TRN2", target_bir_lowering=False, num_devices=1)
    arrays, args = {}, []
    for name in _INS:
        a = np.ascontiguousarray(inputs[name])
        arrays[f"in_{name}"] = a
        args.append(nc.dram_tensor(f"in_{name}", a.shape, mybir.dt.from_np(a.dtype), kind="ExternalInput").ap())
    shape = arrays["in_x"].shape
    args.append(nc.dram_tensor("layer_out", shape, mybir.dt.float32, kind="ExternalOutput").ap())
    hybrid_layer_kernel(nc, *args)
    return run_bass_kernel_spmd(nc, [arrays], core_ids=[0]).results[0]["layer_out"]
```
